# Optimizing a Trainium2 kernel written in Bass

```python
import math
import jax
import jax.numpy as jnp
from jax import lax
import numpy as np

D_MODEL = 1024
BATCH = 1
SEQ = 256
DEPTH = 4

N_MIXERS = 3
N_GDN = (DEPTH + 2) // 3
N_SB = (DEPTH + 1) // 3
N_DSA = DEPTH // 3

D_FF = 2816
NORM_EPS = 1e-6
ROPE_THETA = 500000.0
Q_BLOCK = 128

GDN_HEADS = 8
GDN_HEAD_DIM = 128
GDN_DIM = GDN_HEADS * GDN_HEAD_DIM
GDN_CONV = 4
GDN_CHUNK = 64
GDN_IN = 4 * GDN_DIM + 2 * GDN_HEADS

SB_HEADS = 8
SB_HEAD_DIM = 128
SB_DIM = SB_HEADS * SB_HEAD_DIM

DSA_HEADS = 8
DSA_Q_RANK = 384
DSA_KV_RANK = 256
DSA_ROPE_DIM = 32
DSA_NOPE_DIM = 96
DSA_QK_DIM = DSA_ROPE_DIM + DSA_NOPE_DIM
DSA_V_DIM = 128
DSA_IDX_HEADS = 8
DSA_IDX_DIM = 64
DSA_TOPK_MAX = 256
DSA_IN = DSA_Q_RANK + DSA_KV_RANK + DSA_ROPE_DIM + DSA_IDX_DIM + DSA_IDX_HEADS


def rmsnorm(x, g):
    xf = x.astype(jnp.float32)
    y = xf * lax.rsqrt(jnp.mean(xf * xf, axis=-1, keepdims=True) + NORM_EPS)
    return (y * g.astype(jnp.float32)).astype(x.dtype)

def l2norm(x):
    return x * lax.rsqrt(jnp.sum(x * x, axis=-1, keepdims=True) + NORM_EPS)

def rope(x, pos):
    r = x.shape[-1]
    half = r // 2
    inv_freq = ROPE_THETA ** (-jnp.arange(half, dtype=jnp.float32) * (2.0 / r))
    ang = pos.astype(jnp.float32)[:, None] * inv_freq[None, :]
    shape = (pos.shape[0],) + (1,) * (x.ndim - 3) + (half,)
    cos = jnp.cos(ang).reshape(shape)
    sin = jnp.sin(ang).reshape(shape)
    xf = x.astype(jnp.float32)
    x1, x2 = xf[..., :half], xf[..., half:]
    return jnp.concatenate([x1 * cos - x2 * sin, x2 * cos + x1 * sin], axis=-1).astype(x.dtype)

def partial_rope(x, pos):
    r = x.shape[-1] // 4
    return jnp.concatenate([rope(x[..., :r], pos), x[..., r:]], axis=-1)

def swiglu(h, w_gu, w_down):
    gate, up = jnp.split(h @ w_gu, 2, axis=-1)
    return (jax.nn.silu(gate) * up) @ w_down

def causal_depthwise_conv(x, w):
    kw, ch = w.shape
    return lax.conv_general_dilated(
        x, w[:, None, :].astype(x.dtype), window_strides=(1,), padding=[(kw - 1, 0)],
        dimension_numbers=('NWC', 'WIO', 'NWC'), feature_group_count=ch)

def to_blocks(t, block):
    b, s = t.shape[:2]
    return jnp.swapaxes(t.reshape((b, s // block, block) + t.shape[2:]), 0, 1)

def from_blocks(t):
    nb, b, blk = t.shape[:3]
    return jnp.swapaxes(t, 0, 1).reshape((b, nb * blk) + t.shape[3:])

def chunk_gated_delta_rule(q, k, v, g, beta):
    bsz, seq, nh, dk = q.shape
    dv = v.shape[-1]
    c = GDN_CHUNK
    n = seq // c

    def chunks(t):
        return jnp.moveaxis(t.reshape((bsz, n, c, nh) + t.shape[3:]), 3, 1)

    q, k, v, g, beta = chunks(q), chunks(k), chunks(v), chunks(g), chunks(beta)
    g_cum = jnp.cumsum(g, axis=-1)
    incl = jnp.tril(jnp.ones((c, c), dtype=bool))
    strict = jnp.tril(jnp.ones((c, c), dtype=bool), -1)
    seg = g_cum[..., :, None] - g_cum[..., None, :]
    decay = jnp.where(incl, jnp.exp(jnp.where(incl, seg, 0.0)), 0.0)
    kk = jnp.einsum('bhnid,bhnjd->bhnij', k, k)
    lower = jnp.where(strict, beta[..., :, None] * kk * decay, 0.0)
    eye = jnp.eye(c, dtype=jnp.float32)
    rhs = jnp.concatenate([v * beta[..., None], k * (beta * jnp.exp(g_cum))[..., None]], axis=-1)
    sol = lax.linalg.triangular_solve(lower + eye, rhs, left_side=True, lower=True, unit_diagonal=True)
    u_in, w = sol[..., :dv], sol[..., dv:]
    qk = jnp.einsum('bhnid,bhnjd->bhnij', q, k) * decay
    q_dec = q * jnp.exp(g_cum)[..., None]
    k_dec = k * jnp.exp(g_cum[..., -1:] - g_cum)[..., None]
    g_tot = jnp.exp(g_cum[..., -1])
    xs = tuple(jnp.moveaxis(t, 2, 0) for t in (u_in, w, qk, q_dec, k_dec, g_tot))

    def step(state, inp):
        u_c, w_c, qk_c, qd_c, kd_c, gt_c = inp
        u = u_c - jnp.einsum('bhck,bhkv->bhcv', w_c, state)
        o = jnp.einsum('bhck,bhkv->bhcv', qd_c, state) + jnp.einsum('bhcj,bhjv->bhcv', qk_c, u)
        state = state * gt_c[..., None, None] + jnp.einsum('bhck,bhcv->bhkv', kd_c, u)
        return state, o

    state0 = jnp.zeros((bsz, nh, dk, dv), jnp.float32)
    _, o = lax.scan(step, state0, xs)
    return jnp.transpose(o, (1, 0, 3, 2, 4)).reshape(bsz, seq, nh, dv)

def gated_deltanet(h, w_in, conv_w, a_log, dt_bias, norm_g, w_out):
    bsz, seq, _ = h.shape
    proj = h @ w_in
    qkv = jax.nn.silu(causal_depthwise_conv(proj[..., :3 * GDN_DIM], conv_w))
    z = proj[..., 3 * GDN_DIM:4 * GDN_DIM]
    b_logit = proj[..., 4 * GDN_DIM:4 * GDN_DIM + GDN_HEADS].astype(jnp.float32)
    a = proj[..., 4 * GDN_DIM + GDN_HEADS:].astype(jnp.float32)

    def heads(t):
        return t.reshape(bsz, seq, GDN_HEADS, GDN_HEAD_DIM).astype(jnp.float32)

    q, k, v = (heads(t) for t in jnp.split(qkv, 3, axis=-1))
    q = l2norm(q) * GDN_HEAD_DIM ** -0.5
    k = l2norm(k)
    beta = jax.nn.sigmoid(b_logit)
    g = -jnp.exp(a_log.astype(jnp.float32)) * jax.nn.softplus(a + dt_bias.astype(jnp.float32))
    o = chunk_gated_delta_rule(q, k, v, g, beta)
    o = rmsnorm(o, norm_g) * jax.nn.silu(heads(z))
    return o.reshape(bsz, seq, GDN_DIM).astype(h.dtype) @ w_out

def stick_breaking_attention(h, w_in, w_out):
    bsz, seq, _ = h.shape
    q, k, v = (t.reshape(bsz, seq, SB_HEADS, SB_HEAD_DIM).astype(jnp.float32)
               for t in jnp.split(h @ w_in, 3, axis=-1))
    scale = SB_HEAD_DIM ** -0.5
    key_pos = jnp.arange(seq)

    def block(args):
        q_blk, t0 = args
        z = jnp.einsum('bqhd,bkhd->bhqk', q_blk, k) * scale
        q_pos = t0 + jnp.arange(Q_BLOCK)
        earlier = key_pos[None, :] < q_pos[:, None]
        log_beta = jax.nn.log_sigmoid(z)
        log_fail = jnp.where(earlier, log_beta - z, 0.0)
        log_a = log_beta + lax.cumsum(log_fail, axis=3, reverse=True) - log_fail
        att = jnp.where(earlier, jnp.exp(log_a), 0.0)
        return jnp.einsum('bhqk,bkhd->bqhd', att, v)

    starts = jnp.arange(seq // Q_BLOCK, dtype=jnp.int32) * Q_BLOCK
    o = from_blocks(lax.map(block, (to_blocks(q, Q_BLOCK), starts)))
    return o.reshape(bsz, seq, SB_DIM).astype(h.dtype) @ w_out

def dsa_sparse_attention(h, w_in, cq_g, ckv_g, kidx_g, w_uq, w_qidx, w_uk, w_uv, w_out):
    bsz, seq, _ = h.shape
    topk = min(DSA_TOPK_MAX, seq // 4)
    pos = jnp.arange(seq)
    proj = h @ w_in
    o1 = DSA_Q_RANK
    o2 = o1 + DSA_KV_RANK
    o3 = o2 + DSA_ROPE_DIM
    o4 = o3 + DSA_IDX_DIM
    c_q = rmsnorm(proj[..., :o1], cq_g)
    c_kv = rmsnorm(proj[..., o1:o2], ckv_g)
    k_rope = rope(proj[..., o2:o3], pos)
    k_idx = partial_rope(rmsnorm(proj[..., o3:o4], kidx_g), pos).astype(jnp.float32)
    w_idx = proj[..., o4:].astype(jnp.float32) * (DSA_IDX_HEADS ** -0.5 * DSA_IDX_DIM ** -0.5)
    q = (c_q @ w_uq).reshape(bsz, seq, DSA_HEADS, DSA_QK_DIM)
    q_rope = rope(q[..., :DSA_ROPE_DIM], pos)
    q_nope = q[..., DSA_ROPE_DIM:]
    q_idx = partial_rope((c_q @ w_qidx).reshape(bsz, seq, DSA_IDX_HEADS, DSA_IDX_DIM), pos)
    q_abs = jnp.einsum('bshn,chn->bshc', q_nope, w_uk.reshape(DSA_KV_RANK, DSA_HEADS, DSA_NOPE_DIM))
    q_lat = jnp.concatenate([q_abs, q_rope], axis=-1).astype(jnp.float32)
    k_lat = jnp.concatenate([c_kv, k_rope], axis=-1).astype(jnp.float32)
    scale = DSA_QK_DIM ** -0.5
    batch_ix = jnp.arange(bsz)[:, None, None]

    def block(args):
        qi, wi, ql, t0 = args
        q_pos = t0 + jnp.arange(Q_BLOCK)
        logits = jnp.einsum('bqhd,bkd->bqhk', qi, k_idx)
        score = jnp.einsum('bqh,bqhk->bqk', wi, jax.nn.relu(logits))
        score = jnp.where(pos[None, None, :] <= q_pos[None, :, None], score, -jnp.inf)
        _, idx = lax.top_k(score, topk)
        sel = k_lat[batch_ix, idx]
        att = jnp.einsum('bqhr,bqkr->bqhk', ql, sel) * scale
        att = jnp.where((idx <= q_pos[None, :, None])[:, :, None, :], att, -jnp.inf)
        p = jax.nn.softmax(att, axis=-1)
        return jnp.einsum('bqhk,bqkc->bqhc', p, sel[..., :DSA_KV_RANK])

    starts = jnp.arange(seq // Q_BLOCK, dtype=jnp.int32) * Q_BLOCK
    o_lat = from_blocks(lax.map(block, (to_blocks(q_idx.astype(jnp.float32), Q_BLOCK),
                                        to_blocks(w_idx, Q_BLOCK),
                                        to_blocks(q_lat, Q_BLOCK), starts)))
    o = jnp.einsum('bshc,chv->bshv', o_lat,
                   w_uv.reshape(DSA_KV_RANK, DSA_HEADS, DSA_V_DIM).astype(jnp.float32))
    return o.reshape(bsz, seq, DSA_HEADS * DSA_V_DIM).astype(h.dtype) @ w_out

def first_inputs(seed: int = 0) -> dict:
    key = jax.random.key(seed)
    ks = jax.random.split(key, 26)
    f32 = jnp.float32

    def dense(k, shape):
        return jax.random.normal(k, shape, f32) * shape[-2] ** -0.5

    def gain(k, shape):
        return 1.0 + 0.02 * jax.random.normal(k, shape, f32)

    x = jax.random.normal(ks[0], (BATCH, SEQ, D_MODEL), f32)
    dt = jnp.exp(jax.random.uniform(ks[12], (N_GDN, GDN_HEADS), f32, math.log(1e-3), math.log(1e-1)))
    return {
        'x': x,
        'ffn1_norm': gain(ks[1], (DEPTH, D_MODEL)),
        'ffn1_w_gu': dense(ks[2], (DEPTH, D_MODEL, 2 * D_FF)),
        'ffn1_w_down': dense(ks[3], (DEPTH, D_FF, D_MODEL)),
        'mix_norm': gain(ks[4], (DEPTH, D_MODEL)),
        'ffn2_norm': gain(ks[5], (DEPTH, D_MODEL)),
        'ffn2_w_gu': dense(ks[6], (DEPTH, D_MODEL, 2 * D_FF)),
        'ffn2_w_down': dense(ks[7], (DEPTH, D_FF, D_MODEL)),
        'gdn_w_in': dense(ks[8], (N_GDN, D_MODEL, GDN_IN)),
        'gdn_conv': jax.random.normal(ks[10], (N_GDN, GDN_CONV, 3 * GDN_DIM), f32) * GDN_CONV ** -0.5,
        'gdn_a_log': jnp.log(jax.random.uniform(ks[11], (N_GDN, GDN_HEADS), f32, 1.0, 16.0)),
        'gdn_dt_bias': dt + jnp.log(-jnp.expm1(-dt)),
        'gdn_norm': gain(ks[13], (N_GDN, GDN_HEAD_DIM)),
        'gdn_w_out': dense(ks[9], (N_GDN, GDN_DIM, D_MODEL)),
        'sb_w_in': dense(ks[14], (N_SB, D_MODEL, 3 * SB_DIM)),
        'sb_w_out': dense(ks[15], (N_SB, SB_DIM, D_MODEL)),
        'dsa_w_in': dense(ks[16], (N_DSA, D_MODEL, DSA_IN)),
        'dsa_cq_norm': gain(ks[17], (N_DSA, DSA_Q_RANK)),
        'dsa_ckv_norm': gain(ks[18], (N_DSA, DSA_KV_RANK)),
        'dsa_kidx_norm': gain(ks[19], (N_DSA, DSA_IDX_DIM)),
        'dsa_w_uq': dense(ks[20], (N_DSA, DSA_Q_RANK, DSA_HEADS * DSA_QK_DIM)),
        'dsa_w_qidx': dense(ks[21], (N_DSA, DSA_Q_RANK, DSA_IDX_HEADS * DSA_IDX_DIM)),
        'dsa_w_uk': dense(ks[22], (N_DSA, DSA_KV_RANK, DSA_HEADS * DSA_NOPE_DIM)),
        'dsa_w_uv': dense(ks[23], (N_DSA, DSA_KV_RANK, DSA_HEADS * DSA_V_DIM)),
        'dsa_w_out': dense(ks[24], (N_DSA, DSA_HEADS * DSA_V_DIM, D_MODEL)),
        'final_norm': gain(ks[25], (D_MODEL,)),
    }

def first_block(x, ffn1_norm, ffn1_w_gu, ffn1_w_down, mix_norm, ffn2_norm, ffn2_w_gu, ffn2_w_down,
              gdn_w_in, gdn_conv, gdn_a_log, gdn_dt_bias, gdn_norm, gdn_w_out,
              sb_w_in, sb_w_out,
              dsa_w_in, dsa_cq_norm, dsa_ckv_norm, dsa_kidx_norm, dsa_w_uq, dsa_w_qidx,
              dsa_w_uk, dsa_w_uv, dsa_w_out, final_norm):
    for i in range(DEPTH):
        kind, j = i % N_MIXERS, i // N_MIXERS
        x = x + 0.5 * swiglu(rmsnorm(x, ffn1_norm[i]), ffn1_w_gu[i], ffn1_w_down[i])
        h = rmsnorm(x, mix_norm[i])
        if kind == 0:
            m = gated_deltanet(h, gdn_w_in[j], gdn_conv[j], gdn_a_log[j], gdn_dt_bias[j],
                               gdn_norm[j], gdn_w_out[j])
        elif kind == 1:
            m = stick_breaking_attention(h, sb_w_in[j], sb_w_out[j])
        else:
            m = dsa_sparse_attention(h, dsa_w_in[j], dsa_cq_norm[j], dsa_ckv_norm[j],
                                     dsa_kidx_norm[j], dsa_w_uq[j], dsa_w_qidx[j],
                                     dsa_w_uk[j], dsa_w_uv[j], dsa_w_out[j])
        x = x + m.astype(x.dtype)
        x = x + 0.5 * swiglu(rmsnorm(x, ffn2_norm[i]), ffn2_w_gu[i], ffn2_w_down[i])
    return rmsnorm(x, final_norm)


DEPTH_2 = 2

GRID_W = 64
CTX_LEN = 256
N_SUB = 3
NA_HEADS = 8
NA_HEAD_DIM = 64
NA_KH = 8
NA_KW = 16
ML_HEADS = 4
ML_HEAD_DIM = 128
ML_CHUNK = 128
ROPE_THETA_2 = 10000.0
SG_CHUNK = 128
SG_WIDTH = 2048
SG_GROUPS = 8
NA_WIDTH = NA_HEADS * NA_HEAD_DIM
ML_WIDTH = ML_HEADS * ML_HEAD_DIM
MIX_WIDTH = NA_WIDTH + ML_WIDTH
N_GATES = 4 * ML_HEADS
P_EVEN = 3 * NA_WIDTH + 4 * ML_WIDTH + N_GATES
SPLITS = (NA_WIDTH, 2 * NA_WIDTH, 3 * NA_WIDTH, 3 * NA_WIDTH + ML_WIDTH, 3 * NA_WIDTH + 2 * ML_WIDTH,
          3 * NA_WIDTH + 3 * ML_WIDTH, 3 * NA_WIDTH + 4 * ML_WIDTH)
N_EVEN = (DEPTH_2 + 1) // 2
N_ODD = DEPTH_2 // 2
EPS = 1e-6


def rms_norm(x, g):
    xf = x.astype(jnp.float32)
    y = xf * lax.rsqrt(jnp.mean(jnp.square(xf), axis=-1, keepdims=True) + EPS)
    return (y * g.astype(jnp.float32)).astype(x.dtype)

def layer_norm(x, g, b):
    xf = x.astype(jnp.float32)
    mu = jnp.mean(xf, axis=-1, keepdims=True)
    var = jnp.mean(jnp.square(xf - mu), axis=-1, keepdims=True)
    y = (xf - mu) * lax.rsqrt(var + EPS)
    return (y * g.astype(jnp.float32) + b.astype(jnp.float32)).astype(x.dtype)

def modulate(x, g, shift, scale):
    return rms_norm(x, g) * (1.0 + scale) + shift

def swiglu_2(h, w_in, w_out):
    a, b = jnp.split(h @ w_in, 2, axis=-1)
    return (jax.nn.silu(a) * b) @ w_out

def macaron_half_ffn(x, g, shift, scale, gate, w_in, w_out):
    return x + 0.5 * gate * swiglu_2(modulate(x, g, shift, scale), w_in, w_out)

def mod_terms(m, j):
    return m[:, 3 * j], m[:, 3 * j + 1], m[:, 3 * j + 2]

def axial_rope(x):
    n, dh = x.shape[1], x.shape[-1]
    n_pairs = dh // 4
    pos = jnp.arange(n)
    row = (pos // GRID_W).astype(jnp.float32)
    col = (pos % GRID_W).astype(jnp.float32)
    inv_freq = ROPE_THETA_2 ** (-jnp.arange(n_pairs, dtype=jnp.float32) / n_pairs)
    ang = jnp.concatenate([row[:, None] * inv_freq, col[:, None] * inv_freq], axis=-1)
    cos = jnp.cos(ang)[None, :, None, :]
    sin = jnp.sin(ang)[None, :, None, :]
    xp = x.astype(jnp.float32).reshape(*x.shape[:-1], dh // 2, 2)
    x1, x2 = xp[..., 0], xp[..., 1]
    out = jnp.stack([x1 * cos - x2 * sin, x1 * sin + x2 * cos], axis=-1)
    return out.reshape(x.shape).astype(x.dtype)

def dense_attention(q, k, v):
    s = jnp.einsum('bqhd,bkhd->bhqk', q, k) * (q.shape[-1] ** -0.5)
    p = jax.nn.softmax(s.astype(jnp.float32), axis=-1).astype(v.dtype)
    return jnp.einsum('bhqk,bkhd->bqhd', p, v)

def neighbourhood_attention(q, k, v, kx, vx, rpb):
    B, N, H, Dh = q.shape
    rows = N // GRID_W
    kh = min(NA_KH, rows)
    kw = NA_KW
    scale = Dh ** -0.5
    qg = q.reshape(B, rows, GRID_W, H, Dh)
    kg = k.reshape(B, rows, GRID_W, H, Dh)
    vg = v.reshape(B, rows, GRID_W, H, Dh)
    cols = jnp.arange(GRID_W)
    col_idx = jnp.clip(cols - kw // 2, 0, GRID_W - kw)[:, None] + jnp.arange(kw)[None, :]
    col_rel = col_idx - cols[:, None] + (NA_KW - 1)

    def row_block(i):
        r0 = jnp.clip(i - kh // 2, 0, rows - kh)
        q_i = lax.dynamic_index_in_dim(qg, i, axis=1, keepdims=False)
        k_win = lax.dynamic_slice_in_dim(kg, r0, kh, axis=1)[:, :, col_idx]
        v_win = lax.dynamic_slice_in_dim(vg, r0, kh, axis=1)[:, :, col_idx]
        row_rel = r0 + jnp.arange(kh) - i + (NA_KH - 1)
        bias = rpb[:, row_rel[None, :, None], col_rel[:, None, :]]
        s_loc = jnp.einsum('bqhd,baqkhd->bhqak', q_i, k_win) * scale + bias
        s_ctx = jnp.einsum('bqhd,bchd->bhqc', q_i, kx) * scale
        s = jnp.concatenate([s_loc.reshape(B, H, GRID_W, kh * kw), s_ctx], axis=-1).astype(jnp.float32)
        p = jax.nn.softmax(s, axis=-1).astype(v.dtype)
        p_loc = p[..., :kh * kw].reshape(B, H, GRID_W, kh, kw)
        p_ctx = p[..., kh * kw:]
        return (jnp.einsum('bhqak,baqkhd->bqhd', p_loc, v_win)
                + jnp.einsum('bhqc,bchd->bqhd', p_ctx, vx))

    out = lax.map(row_block, jnp.arange(rows))
    return jnp.moveaxis(out, 0, 1).reshape(B, N, H, Dh)

def mlstm_scan(q, k, v, log_i, log_f, state, with_output):
    B, H, N, Dk = q.shape
    nc = N // ML_CHUNK

    def chunks(a):
        return jnp.moveaxis(a.reshape(B, H, nc, ML_CHUNK, *a.shape[3:]), 2, 0)

    tri = jnp.tril(jnp.ones((ML_CHUNK, ML_CHUNK), dtype=bool))

    def step(carry, inp):
        C, n, m = carry
        qc, kc, vc, ic, fc = inp
        b = jnp.cumsum(fc, axis=-1)
        b_end = b[..., -1]
        w_end = b_end[..., None] - b + ic
        m_new = jnp.maximum(b_end + m, jnp.max(w_end, axis=-1))
        a_prev = jnp.exp(b_end + m - m_new)
        a_tok = jnp.exp(w_end - m_new[..., None])
        C_new = a_prev[..., None, None] * C + jnp.einsum('bhs,bhsv,bhsk->bhvk', a_tok, vc, kc)
        n_new = a_prev[..., None] * n + jnp.einsum('bhs,bhsk->bhk', a_tok, kc)
        if not with_output:
            return (C_new, n_new, m_new), None
        log_w = jnp.where(tri, b[..., :, None] - b[..., None, :] + ic[..., None, :], -jnp.inf)
        log_inter = b + m[..., None]
        m_t = jnp.maximum(log_inter, jnp.max(log_w, axis=-1))
        w_intra = jnp.exp(log_w - m_t[..., None])
        w_inter = jnp.exp(log_inter - m_t)
        s = jnp.einsum('bhtk,bhsk->bhts', qc, kc) * w_intra
        num = (w_inter[..., None] * jnp.einsum('bhvk,bhtk->bhtv', C, qc)
               + jnp.einsum('bhts,bhsv->bhtv', s, vc))
        den = w_inter * jnp.einsum('bhk,bhtk->bht', n, qc) + jnp.sum(s, axis=-1)
        h = num / jnp.maximum(jnp.abs(den), jnp.exp(-m_t))[..., None]
        return (C_new, n_new, m_new), h

    state, hs = lax.scan(step, state, (chunks(q), chunks(k), chunks(v), chunks(log_i), chunks(log_f)))
    if not with_output:
        return state, None
    return state, jnp.moveaxis(hs, 0, 2).reshape(B, H, N, Dk)

def _flip(a, rev):
    return jnp.flip(a, axis=2) if rev else a

def mlstm_bidirectional(q, k, v, log_i, log_f, qx, kx, vx, log_ix, log_fx, ctx_out):
    B, _, H, Dk = q.shape
    bh = lambda a: jnp.moveaxis(a.astype(jnp.float32), 1, 2)
    lat = [bh(a) for a in (q, k, v)]
    cx = [bh(a) for a in (qx, kx, vx)]
    h_lat, h_ctx = [], []
    for d in range(2):
        rev = d == 1
        init = (jnp.zeros((B, H, Dk, Dk), jnp.float32), jnp.zeros((B, H, Dk), jnp.float32),
                jnp.zeros((B, H), jnp.float32))
        st, hc = mlstm_scan(*[_flip(a, rev) for a in cx], _flip(bh(log_ix[..., d]), rev),
                            _flip(bh(log_fx[..., d]), rev), init, ctx_out)
        _, hl = mlstm_scan(*[_flip(a, rev) for a in lat], _flip(bh(log_i[..., d]), rev),
                           _flip(bh(log_f[..., d]), rev), st, True)
        h_lat.append(_flip(hl, rev))
        if ctx_out:
            h_ctx.append(_flip(hc, rev))
    y = jnp.moveaxis(h_lat[0] + h_lat[1], 2, 1)
    yx = jnp.moveaxis(h_ctx[0] + h_ctx[1], 2, 1) if ctx_out else None
    return y, yx

def mlstm_readout(h, o, head_g):
    B, L, H, Dk = h.shape
    y = rms_norm(h, head_g) * jax.nn.sigmoid(o.astype(jnp.float32)).reshape(B, L, H, Dk)
    return y.reshape(B, L, H * Dk).astype(o.dtype)

def even_mixer(h, hx, w_in, rpb, gate_b, head_g, w_out, ctx_out):
    def project(t):
        p = t @ w_in
        Bt, L, _ = p.shape
        qa, ka, va, qb, kb, vb, ob, g = jnp.split(p, SPLITS, axis=-1)
        na = [a.reshape(Bt, L, NA_HEADS, NA_HEAD_DIM) for a in (qa, ka, va)]
        ml = [a.reshape(Bt, L, ML_HEADS, ML_HEAD_DIM) for a in (qb, kb, vb)]
        g = g.reshape(Bt, L, ML_HEADS, 2, 2).astype(jnp.float32) + gate_b
        return na, ml, ob, g[..., 0], jax.nn.log_sigmoid(g[..., 1])

    (qa, ka, va), (qb, kb, vb), ob, li, lf = project(h)
    (qax, kax, vax), (qbx, kbx, vbx), obx, lix, lfx = project(hx)
    B, N, _ = h.shape
    y_a = neighbourhood_attention(qa, ka, va, kax, vax, rpb).reshape(B, N, NA_WIDTH)
    k_scale = ML_HEAD_DIM ** -0.5
    h_b, h_bx = mlstm_bidirectional(axial_rope(qb), axial_rope(kb) * k_scale, vb, li, lf,
                                    qbx, kbx * k_scale, vbx, lix, lfx, ctx_out)
    y = jnp.concatenate([y_a, mlstm_readout(h_b, ob, head_g)], axis=-1) @ w_out
    if not ctx_out:
        return y, None
    Bx, Lc, _ = hx.shape
    y_ax = dense_attention(qax, kax, vax).reshape(Bx, Lc, NA_WIDTH)
    yx = jnp.concatenate([y_ax, mlstm_readout(h_bx, obx, head_g)], axis=-1) @ w_out
    return y, yx

def spatial_gating(h, w_in, ln_g, ln_b, w_s, b_s, w_out):
    B, L, _ = h.shape
    u, v = jnp.split(jax.nn.gelu(h @ w_in), 2, axis=-1)
    v = layer_norm(v, ln_g, ln_b)
    nc = L // SG_CHUNK
    vg = v.reshape(B, nc, SG_CHUNK, SG_GROUPS, SG_WIDTH // SG_GROUPS)
    mixed = jnp.einsum('gts,bcsgd->bctgd', w_s, vg) + b_s.T[None, None, :, :, None]
    return (u * mixed.reshape(B, L, SG_WIDTH)) @ w_out

def second_inputs(seed: int = 0) -> dict:
    key = jax.random.key(seed)
    ks = jax.random.split(key, 24)
    nrm = lambda k, shape, std: jax.random.normal(k, shape, jnp.float32) * std
    D = D_MODEL
    forget_base = jnp.linspace(3.0, 6.0, ML_HEADS, dtype=jnp.float32)[:, None]
    gate_b = jnp.stack([nrm(ks[11], (N_EVEN, ML_HEADS, 2), 0.1),
                        forget_base + nrm(ks[12], (N_EVEN, ML_HEADS, 2), 0.1)], axis=-1)
    return {
        'x': nrm(ks[0], (BATCH, SEQ, D), 1.0),
        'c': nrm(ks[1], (BATCH, D), 1.0),
        'ctx': nrm(ks[2], (BATCH, CTX_LEN, D), 1.0),
        'c_ctx': nrm(ks[3], (D,), 1.0),
        'w_mod': nrm(ks[4], (DEPTH_2, D, 3 * N_SUB * D), 0.5 * D ** -0.5),
        'b_mod': nrm(ks[5], (DEPTH_2, 3 * N_SUB * D), 0.02),
        'norm_g': 1.0 + nrm(ks[6], (DEPTH_2, N_SUB, D), 0.05),
        'ffn_w_in': nrm(ks[7], (DEPTH_2, 2, D, 2 * D_FF), D ** -0.5),
        'ffn_w_out': nrm(ks[8], (DEPTH_2, 2, D_FF, D), D_FF ** -0.5),
        'mix_w_in': nrm(ks[9], (N_EVEN, D, P_EVEN), D ** -0.5),
        'na_rpb': nrm(ks[10], (N_EVEN, NA_HEADS, 2 * NA_KH - 1, 2 * NA_KW - 1), 0.1),
        'ml_gate_b': gate_b,
        'ml_head_g': 1.0 + nrm(ks[13], (N_EVEN, ML_HEADS, ML_HEAD_DIM), 0.05),
        'mix_w_out': nrm(ks[14], (N_EVEN, MIX_WIDTH, D), MIX_WIDTH ** -0.5),
        'sg_w_in': nrm(ks[15], (N_ODD, D, 2 * SG_WIDTH), D ** -0.5),
        'sg_ln_g': 1.0 + nrm(ks[16], (N_ODD, SG_WIDTH), 0.05),
        'sg_ln_b': nrm(ks[17], (N_ODD, SG_WIDTH), 0.02),
        'sg_w_s': nrm(ks[18], (N_ODD, SG_GROUPS, SG_CHUNK, SG_CHUNK), 0.5 * SG_CHUNK ** -0.5),
        'sg_b_s': 1.0 + nrm(ks[19], (N_ODD, SG_GROUPS, SG_CHUNK), 0.1),
        'sg_w_out': nrm(ks[20], (N_ODD, SG_WIDTH, D), SG_WIDTH ** -0.5),
        'final_g': 1.0 + nrm(ks[21], (D,), 0.05),
    }

def second_block(x, c, ctx, c_ctx, w_mod, b_mod, norm_g, ffn_w_in, ffn_w_out, mix_w_in, na_rpb, ml_gate_b,
              ml_head_g, mix_w_out, sg_w_in, sg_ln_g, sg_ln_b, sg_w_s, sg_b_s, sg_w_out, final_g):
    B, N, D = x.shape
    last_ctx_layer = ((DEPTH_2 - 1) // 2) * 2
    silu_c = jax.nn.silu(c)
    silu_cx = jax.nn.silu(c_ctx)[None]
    xc = ctx
    for l in range(DEPTH_2):
        ctx_in = l <= last_ctx_layer
        ctx_out = l < last_ctx_layer
        mod = (silu_c @ w_mod[l] + b_mod[l]).reshape(B, 3 * N_SUB, 1, D)
        x = macaron_half_ffn(x, norm_g[l, 0], *mod_terms(mod, 0), ffn_w_in[l, 0], ffn_w_out[l, 0])
        sh, sc, gt = mod_terms(mod, 1)
        h = modulate(x, norm_g[l, 1], sh, sc)
        hx = None
        if ctx_in:
            modx = (silu_cx @ w_mod[l] + b_mod[l]).reshape(1, 3 * N_SUB, 1, D)
            xc = macaron_half_ffn(xc, norm_g[l, 0], *mod_terms(modx, 0), ffn_w_in[l, 0], ffn_w_out[l, 0])
            shx, scx, gtx = mod_terms(modx, 1)
            hx = modulate(xc, norm_g[l, 1], shx, scx)
        if l % 2 == 0:
            e = l // 2
            y, yx = even_mixer(h, hx, mix_w_in[e], na_rpb[e], ml_gate_b[e], ml_head_g[e], mix_w_out[e], ctx_out)
        else:
            o = l // 2
            y = spatial_gating(h, sg_w_in[o], sg_ln_g[o], sg_ln_b[o], sg_w_s[o], sg_b_s[o], sg_w_out[o])
            yx = (spatial_gating(hx, sg_w_in[o], sg_ln_g[o], sg_ln_b[o], sg_w_s[o], sg_b_s[o], sg_w_out[o])
                  if ctx_out else None)
        x = x + gt * y
        x = macaron_half_ffn(x, norm_g[l, 2], *mod_terms(mod, 2), ffn_w_in[l, 1], ffn_w_out[l, 1])
        if ctx_out:
            xc = xc + gtx * yx
            xc = macaron_half_ffn(xc, norm_g[l, 2], *mod_terms(modx, 2), ffn_w_in[l, 1], ffn_w_out[l, 1])
    return rms_norm(x, final_g)


def setup_inputs(seed=0):
    out = dict(first_inputs(seed))
    for name, value in second_inputs(seed + 1).items():
        if name != "x":
            out[name + "_2"] = value
    return out


def reference(
    x, ffn1_norm, ffn1_w_gu, ffn1_w_down, mix_norm, ffn2_norm, ffn2_w_gu, ffn2_w_down, gdn_w_in,
    gdn_conv, gdn_a_log, gdn_dt_bias, gdn_norm, gdn_w_out, sb_w_in, sb_w_out, dsa_w_in,
    dsa_cq_norm, dsa_ckv_norm, dsa_kidx_norm, dsa_w_uq, dsa_w_qidx, dsa_w_uk, dsa_w_uv,
    dsa_w_out, final_norm, c_2, ctx_2, c_ctx_2, w_mod_2, b_mod_2, norm_g_2, ffn_w_in_2,
    ffn_w_out_2, mix_w_in_2, na_rpb_2, ml_gate_b_2, ml_head_g_2, mix_w_out_2, sg_w_in_2,
    sg_ln_g_2, sg_ln_b_2, sg_w_s_2, sg_b_s_2, sg_w_out_2, final_g_2,
):
    x = first_block(
        x, ffn1_norm, ffn1_w_gu, ffn1_w_down, mix_norm, ffn2_norm, ffn2_w_gu, ffn2_w_down,
        gdn_w_in, gdn_conv, gdn_a_log, gdn_dt_bias, gdn_norm, gdn_w_out, sb_w_in, sb_w_out,
        dsa_w_in, dsa_cq_norm, dsa_ckv_norm, dsa_kidx_norm, dsa_w_uq, dsa_w_qidx, dsa_w_uk,
        dsa_w_uv, dsa_w_out, final_norm,
    )
    return second_block(
        x, c_2, ctx_2, c_ctx_2, w_mod_2, b_mod_2, norm_g_2, ffn_w_in_2, ffn_w_out_2, mix_w_in_2,
        na_rpb_2, ml_gate_b_2, ml_head_g_2, mix_w_out_2, sg_w_in_2, sg_ln_g_2, sg_ln_b_2,
        sg_w_s_2, sg_b_s_2, sg_w_out_2, final_g_2,
    )


_drawn_inputs = setup_inputs


def setup_inputs(seed=0):
    import zlib

    import numpy as np

    out = dict(_drawn_inputs(seed))
    spreads = {}
    factors = {'dsa_cq_norm': 3.309,
     'dsa_ckv_norm': 8.0,
     'dsa_kidx_norm': 3.391,
     'na_rpb_2': 47.613,
     'ml_head_g_2': 8.0,
     'sg_ln_g_2': 8.0,
     'sg_ln_b_2': 40.959,
     'sg_b_s_2': 3.888}
    for name, (base, spread) in spreads.items():
        noise = np.random.default_rng([zlib.crc32(name.encode()), seed]).standard_normal(out[name].shape)
        drawn = base * np.exp(spread * noise) if base else spread * noise
        out[name] = jnp.asarray(drawn.astype(out[name].dtype))
    for name, factor in factors.items():
        out[name] = (out[name] * factor).astype(out[name].dtype)
    return out
```

```python
import math
import concourse.bass as bass
from concourse import mybir
from contextlib import ExitStack

FP32 = mybir.dt.float32
ALU = mybir.AluOpType
ACT = mybir.ActivationFunctionType
AX = mybir.AxisListType

P = 128
D = 1024
KD = D // P
T = 256
TT = T // P
FF = 2816
EPS = 1e-6
CH = 256
NCH = FF // CH
NFT = FF // P
RING = 3
SLOT = 3 * KD * CH
PART = KD * CH
PEEL = NCH % RING
ITERS = NCH // RING
UPB = 3
PB = 512

PLAN = [("ffn", 0), ("gdn", 0), ("ffn", 1), ("ffn", 2), ("sb", 0), ("ffn", 3), ("ffn", 4), ("dsa", 0),
        ("ffn", 5), ("ffn", 6), ("gdn", 1), ("ffn", 7), ("final", 0), ("mod", 0), ("ffn", 8), ("ffn", 9), ("even", 0),
        ("ffn", 10), ("ffn", 11), ("sgu", 0), ("ffn", 12), ("final", 1)]
LOADS = {"ffn": NCH, "gdn": 8, "sb": 6, "dsa": 5, "mod": 24, "even": 7, "sgu": 10, "final": 0}
OWN_SIGNAL = {"gdn": 4, "sb": 2, "even": 5, "sgu": 6}
CTX_FFN = 8
NORMS = {"ffn": 1, "gdn": 1, "sb": 1, "dsa": 1, "mod": 0, "even": 2, "sgu": 1, "final": 0}


def places():
    out, loads, mixer_loads, norms, ffns, updates = [], 0, 0, 0, 0, 0
    for kind, n in PLAN:
        out.append(dict(kind=kind, n=n, load=loads, mixer_load=mixer_loads, norm=norms, layer=sum(k in ("gdn", "sb", "dsa") for k, _ in PLAN[:len(out)]), ffn=ffns, update=updates))
        loads += LOADS[kind]
        mixer_loads += LOADS[kind] - OWN_SIGNAL.get(kind, 0) if kind != "ffn" else 0
        norms += NORMS[kind]
        ffns += kind == "ffn"
        updates += kind != "mod" and not (kind == "ffn" and n == CTX_FFN)
    return out


PLACES = places()

INPUTS = ["x", "ffn1_norm", "ffn1_w_gu", "ffn1_w_down", "mix_norm", "ffn2_norm", "ffn2_w_gu", "ffn2_w_down",
          "gdn_w_in", "gdn_conv", "gdn_a_log", "gdn_dt_bias", "gdn_norm", "gdn_w_out", "sb_w_in", "sb_w_out",
          "dsa_w_in", "dsa_cq_norm", "dsa_ckv_norm", "dsa_kidx_norm", "dsa_w_uq", "dsa_w_qidx", "dsa_w_uk",
          "dsa_w_uv", "dsa_w_out", "final_norm", "c_2", "ctx_2", "c_ctx_2", "w_mod_2", "b_mod_2", "norm_g_2",
          "ffn_w_in_2", "ffn_w_out_2", "mix_w_in_2", "na_rpb_2", "ml_gate_b_2", "ml_head_g_2", "mix_w_out_2",
          "sg_w_in_2", "sg_ln_g_2", "sg_ln_b_2", "sg_w_s_2", "sg_b_s_2", "sg_w_out_2", "final_g_2"]

NGAIN = 20

ARENA = 19456
ROWS_DMAS = 16 * 6

C_IDENT = 0
C_NHALF = 128
C_ONES = 192
C_UPPER = 320
C_LOWER = 448
C_BLOCK = 576
C_SB = C_BLOCK + 7 * P
C_CNEG = C_SB + 384
C_ROPE16 = C_CNEG + 384
C_ROPE8 = C_ROPE16 + 64
C_AXIAL = C_ROPE8 + 32
C_FROM = C_AXIAL + 256
C_EARLIER = C_FROM + P
C_WINDOW = C_EARLIER + P
NCONST = C_WINDOW + 512


def rope_table(np, rot):
    half = rot // 2
    inv = np.float32(500000.0) ** (-np.arange(half, dtype=np.float32) * np.float32(2.0 / rot))
    ang = (np.arange(T, dtype=np.float32)[:, None] * inv[None, :]).astype(np.float32)
    return np.concatenate([np.cos(ang), np.sin(ang)], axis=1)


def constants(np):
    c = np.zeros((P, NCONST), np.float32)
    r, k = np.arange(P)[:, None], np.arange(P)[None, :]
    c[:, C_IDENT:C_IDENT + P] = r == k
    c[:, C_NHALF:C_NHALF + 64] = -0.5
    c[:, C_ONES:C_ONES + P] = 1
    c[:, C_UPPER:C_UPPER + P] = r <= k
    c[:, C_LOWER:C_LOWER + P] = r > k
    for n in range(7):
        m = 2 ** n
        c[:, C_BLOCK + n * P:C_BLOCK + (n + 1) * P] = (r // m % 2 == 1) & (k // m == r // m - 1)
    upper = (r < k).astype(np.float32)
    c[:, C_SB:C_SB + 384] = np.concatenate([upper, np.ones((P, P)), upper], axis=1)
    later = np.where(k > r, np.float32(-1e30), np.float32(0))
    c[:, C_CNEG:C_CNEG + 384] = np.concatenate([later, np.zeros((P, P)), later], axis=1)
    for t in range(TT):
        rows = slice(t * P, (t + 1) * P)
        c[:, C_ROPE16 + 32 * t:C_ROPE16 + 32 * t + 32] = rope_table(np, 32)[rows]
        c[:, C_ROPE8 + 16 * t:C_ROPE8 + 16 * t + 16] = rope_table(np, 16)[rows]
    c[:, C_FROM:C_FROM + P] = r >= k
    c[:, C_EARLIER:C_EARLIER + P] = np.where(k < r, np.float32(-1e30), np.float32(0))
    token = np.arange(T)
    inv = np.float32(10000.0) ** (-np.arange(32, dtype=np.float32) / np.float32(32))
    ang = np.concatenate([(token // 64).astype(np.float32)[:, None] * inv,
                          (token % 64).astype(np.float32)[:, None] * inv], axis=1)
    start = np.clip(token % 64 - 8, 0, 48)[:, None]
    inside = (token[None, :] % 64 >= start) & (token[None, :] % 64 < start + 16)
    for t in range(TT):
        rows = slice(t * P, (t + 1) * P)
        c[:, C_AXIAL + 128 * t:C_AXIAL + 128 * t + 64] = np.cos(ang)[rows]
        c[:, C_AXIAL + 128 * t + 64:C_AXIAL + 128 * t + 128] = np.sin(ang)[rows]
        c[:, C_WINDOW + T * t:C_WINDOW + T * (t + 1)] = np.where(inside[rows], np.float32(0), np.float32(-1e30))
    return c


def build(nc, A, out):
    ctx = ExitStack()

    def sb(name, shape):
        return ctx.enter_context(nc.sbuf_tensor(name, shape, FP32))

    def sem(name):
        return ctx.enter_context(nc.semaphore(name))

    ring = sb("ring", [P, RING, SLOT])
    x_sb = sb("x_sb", [P, TT, D])
    xn = sb("xn", [P, TT, D])
    hT = sb("hT", [P, KD, T])
    silu = sb("silu", [P, UPB, T])
    aT = sb("aT", [P, UPB, T])
    sumsq = sb("sumsq", [P, TT])
    rstd = sb("rstd", [P, TT])
    consts = sb("consts", [P, NCONST])
    h_flat = hT[:, :, :].rearrange("p k t -> p (k t)")
    gain_rows = h_flat[0:NGAIN, 0:D]
    col_rows = h_flat[:, D:D + 2 * P].rearrange("p (j c) -> p j c", j=2)
    cols_T = sb("cols_T", [P, 2, P])
    gain = sb("gain", [P, KD, NGAIN])
    ps = ctx.enter_context(nc.psum_tensor("ps", [P, 8, PB], FP32))
    ident = consts[:, C_IDENT:C_IDENT + P]

    x_loaded = sem("x_loaded")
    rows_loaded = sem("rows_loaded")
    consts_loaded = sem("consts_loaded")
    gains_loaded = sem("gains_loaded")
    gains_turned = sem("gains_turned")
    gains_ready = sem("gains_ready")
    load_done = [sem(f"load_done{i}") for i in range(RING)]
    load_used = sem("load_used")
    x_ready = sem("x_ready")
    sumsq_ready = sem("sumsq_ready")
    rstd_ready = sem("rstd_ready")
    xn_ready = sem("xn_ready")
    turned = sem("turned")
    hT_ready = sem("hT_ready")
    up_done = sem("up_done")
    silu_done = sem("silu_done")
    act_done = sem("act_done")
    down_done = sem("down_done")
    out_done = sem("out_done")
    dve_step = sem("dve_step")
    act_step = sem("act_step")
    pool_step = sem("pool_step")

    class Steps:

        def __init__(self, sem):
            self.sem, self.count = sem, 0

        def done(self, eng, ins):
            self.count += 1
            ins.then_inc(self.sem, 1)
            eng.wait_ge(self.sem, self.count)

    dve_steps, act_steps, pool_steps = Steps(dve_step), Steps(act_step), Steps(pool_step)

    def wait_loaded(pe, load):
        pe.wait_ge(load_done[load % RING], 48 * (load // RING + 1))

    def wait_slot_free(sp, load):
        before = load - RING
        if before < 0:
            return
        at = [at for at in PLACES if at["load"] <= before and LOADS[at["kind"]]][-1]
        if at["kind"] == "ffn":
            sp.wait_ge(down_done, NFT * at["ffn"] + 2 * (before - at["load"] + 1))
        elif before - at["load"] < OWN_SIGNAL.get(at["kind"], 0):
            n = before - at["load"] + 1
            if at["kind"] == "gdn":
                sp.wait_ge(gdn_qkv, NQKV * at["n"] + 6 * n)
            elif at["kind"] == "sb":
                sp.wait_ge(sb_qk, 6 * n)
            elif at["kind"] == "even":
                sp.wait_ge(even_ps, EVEN_ENDS[n - 1])
            else:
                sp.wait_ge(sgu_ps, min(6 * n, len(SGU)))
        else:
            before -= OWN_SIGNAL.get(at["kind"], 0)
            sp.wait_ge(load_used, at["mixer_load"] + before - at["load"] + 1)

    def slot(load):
        return ring[:, load % RING, :]

    def part(load, n):
        return ring[:, load % RING, n * PART:(n + 1) * PART]

    def norm_act(act, at, k=0, src=x_sb):
        n = at["norm"] + k
        for t in range(TT):
            if src is not x_sb:
                if at["kind"] == "ffn":
                    act.wait_ge(ctx_loaded, 48)
                else:
                    act.wait_ge(ctx_ready, t + 1)
                    if at["update"]:
                        act.wait_ge(x_ready, TT * at["update"])
            elif at["update"]:
                act.wait_ge(x_ready, TT * (at["update"] - 1) + t + 1)
            else:
                act.wait_ge(x_loaded, 16)
            if n:
                act.wait_ge(turned, 2 * TT * n)
            if at["kind"] == "ffn" and at["n"] == CTX_FFN + 1:
                act.wait_ge(ctx_ready, TT)
            nc.scalar.activation(xn[:, t, :], src[:, t, :], ACT.Square,
                                 accum_out=sumsq[:, t:t + 1]).then_inc(sumsq_ready, 1)

    def inv_sqrt(pool, dst, src, factor, eps):
        pool_steps.done(pool, nc.gpsimd.tensor_scalar(dst, src, factor, eps, ALU.mult, ALU.add))
        return nc.gpsimd.tensor_tensor(dst, dst, consts[:, C_NHALF:C_NHALF + dst.shape[-1]], ALU.pow)

    def norm_pool(pool, at, k=0):
        for t in range(TT):
            pool.wait_ge(sumsq_ready, TT * (at["norm"] + k) + t + 1)
            inv_sqrt(pool, rstd[:, t:t + 1], sumsq[:, t:t + 1], 1.0 / D, EPS).then_inc(rstd_ready, 1)

    def norm_dve(dve, at, scale, shift=None, k=0, src=x_sb, dst=hT):
        n = at["norm"] + k
        for t in range(TT):
            dve.wait_ge(rstd_ready, TT * n + t + 1)
            nc.vector.tensor_scalar(xn[:, t, :], src[:, t, :], rstd[:, t:t + 1], None,
                                    ALU.mult).then_inc(xn_ready, 1)
        for t in range(TT):
            for h in range(2):
                dve.wait_ge(turned, 2 * TT * n + 2 * t + h + 1)
                src_ps = ps[:, 4 + 2 * t + h, :].rearrange("p (k c) -> p k c", c=P)
                dst_h = dst[:, 4 * h:4 * h + 4, t * P:(t + 1) * P]
                g = scale[:, 4 * h:4 * h + 4, None].to_broadcast([P, 4, P])
                ins = nc.vector.tensor_tensor(dst_h, src_ps, g, ALU.mult)
                if shift is not None:
                    dve_steps.done(dve, ins)
                    s = shift[:, 4 * h:4 * h + 4, None].to_broadcast([P, 4, P])
                    ins = nc.vector.tensor_tensor(dst_h, dst_h, s, ALU.add)
                ins.then_inc(hT_ready, 1)

    def norm_pe(pe, at, k=0):
        n = at["norm"] + k
        for t in range(TT):
            pe.wait_ge(xn_ready, TT * n + t + 1)
            for h in range(2):
                for c in range(4):
                    col = (4 * h + c) * P
                    ins = nc.tensor.transpose(ps[:, 4 + 2 * t + h, c * P:(c + 1) * P],
                                              xn[:, t, col:col + P], ident)
                ins.then_inc(turned, 1)

    def ffn_weights(n):
        if n < 8:
            i, second = divmod(n, 2)
            gu, down = (A["ffn2_w_gu"], A["ffn2_w_down"]) if second else (A["ffn1_w_gu"], A["ffn1_w_down"])
            return gu[i], down[i]
        l, j = {8: (0, 0), 9: (0, 0), 10: (0, 1), 11: (1, 0), 12: (1, 1)}[n]
        return A["ffn_w_in_2"][l, j], A["ffn_w_out_2"][l, j]

    def ffn_sp(sp, at):
        gu, down = ffn_weights(at["n"])
        gu_v = gu.rearrange("(k p) f -> p k f", p=P)
        down_v = down.rearrange("(c j p) d -> c p j d", p=P, j=CH // P)

        def load(first, it=None):
            g = at["load"] + first
            s = g % RING
            if it is None:
                wait_slot_free(sp, g)
                col, chunk = first * CH, first
            else:
                sp.wait_ge(down_done, NFT * at["ffn"] + 2 * (first - RING + 1) + it * (2 * RING))
                col, chunk = first * CH + it * (RING * CH), it * RING + first
            for side in range(2):
                sp.dma_start(part(g, side).rearrange("p (k f) -> p k f", k=KD),
                             gu_v[:, :, bass.ds(col + side * FF, CH)]).then_inc(load_done[s], 16)
            sp.dma_start(part(g, 2).rearrange("p (j d) -> p j d", d=D),
                         down_v[bass.ds(chunk, 1)].rearrange("a p j d -> p (a j) d")).then_inc(load_done[s], 16)

        first_loop = PEEL + RING
        for c in range(first_loop):
            load(c)
        with sp.Fori(0, (NCH - first_loop) // RING) as it:
            for u in range(RING):
                load(first_loop + u, it)

    def ffn_pe(pe, at):
        norm_pe(pe, at)
        if at["n"] >= 8:
            gate_pe(pe, at)
        f0 = NFT * at["ffn"]
        pe.wait_ge(hT_ready, 2 * TT * (at["norm"] + 1))

        def up(i, it=None, step=0):
            g = at["load"] + i // 2
            if i % 2 == 0:
                n = 48 * (g // RING + 1)
                pe.wait_ge(load_done[g % RING], n if it is None else n + 48 * it)
            if f0 + i >= UPB:
                n = f0 + i - UPB + 1
                pe.wait_ge(act_done, n if it is None else n + step * it)
            bank = 4 + i % UPB
            for side in range(2):
                w = part(g, side).rearrange("p (k f) -> p k f", k=KD)
                for k in range(KD):
                    ins = nc.tensor.matmul(ps[:, bank, side * T:(side + 1) * T],
                                           w[:, k, (i % 2) * P:(i % 2 + 1) * P], hT[:, k, :],
                                           start=(k == 0), stop=(k == KD - 1))
            ins.then_inc(up_done, 1)

        def down(i, it=None, step=0, first=False, last=False):
            g = at["load"] + i // 2
            n = f0 + i + 1
            pe.wait_ge(act_done, n if it is None else n + step * it)
            w = part(g, 2).rearrange("p (j d) -> p j d", d=D)
            for t in range(TT):
                for h in range(2):
                    ins = nc.tensor.matmul(ps[:, 2 * t + h, :], aT[:, i % UPB, t * P:(t + 1) * P],
                                           w[:, i % 2, h * PB:(h + 1) * PB], start=first, stop=last,
                                           skip_group_check=True)
            ins.then_inc(down_done, 1)

        tiles0 = 2 * PEEL
        for i in range(tiles0):
            up(i)
            if i:
                down(i - 1, first=(i == 1))
        step = 2 * RING
        with pe.Fori(0, ITERS) as it:
            for u in range(step):
                up(tiles0 + u, it, step)
                down(tiles0 + u - 1, it, step)
        down(NFT - 1, last=True)

    def ffn_act(act, at):
        norm_act(act, at, src=x_ctx if at["n"] == CTX_FFN else x_sb)
        if at["n"] >= 8:
            gate_act(act, at)
        f0 = NFT * at["ffn"]

        def tile(i, it=None, step=0):
            def count(n):
                return n if it is None else n + step * it
            act.wait_ge(up_done, count(f0 + i + 1))
            if f0 + i >= UPB:
                act.wait_ge(act_done, count(f0 + i - UPB + 1))
            nc.scalar.activation(silu[:, i % UPB, :], ps[:, 4 + i % UPB, 0:T], ACT.Silu).then_inc(silu_done, 1)

        ffn_tiles(act, tile)

    def ffn_tiles(eng, tile):
        for i in range(2 * PEEL):
            tile(i)
        with eng.Fori(0, ITERS) as it:
            for u in range(2 * RING):
                tile(2 * PEEL + u, it, 2 * RING)

    def ffn_dve(dve, at):
        n, f0 = at["n"], NFT * at["ffn"]
        if n < 8:
            norm_dve(dve, at, gain[:, :, 8 * (n % 2) + n // 2])
        else:
            layer, j, cond, _ = GATES["ffn", n]
            norm_dve(dve, at, amp[:, 3 * layer + j + 6 * cond, :], mod_cols(layer, 3 * j, cond),
                     src=x_ctx if cond else x_sb)

        def tile(i, it=None, step=0):
            def count(n):
                return n if it is None else n + step * it
            dve.wait_ge(silu_done, count(f0 + i + 1))
            if f0 + i >= UPB:
                dve.wait_ge(down_done, count(f0 + i - UPB + 1))
            nc.vector.tensor_tensor(aT[:, i % UPB, :], silu[:, i % UPB, :], ps[:, 4 + i % UPB, T:2 * T],
                                    ALU.mult).then_inc(act_done, 1)

        ffn_tiles(dve, tile)
        dve.wait_ge(down_done, f0 + NFT)
        if n < 8:
            add_to_x(dve, x_sb, 0.5)
        elif n == CTX_FFN:
            add_to_x(dve, x_ctx, 1.0, gate_row, ctx_ready)
        else:
            add_to_x(dve, x_sb, 1.0, gate_row)

    def add_to_x(dve, dst, factor, row=None, signal=None):
        for t in range(TT):
            for h in range(2):
                cols = slice(h * PB, (h + 1) * PB)
                src = ps[:, 2 * t + h, :]
                if row is not None:
                    dve_steps.done(dve, nc.vector.tensor_tensor(xn[:, t, cols], src, row[:, cols], ALU.mult))
                    src = xn[:, t, cols]
                ins = nc.vector.scalar_tensor_tensor(out=dst[:, t, cols], in0=src, scalar=factor,
                                                     in1=dst[:, t, cols], op0=ALU.mult, op1=ALU.add)
                if h == 1:
                    ins.then_inc(signal or x_ready, 1)
                else:
                    dve_steps.done(dve, ins)

    GH = 8

    arena = sb("arena", [P, ARENA])
    mix_out_done = sem("mix_out_done")
    mix_in_ready = sem("mix_in_ready")

    class Carve:

        def __init__(self):
            self.at = 0

        def take(self, *shape):
            n = 1
            for s in shape:
                n *= s
            ap = arena[:, self.at:self.at + n]
            self.at += n
            assert self.at <= ARENA
            if len(shape) == 2:
                ap = ap.rearrange("p (a b) -> p a b", b=shape[1])
            if len(shape) == 3:
                ap = ap.rearrange("p (a b c) -> p a b c", b=shape[1], c=shape[2])
            return ap

    MIXERS = [a for a in PLACES if a["kind"] in ("gdn", "sb", "dsa", "even", "sgu")]

    MIX_IN = {"gdn": 4, "sb": GH, "dsa": GH, "even": 20, "sgu": 0}

    def mix_in_before(at):
        return sum(MIX_IN[a["kind"]] for a in MIXERS[:MIXERS.index(at)])

    def w_out_sp(sp, at, first, w, tiles=KD, per_load=4):
        w_v = w.rearrange("(k p) d -> p k d", p=P)
        for n in range(tiles // per_load):
            g = at["load"] + first + n
            wait_slot_free(sp, g)
            for m, (a, b) in enumerate(((0, 1), (1, 2), (2, per_load))):
                sp.dma_start(slot(g)[:, a * D:b * D].rearrange("p (k d) -> p k d", d=D),
                             w_v[:, per_load * n + a:per_load * n + b, :]).then_inc(load_done[g % RING], 16)

    def w_out_pe(pe, at, first, lhs, tiles=KD, per_load=4):
        if lhs is hT:
            pe.wait_ge(mix_in_ready, mix_in_before(at) + MIX_IN[at["kind"]])
        for k in range(tiles):
            g = at["load"] + first + k // per_load
            if k % per_load == 0:
                wait_loaded(pe, g)
            for t in range(TT):
                for h in range(2):
                    col = (k % per_load) * D + h * PB
                    ins = nc.tensor.matmul(ps[:, 2 * t + h, :], lhs[:, k, t * P:(t + 1) * P],
                                           slot(g)[:, col:col + PB], start=(k == 0), stop=(k == tiles - 1),
                                           skip_group_check=True)
            if k % per_load == per_load - 1:
                ins.then_inc(load_used, 1)

    def w_out_wait(eng, at):
        eng.wait_ge(load_used, at["mixer_load"] + LOADS[at["kind"]] - OWN_SIGNAL.get(at["kind"], 0))

    def bc_last(ap, n):
        return ap[:, :, None].to_broadcast([P, ap.shape[1], n])

    def bc_mid(ap, n):
        return ap[:, None, :].to_broadcast([P, n, ap.shape[1]])

    def col(name, n=P):
        return consts[:, name:name + n]

    NQKV, LEVELS = 24, 7
    HG = 2
    GW = 4 * P
    car = Carve()
    g_tok = car.take(TT, 3 * D)
    g_T = car.take(16, T)
    g_z = car.take(TT, D)
    g_L, g_C, g_Ti, g_V, g_W, g_QK = (car.take(HG, GW) for _ in range(6))
    g_S = car.take(GH, P)
    g_sq = g_T[:, 0:8, :].rearrange("p c t -> p (c t)")
    g_small = sb("g_small", [P, 256])
    g_in = g_small[:, 0:16]
    g_g = g_small[:, 16:32]
    g_beta = g_small[:, 32:48]
    g_gc = g_small[:, 48:64]
    g_eg = g_small[:, 64:80]
    g_kd = g_small[:, 80:88]
    g_nb = g_small[:, 88:96]
    g_t1 = g_small[:, 96:112]
    g_t2 = g_small[:, 112:128]
    g_ss = g_small[:, 128:160]
    g_oss = g_small[:, 160:176]
    g_A = g_small[:, 176:184]
    g_rows = sb("g_rows", [P, 2, 16])
    g_cw = cols_T[:, :, 0:96]
    g_ng = cols_T[:, 0, 96:98]

    gdn_qkv = sem("gdn_qkv")
    gdn_tap = sem("gdn_tap")
    gdn_conv = sem("gdn_conv")
    gdn_silu = sem("gdn_silu")
    gdn_flip = sem("gdn_flip")
    gdn_tok = sem("gdn_tok")
    gdn_zps = sem("gdn_zps")
    gdn_z = sem("gdn_z")
    gdn_gps = sem("gdn_gps")
    gdn_y = sem("gdn_y")
    gdn_sp = sem("gdn_sp")
    gdn_g = sem("gdn_g")
    gdn_gcps = sem("gdn_gcps")
    gdn_gc = sem("gdn_gc")
    gdn_eg = sem("gdn_eg")
    gdn_ss = sem("gdn_ss")
    gdn_rs = sem("gdn_rs")
    gdn_n = sem("gdn_n")
    gdn_Tps = sem("gdn_Tps")
    gdn_T = sem("gdn_T")
    gdn_kd = sem("gdn_kd")
    gdn_prep = sem("gdn_prep")
    gdn_D = sem("gdn_D")
    gdn_E = sem("gdn_E")
    gdn_L = sem("gdn_L")
    gdn_C = sem("gdn_C")
    gdn_Wps = sem("gdn_Wps")
    gdn_W = sem("gdn_W")
    gdn_TV = sem("gdn_TV")
    gdn_V = sem("gdn_V")
    gdn_ks = sem("gdn_ks")
    gdn_r = sem("gdn_r")
    gdn_ups = sem("gdn_ups")
    gdn_u = sem("gdn_u")
    gdn_Sps = sem("gdn_Sps")
    gdn_S = sem("gdn_S")
    gdn_ops = sem("gdn_ops")
    gdn_o = sem("gdn_o")
    gdn_on = sem("gdn_on")
    gdn_oT = sem("gdn_oT")

    def gdn_sp_(sp, at):
        w = A["gdn_w_in"][at["n"]].rearrange("(k p) c -> p k c", p=P)

        def cols(g, n, c, width=CH):
            return sp.dma_start(part(g, n)[:, 0:KD * width].rearrange("p (k c) -> p k c", k=KD),
                                w[:, :, c:c + width])

        for n in range(4):
            g = at["load"] + n
            wait_slot_free(sp, g)
            for m in range(3):
                cols(g, m, (3 * n + m) * CH).then_inc(load_done[g % RING], 16)
        g = at["load"] + 4
        wait_slot_free(sp, g)
        for m in range(3):
            cols(g, m, 3 * D + m * CH).then_inc(load_done[g % RING], 16)
        g = at["load"] + 5
        wait_slot_free(sp, g)
        cols(g, 0, 3 * D + 3 * CH).then_inc(load_done[g % RING], 16)
        cols(g, 1, 4 * D, 16).then_inc(load_done[g % RING], 32)
        w_out_sp(sp, at, 6, A["gdn_w_out"][at["n"]])

    def gdn_pe(pe, at):
        j = at["n"]
        norm_pe(pe, at)
        pe.wait_ge(hT_ready, 2 * TT * (at["norm"] + 1))

        def turn(c):
            pe.wait_ge(gdn_silu, NQKV * j + c + 1)
            if NQKV * j + c >= 3:
                pe.wait_ge(gdn_tok, NQKV * j + c - 2)
            for t in range(TT):
                ins = nc.tensor.transpose(ps[:, 4 + c % 3, t * P:(t + 1) * P],
                                          silu[:, c % 3, t * P:(t + 1) * P], ident)
            ins.then_inc(gdn_flip, 1)

        for c in range(NQKV):
            g = at["load"] + c // 6
            if c % 6 == 0:
                wait_loaded(pe, g)
            if NQKV * j + c >= 3:
                pe.wait_ge(gdn_conv, NQKV * j + c - 2)
            w = part(g, c % 6 // 2).rearrange("p (k c) -> p k c", k=KD)
            for k in range(KD):
                ins = nc.tensor.matmul(ps[:, c % 3, 0:T], w[:, k, (c % 2) * P:(c % 2 + 1) * P], hT[:, k, :],
                                       start=(k == 0), stop=(k == KD - 1))
            ins.then_inc(gdn_qkv, 1)
            if c >= 2:
                turn(c - 2)
        turn(NQKV - 2)
        turn(NQKV - 1)
        pe.wait_ge(gdn_conv, NQKV * (j + 1))
        pe.wait_ge(gdn_tok, NQKV * (j + 1))
        for q in range(4):
            g = at["load"] + 4 + q // 3
            if q % 3 == 0:
                wait_loaded(pe, g)
            w = part(g, q % 3).rearrange("p (k c) -> p k c", k=KD)
            for t in range(TT):
                for k in range(KD):
                    ins = nc.tensor.matmul(ps[:, 2 * t + q // 2, (q % 2) * CH:(q % 2 + 1) * CH],
                                           hT[:, k, t * P:(t + 1) * P], w[:, k, :],
                                           start=(k == 0), stop=(k == KD - 1))
                if q % 2:
                    ins.then_inc(gdn_zps, 1)
            if q == 2:
                ins.then_inc(load_used, 1)
        w = part(g, 1)[:, 0:16 * KD].rearrange("p (k c) -> p k c", k=KD)
        for t in range(TT):
            for k in range(KD):
                ins = nc.tensor.matmul(ps[:, 7, t * 16:(t + 1) * 16], hT[:, k, t * P:(t + 1) * P], w[:, k, :],
                                       start=(k == 0), stop=(k == KD - 1))
        ins.then_inc(load_used, 1)
        pe.wait_ge(gdn_g, j + 1)
        for t in range(TT):
            nc.tensor.matmul(ps[:, 7, 64 + 8 * t:72 + 8 * t], col(C_UPPER), g_g[:, 8 * t:8 * t + 8],
                             start=True, stop=True)
        nc.tensor.matmul(ps[:, 7, 80:88], col(C_ONES), g_g[:, 0:8], start=True, stop=True).then_inc(gdn_gcps, 1)
        for t in range(TT):
            pe.wait_ge(gdn_n, TT * j + t + 1)
            for q in range(4):
                if t == 0 and q == 0:
                    pe.wait_ge(gdn_z, 4 * (j + 1))
                if t == 1:
                    pe.wait_ge(gdn_T, 8 * j + q + 1)
                for c in range(4):
                    ins = nc.tensor.transpose(ps[:, q, c * P:(c + 1) * P],
                                              g_tok[:, t, (4 * q + c) * P:(4 * q + c + 1) * P], ident)
                ins.then_inc(gdn_Tps, 1)
        pe.wait_ge(gdn_T, 8 * (j + 1))
        for t in range(TT):
            for hg in range(HG):
                if t == 1:
                    pe.wait_ge(gdn_u, 4 * j + hg + 1)
                    pe.wait_ge(gdn_S, 2 * j + hg + 1)
                    pe.wait_ge(gdn_o, 4 * j + hg + 1)
                for h4 in range(4):
                    h, cs = 4 * hg + h4, slice(h4 * P, (h4 + 1) * P)
                    q_h, k_h = (g_T[:, h + o, t * P:(t + 1) * P] for o in (0, GH))
                    nc.tensor.matmul(ps[:, hg, cs], k_h, k_h, start=True, stop=True)
                    nc.tensor.matmul(ps[:, 2 + hg, cs], k_h, q_h, start=True, stop=True)
                    ins = nc.tensor.matmul(ps[:, 4 + hg, cs],
                                           g_g[:, 8 * t + h:8 * t + h + 1].to_broadcast([P, P]), col(C_UPPER),
                                           start=True, stop=True)
                ins.then_inc(gdn_prep, 1)
            for lv in range(LEVELS):
                for hg in range(HG):
                    pe.wait_ge(gdn_C, 28 * j + (LEVELS * t + lv) * HG + hg + 1)
                    if lv:
                        pe.wait_ge(gdn_V, 28 * j + (LEVELS * t + lv - 1) * HG + hg + 1)
                    for h4 in range(4):
                        cs = slice(h4 * P, (h4 + 1) * P)
                        if lv == 0:
                            ins = nc.tensor.transpose(ps[:, hg, cs], g_C[:, hg, cs], ident)
                        else:
                            ins = nc.tensor.matmul(ps[:, hg, cs], g_C[:, hg, cs], g_V[:, hg, cs],
                                                   start=True, stop=True)
                    ins.then_inc(gdn_Wps, 1)
                if lv == 0:
                    continue
                for hg in range(HG):
                    pe.wait_ge(gdn_W, 24 * j + ((LEVELS - 1) * t + lv - 1) * HG + hg + 1)
                    for h4 in range(4):
                        cs = slice(h4 * P, (h4 + 1) * P)
                        if lv < LEVELS - 1:
                            nc.tensor.matmul(ps[:, 2 + hg, cs], g_W[:, hg, cs], g_Ti[:, hg, cs],
                                             start=True, stop=True)
                        ins = nc.tensor.matmul(ps[:, 4 + hg, cs], g_Ti[:, hg, cs], g_W[:, hg, cs],
                                               start=True, stop=True)
                    ins.then_inc(gdn_TV, 1)
            for hg in range(HG):
                heads = [(4 * hg + h4, slice(h4 * P, (h4 + 1) * P)) for h4 in range(4)]
                pe.wait_ge(gdn_kd, j + 1)
                pe.wait_ge(gdn_V, 28 * j + (LEVELS * t + LEVELS - 1) * HG + hg + 1)
                if t == 1:
                    for h, cs in heads:
                        nc.tensor.matmul(ps[:, 6 + hg, cs], g_T[:, h, P:T], g_S[:, h, :], start=True, stop=True)
                        ins = nc.tensor.matmul(ps[:, 2 + hg, cs], g_T[:, GH + h, P:T], g_S[:, h, :],
                                               start=True, stop=True)
                    ins.then_inc(gdn_ks, 1)
                    pe.wait_ge(gdn_r, 2 * j + hg + 1)
                for h, cs in heads:
                    ins = nc.tensor.matmul(ps[:, hg, cs], g_V[:, hg, cs],
                                           g_tok[:, t, 2 * D + h * P:2 * D + (h + 1) * P], start=True, stop=True)
                ins.then_inc(gdn_ups, 1)
                pe.wait_ge(gdn_u, 4 * j + 2 * t + hg + 1)
                if t == 0:
                    for h, cs in heads:
                        ins = nc.tensor.matmul(ps[:, 2 + hg, cs], g_tok[:, 0, D + h * P:D + (h + 1) * P],
                                               g_tok[:, 0, 2 * D + h * P:2 * D + (h + 1) * P],
                                               start=True, stop=True)
                    ins.then_inc(gdn_Sps, 1)
                for h, cs in heads:
                    ins = nc.tensor.matmul(ps[:, 4 + hg, cs], g_QK[:, hg, cs],
                                           g_tok[:, t, 2 * D + h * P:2 * D + (h + 1) * P], start=True, stop=True)
                ins.then_inc(gdn_ops, 1)
        heads_to_hT_pe(pe, xn, gdn_on, TT * j, gdn_oT)
        w_out_pe(pe, at, 6, hT)

    def heads_to_hT_pe(pe, src, ready, before, turned_sem):
        for t in range(TT):
            pe.wait_ge(ready, before + t + 1)
            for h in range(2):
                for c in range(4):
                    ins = nc.tensor.transpose(ps[:, 4 + 2 * t + h, c * P:(c + 1) * P],
                                              src[:, t, (4 * h + c) * P:(4 * h + c + 1) * P], ident)
                ins.then_inc(turned_sem, 1)

    def gdn_act(act, at):
        j = at["n"]
        act.wait_ge(gains_ready, 3)
        act.wait_ge(rows_loaded, ROWS_DMAS)
        norm_act(act, at)

        def tap(c):
            act.wait_ge(gdn_qkv, NQKV * j + c + 1)
            if NQKV * j + c >= 3:
                act.wait_ge(gdn_silu, NQKV * j + c - 2)
            nc.scalar.activation(aT[:, c % 3, :], ps[:, c % 3, 0:T], ACT.Copy,
                                 scale=g_cw[:, j, 3 * NQKV + c:3 * NQKV + c + 1]).then_inc(gdn_tap, 1)

        def silu_of(c):
            act.wait_ge(gdn_conv, NQKV * j + c + 1)
            if NQKV * j + c >= 3:
                act.wait_ge(gdn_flip, NQKV * j + c - 2)
            nc.scalar.activation(silu[:, c % 3, :], aT[:, c % 3, :], ACT.Silu).then_inc(gdn_silu, 1)

        def to_tok(c):
            act.wait_ge(gdn_flip, NQKV * j + c + 1)
            nc.scalar.activation(g_tok[:, :, c * P:(c + 1) * P],
                                 ps[:, 4 + c % 3, 0:T].rearrange("p (t c) -> p t c", t=TT), ACT.Copy)\
                .then_inc(gdn_tok, 1)

        for c in range(NQKV + 2):
            if c < NQKV:
                tap(c)
            if 1 <= c <= NQKV:
                silu_of(c - 1)
            if c >= 2:
                to_tok(c - 2)
        for n, (h, t) in enumerate(((0, 0), (0, 1), (1, 0), (1, 1))):
            act.wait_ge(gdn_zps, 4 * j + n + 1)
            nc.scalar.activation(g_z[:, t, h * PB:(h + 1) * PB], ps[:, 2 * t + h, :], ACT.Silu).then_inc(gdn_z, 1)
        act.wait_ge(gdn_y, j + 1)
        nc.scalar.activation(g_beta, ps[:, 7, 0:32].rearrange("p (t c) -> p t c", t=TT)[:, :, 0:8], ACT.Exp,
                             scale=-1.0)
        act_steps.done(act, nc.scalar.activation(g_t1, g_in, ACT.Abs))
        act_steps.done(act, nc.scalar.activation(g_t2, g_t1, ACT.Exp, scale=-1.0))
        nc.scalar.activation(g_A, g_rows[:, j, 8:16], ACT.Exp)
        nc.scalar.activation(g_t1, g_t2, ACT.Ln, bias=1.0).then_inc(gdn_sp, 1)
        act.wait_ge(gdn_gc, j + 1)
        nc.scalar.activation(g_kd, g_t2[:, 0:8], ACT.Exp)
        nc.scalar.activation(g_eg, g_gc, ACT.Exp).then_inc(gdn_eg, 1)
        for t in range(TT):
            for q in range(4):
                act.wait_ge(gdn_Tps, 8 * j + 4 * t + q + 1)
                nc.scalar.activation(g_T[:, 4 * q:4 * q + 4, t * P:(t + 1) * P],
                                     ps[:, q, :].rearrange("p (c i) -> p c i", c=4), ACT.Copy).then_inc(gdn_T, 1)
        for t in range(TT):
            for hg in range(HG):
                act.wait_ge(gdn_D, 4 * j + 2 * t + hg + 1)
                nc.scalar.activation(g_QK[:, hg, :], g_QK[:, hg, :], ACT.Exp)
                nc.scalar.activation(g_L[:, hg, :], g_L[:, hg, :], ACT.Exp, scale=-1.0).then_inc(gdn_E, 1)
            for lv in range(1, LEVELS):
                for hg in range(HG):
                    act.wait_ge(gdn_Wps, 28 * j + (LEVELS * t + lv) * HG + hg + 1)
                    if lv > 1:
                        act.wait_ge(gdn_TV, 24 * j + ((LEVELS - 1) * t + lv - 2) * HG + hg + 1)
                    nc.scalar.activation(g_W[:, hg, :], ps[:, hg, :], ACT.Copy).then_inc(gdn_W, 1)
            for hg in range(HG):
                act.wait_ge(gdn_ups, 4 * j + 2 * t + hg + 1)
                nc.scalar.activation(g_tok[:, t, 2 * D + hg * GW:2 * D + (hg + 1) * GW], ps[:, hg, :], ACT.Copy)\
                    .then_inc(gdn_u, 1)
                if t == 0:
                    act.wait_ge(gdn_Sps, 2 * j + hg + 1)
                    nc.scalar.activation(g_S[:, 4 * hg:4 * hg + 4, :],
                                         ps[:, 2 + hg, :].rearrange("p (h c) -> p h c", c=P), ACT.Copy)\
                        .then_inc(gdn_S, 1)

    def gdn_dve(dve, at):
        j = at["n"]
        dve.wait_ge(rows_loaded, ROWS_DMAS)
        norm_dve(dve, at, gain[:, :, 4 + at["layer"]])
        step = dve_steps.done
        for c in range(NQKV):
            dve.wait_ge(gdn_tap, NQKV * j + c + 1)
            w = [g_cw[:, j, tap * NQKV + c:tap * NQKV + c + 1] for tap in range(4)]
            acc, x_c = aT[:, c % 3, :], ps[:, c % 3, 0:T]
            for back in (1, 2, 3):
                ins = nc.vector.scalar_tensor_tensor(out=acc[:, back:T], in0=x_c[:, 0:T - back],
                                                     scalar=w[3 - back], in1=acc[:, back:T],
                                                     op0=ALU.mult, op1=ALU.add)
                if back < 3:
                    step(dve, ins)
            ins.then_inc(gdn_conv, 1)
        dve.wait_ge(load_used, at["mixer_load"] + 2)
        gates = ps[:, 7, 0:32].rearrange("p (t c) -> p t c", t=TT)
        nc.vector.tensor_tensor(g_in.rearrange("p (t h) -> p t h", t=TT), gates[:, :, 8:16],
                                bc_mid(g_rows[:, j, 0:8], TT), ALU.add).then_inc(gdn_y, 1)
        dve.wait_ge(gdn_sp, j + 1)
        step(dve, nc.vector.tensor_scalar(g_beta, g_beta, 1.0, None, ALU.add))
        step(dve, nc.vector.reciprocal(g_beta, g_beta))
        step(dve, nc.vector.scalar_tensor_tensor(out=g_g, in0=g_in, scalar=0.0, in1=g_t1, op0=ALU.max, op1=ALU.add))
        nc.vector.scalar_tensor_tensor(out=g_g.rearrange("p (t h) -> p t h", t=TT),
                                       in0=g_g.rearrange("p (t h) -> p t h", t=TT), scalar=-1.0,
                                       in1=bc_mid(g_A, TT), op0=ALU.mult, op1=ALU.mult).then_inc(gdn_g, 1)
        for t in range(TT):
            dve.wait_ge(gdn_tok, NQKV * (j + 1))
            step(dve, nc.vector.tensor_tensor(g_sq, g_tok[:, t, 0:2 * D], g_tok[:, t, 0:2 * D], ALU.mult))
            nc.vector.tensor_reduce(g_ss[:, 16 * t:16 * t + 16], g_sq.rearrange("p (c d) -> p c d", d=P), AX.X,
                                    ALU.add).then_inc(gdn_ss, 1)
            dve.wait_ge(gdn_ss, 3 * j + t + 1)
        dve.wait_ge(gdn_gcps, j + 1)
        step(dve, nc.vector.tensor_copy(g_gc, ps[:, 7, 64:80]))
        nc.vector.tensor_tensor(g_t2[:, 0:8], ps[:, 7, 80:88], g_gc[:, 0:8], ALU.subtract).then_inc(gdn_gc, 1)
        for t in range(TT):
            dve.wait_ge(gdn_rs, 3 * j + t + 1)
            qk = g_tok[:, t, 0:2 * D].rearrange("p (c d) -> p c d", d=P)
            nc.vector.tensor_tensor(qk, qk, bc_last(g_ss[:, 16 * t:16 * t + 16], P), ALU.mult).then_inc(gdn_n, 1)
        for t in range(TT):
            v = g_tok[:, t, 2 * D:3 * D].rearrange("p (h d) -> p h d", d=P)
            step(dve, nc.vector.tensor_tensor(v, v, bc_last(g_beta[:, 8 * t:8 * t + 8], P), ALU.mult))
        dve.wait_ge(gdn_eg, j + 1)
        step(dve, nc.vector.scalar_tensor_tensor(out=g_nb, in0=g_beta[:, 8:16], scalar=-1.0, in1=g_eg[:, 8:16],
                                                 op0=ALU.mult, op1=ALU.mult))
        dve.wait_ge(gdn_Tps, 8 * j + 4)
        k0 = g_tok[:, 0, D:2 * D].rearrange("p (h d) -> p h d", d=P)
        nc.vector.tensor_tensor(k0, k0, bc_last(g_kd, P), ALU.mult).then_inc(gdn_kd, 1)

        def wide(ap):
            return ap.rearrange("p (h c) -> p h c", c=P)

        for t in range(TT):
            for hg in range(HG):
                cols = slice(8 * t + 4 * hg, 8 * t + 4 * hg + 4)
                dve.wait_ge(gdn_prep, 4 * j + 2 * t + hg + 1)
                if t or j:
                    dve.wait_ge(gdn_C, 28 * j + LEVELS * t * HG)
                step(dve, nc.vector.tensor_tensor(wide(g_W[:, hg, :]), wide(ps[:, 4 + hg, :]),
                                                  bc_last(g_gc[:, cols], P), ALU.subtract))
                step(dve, nc.vector.tensor_scalar(g_QK[:, hg, :], g_W[:, hg, :], 0.0, None, ALU.min))
                nc.vector.tensor_scalar(g_L[:, hg, :], g_W[:, hg, :], 0.0, None, ALU.max).then_inc(gdn_D, 1)
            for hg in range(HG):
                cols = slice(8 * t + 4 * hg, 8 * t + 4 * hg + 4)
                qk, lo = wide(g_QK[:, hg, :]), wide(g_L[:, hg, :])
                dve.wait_ge(gdn_E, 4 * j + 2 * t + hg + 1)
                step(dve, nc.vector.tensor_tensor(qk, qk, bc_mid(col(C_UPPER), 4), ALU.mult))
                step(dve, nc.vector.tensor_tensor(g_QK[:, hg, :], g_QK[:, hg, :], ps[:, 2 + hg, :], ALU.mult))
                step(dve, nc.vector.tensor_tensor(lo, lo, bc_mid(col(C_LOWER), 4), ALU.mult))
                step(dve, nc.vector.tensor_tensor(lo, lo, bc_last(g_beta[:, cols], P), ALU.mult))
                nc.vector.tensor_tensor(g_L[:, hg, :], g_L[:, hg, :], ps[:, hg, :], ALU.mult).then_inc(gdn_L, 1)
            for lv in range(LEVELS):
                for hg in range(HG):
                    Ti, V = g_Ti[:, hg, :], g_V[:, hg, :]
                    if lv == 0:
                        dve.wait_ge(gdn_Wps, 28 * j + LEVELS * t * HG + hg + 1)
                        step(dve, nc.vector.tensor_tensor(wide(Ti), bc_mid(ident, 4), wide(g_C[:, hg, :]),
                                                          ALU.subtract))
                        nc.vector.tensor_tensor(wide(V), bc_mid(ident, 4), wide(ps[:, hg, :]),
                                                ALU.subtract).then_inc(gdn_V, 1)
                    else:
                        dve.wait_ge(gdn_TV, 24 * j + ((LEVELS - 1) * t + lv - 1) * HG + hg + 1)
                        if lv < LEVELS - 1:
                            step(dve, nc.vector.tensor_tensor(Ti, Ti, ps[:, 2 + hg, :], ALU.subtract))
                        nc.vector.tensor_tensor(V, V, ps[:, 4 + hg, :], ALU.subtract).then_inc(gdn_V, 1)
                    dve.wait_ge(gdn_V, 28 * j + (LEVELS * t + lv) * HG + hg + 1)
            for hg in range(HG):
                o = xn[:, t, hg * GW:(hg + 1) * GW]
                if t == 1:
                    dve.wait_ge(gdn_ks, 2 * j + hg + 1)
                    v = wide(g_tok[:, 1, 2 * D + hg * GW:2 * D + (hg + 1) * GW])
                    step(dve, nc.vector.tensor_tensor(wide(g_C[:, hg, :]), wide(ps[:, 2 + hg, :]),
                                                      bc_last(g_nb[:, 4 * hg:4 * hg + 4], P), ALU.mult))
                    nc.vector.tensor_tensor(v, v, wide(g_C[:, hg, :]), ALU.add).then_inc(gdn_r, 1)
                    step(dve, nc.vector.tensor_tensor(wide(o), wide(ps[:, 6 + hg, :]),
                                                      bc_last(g_eg[:, 8 + 4 * hg:12 + 4 * hg], P), ALU.mult))
                dve.wait_ge(gdn_ops, 4 * j + 2 * t + hg + 1)
                if t == 0:
                    ins = nc.vector.tensor_copy(o, ps[:, 4 + hg, :])
                else:
                    ins = nc.vector.tensor_tensor(o, o, ps[:, 4 + hg, :], ALU.add)
                ins.then_inc(gdn_o, 1)
        dve.wait_ge(gdn_o, 4 * (j + 1))
        for t in range(TT):
            step(dve, nc.vector.tensor_tensor(g_sq[:, t * D:(t + 1) * D], xn[:, t, :], xn[:, t, :], ALU.mult))
        nc.vector.tensor_reduce(g_oss, g_sq.rearrange("p (c d) -> p c d", d=P), AX.X, ALU.add).then_inc(gdn_ss, 1)
        dve.wait_ge(gdn_rs, 3 * j + 3)
        for t in range(TT):
            o = wide(xn[:, t, :])
            step(dve, nc.vector.tensor_tensor(o, o, bc_last(g_oss[:, 8 * t:8 * t + 8], P), ALU.mult))
            nc.vector.tensor_tensor(xn[:, t, :], xn[:, t, :], g_z[:, t, :], ALU.mult).then_inc(gdn_on, 1)
        for t in range(TT):
            for h in range(2):
                dve.wait_ge(gdn_oT, 4 * j + 2 * t + h + 1)
                nc.vector.tensor_scalar(hT[:, 4 * h:4 * h + 4, t * P:(t + 1) * P], wide(ps[:, 4 + 2 * t + h, :]),
                                        g_ng[:, j:j + 1], None, ALU.mult).then_inc(mix_in_ready, 1)
        w_out_wait(dve, at)
        add_to_x(dve, x_sb, 1.0)

    def gdn_pool(pool, at):
        j = at["n"]
        norm_pool(pool, at)
        for t in range(TT):
            pool.wait_ge(gdn_ss, 3 * j + t + 1)
            ss = g_ss[:, 16 * t:16 * t + 16]
            pool_steps.done(pool, nc.gpsimd.tensor_scalar(ss[:, 0:8], ss[:, 0:8], float(P), P * EPS, ALU.mult, ALU.add))
            pool_steps.done(pool, nc.gpsimd.tensor_scalar(ss[:, 8:16], ss[:, 8:16], EPS, None, ALU.add))
            nc.gpsimd.tensor_tensor(ss, ss, consts[:, C_NHALF:C_NHALF + 16], ALU.pow).then_inc(gdn_rs, 1)
        for t in range(TT):
            for lv in range(LEVELS):
                for hg in range(HG):
                    pool.wait_ge(gdn_L, 4 * j + 2 * t + hg + 1)
                    if lv == 1:
                        pool.wait_ge(gdn_V, 28 * j + (LEVELS * t + lv - 1) * HG + hg + 1)
                    if lv:
                        pool.wait_ge(gdn_Wps, 28 * j + (LEVELS * t + lv - 1) * HG + hg + 1)
                    nc.gpsimd.tensor_tensor(g_C[:, hg, :].rearrange("p (h c) -> p h c", c=P),
                                            g_L[:, hg, :].rearrange("p (h c) -> p h c", c=P),
                                            bc_mid(col(C_BLOCK + lv * P), 4), ALU.mult).then_inc(gdn_C, 1)
        pool.wait_ge(gdn_ss, 3 * j + 3)
        inv_sqrt(pool, g_oss, g_oss, 1.0 / P, EPS).then_inc(gdn_rs, 1)

    SC = 3 * P
    car = Carve()
    s_qk = car.take(16, T)
    s_v = car.take(TT, D)
    s_t, s_lb, s_lf, s_att = (car.take(3, SC) for _ in range(4))
    sb_qk = sem("sb_qk")
    sb_qks = sem("sb_qks")
    sb_vs = sem("sb_vs")
    sb_z = sem("sb_z")
    sb_t = sem("sb_t")
    sb_lf = sem("sb_lf")
    sb_cum = sem("sb_cum")
    sb_la = sem("sb_la")
    sb_e = sem("sb_e")
    sb_att = sem("sb_att")
    sb_o = sem("sb_o")

    def sb_sp(sp, at):
        w = A["sb_w_in"][at["n"]].rearrange("(k p) c -> p k c", p=P)
        for n in range(4):
            g = at["load"] + n
            wait_slot_free(sp, g)
            for m in range(3):
                c = (3 * n + m) * CH
                sp.dma_start(part(g, m).rearrange("p (k c) -> p k c", k=KD), w[:, :, c:c + CH])\
                    .then_inc(load_done[g % RING], 16)
        w_out_sp(sp, at, 4, A["sb_w_out"][at["n"]])

    def sb_pe(pe, at):
        norm_pe(pe, at)
        pe.wait_ge(hT_ready, 2 * TT * (at["norm"] + 1))
        for q in range(12):
            g = at["load"] + q // 3
            if q % 3 == 0:
                wait_loaded(pe, g)
            w = part(g, q % 3).rearrange("p (k c) -> p k c", k=KD)
            for i in range(2):
                if q < 8:
                    c = 2 * q + i
                    if c >= 4:
                        pe.wait_ge(sb_qks, c - 3)
                    for k in range(KD):
                        ins = nc.tensor.matmul(ps[:, c % 4, 0:T], w[:, k, i * P:(i + 1) * P], hT[:, k, :],
                                               start=(k == 0), stop=(k == KD - 1))
                    ins.then_inc(sb_qk, 1)
                else:
                    for k in range(KD):
                        ins = nc.tensor.matmul(ps[:, 4 + 2 * i + (q - 8) // 2, (q % 2) * CH:(q % 2 + 1) * CH],
                                               hT[:, k, i * P:(i + 1) * P], w[:, k, :],
                                               start=(k == 0), stop=(k == KD - 1))
                    if i == 1 and q in (8, 11):
                        ins.then_inc(load_used, 1)
        pe.wait_ge(sb_qks, 16)
        for i in range(GH + 2):
            if i < GH:
                if i >= 2:
                    pe.wait_ge(sb_lf, i - 1)
                nc.tensor.matmul(ps[:, i % 2, 0:T], s_qk[:, GH + i, 0:P], s_qk[:, i, :], start=True, stop=True)
                nc.tensor.matmul(ps[:, i % 2, T:SC], s_qk[:, GH + i, P:T], s_qk[:, i, P:T],
                                 start=True, stop=True).then_inc(sb_z, 1)
            if 1 <= i <= GH:
                h = i - 1
                lf, bank = s_lf[:, h % 3, :], ps[:, 2 + h % 2, :]
                pe.wait_ge(sb_lf, h + 1)
                if h >= 2:
                    pe.wait_ge(sb_la, h - 1)
                nc.tensor.matmul(bank[:, T:SC], col(C_LOWER), lf[:, T:SC], start=True, stop=True)
                nc.tensor.matmul(bank[:, 0:T], col(C_LOWER), lf[:, 0:T], start=True, stop=False)
                nc.tensor.matmul(bank[:, P:T], col(C_ONES), lf[:, T:SC], start=False, stop=True)\
                    .then_inc(sb_cum, 1)
            if i >= 2:
                h = i - 2
                att, bank = s_att[:, h % 3, :], ps[:, 4 + h % 2, :]
                pe.wait_ge(sb_att, h + 1)
                pe.wait_ge(sb_vs, 4)
                if h >= 2:
                    pe.wait_ge(mix_in_ready, mix_in_before(at) + h - 1)
                v = [s_v[:, t, h * P:(h + 1) * P] for t in range(TT)]
                nc.tensor.matmul(bank[:, 0:T], v[0], att[:, 0:T], start=True, stop=False)
                nc.tensor.matmul(bank[:, P:T], v[1], att[:, T:SC], start=False, stop=True).then_inc(sb_o, 1)
        w_out_pe(pe, at, 4, hT)

    def sb_act(act, at):
        norm_act(act, at)
        for c in range(16):
            act.wait_ge(sb_qk, c + 1)
            nc.scalar.activation(s_qk[:, c, :], ps[:, c % 4, 0:T], ACT.Copy,
                                 scale=float(P) ** -0.5 if c < GH else 1.0).then_inc(sb_qks, 1)
        for i in range(GH + 3):
            if i < GH:
                t = s_t[:, i % 3, :]
                act.wait_ge(sb_z, i + 1)
                if i >= 3:
                    act.wait_ge(sb_lf, i - 2)
                act_steps.done(act, nc.scalar.activation(t, ps[:, i % 2, 0:SC], ACT.Abs))
                act_steps.done(act, nc.scalar.activation(t, t, ACT.Exp, scale=-1.0))
                nc.scalar.activation(t, t, ACT.Ln, bias=1.0).then_inc(sb_t, 1)
            if 1 <= i <= GH:
                h = i - 1
                act.wait_ge(sb_la, h + 1)
                nc.scalar.activation(s_att[:, h % 3, :], s_att[:, h % 3, :], ACT.Exp).then_inc(sb_e, 1)
            if i >= 3:
                h = i - 3
                act.wait_ge(sb_o, h + 1)
                nc.scalar.activation(hT[:, h, :], ps[:, 4 + h % 2, 0:T], ACT.Copy).then_inc(mix_in_ready, 1)

    def sb_dve(dve, at):
        norm_dve(dve, at, gain[:, :, 4 + at["layer"]])
        dve.wait_ge(load_used, at["mixer_load"] + 2)
        for b in range(4):
            nc.vector.tensor_copy(s_v[:, b // 2, (b % 2) * PB:(b % 2 + 1) * PB], ps[:, 4 + b, :])\
                .then_inc(sb_vs, 1)
        mask = col(C_SB, SC)
        for i in range(GH + 2):
            if i < GH:
                z, t = ps[:, i % 2, 0:SC], s_t[:, i % 3, :]
                lf, lb = s_lf[:, i % 3, :], s_lb[:, i % 3, :]
                dve.wait_ge(sb_t, i + 1)
                if i >= 3:
                    dve.wait_ge(sb_cum, i - 2)
                dve_steps.done(dve, nc.vector.scalar_tensor_tensor(out=lf, in0=z, scalar=0.0, in1=t,
                                                                   op0=ALU.max, op1=ALU.add))
                dve_steps.done(dve, nc.vector.scalar_tensor_tensor(out=lf, in0=lf, scalar=-1.0, in1=mask,
                                                                   op0=ALU.mult, op1=ALU.mult))
                nc.vector.scalar_tensor_tensor(out=lb, in0=z, scalar=0.0, in1=t,
                                               op0=ALU.min, op1=ALU.subtract).then_inc(sb_lf, 1)
            if 1 <= i <= GH:
                h = i - 1
                dve.wait_ge(sb_cum, h + 1)
                dve.wait_ge(sb_lf, h + 1)
                if h >= 3:
                    dve.wait_ge(sb_o, h - 2)
                nc.vector.tensor_tensor(s_att[:, h % 3, :], ps[:, 2 + h % 2, 0:SC], s_lb[:, h % 3, :],
                                        ALU.add).then_inc(sb_la, 1)
            if i >= 2:
                h = i - 2
                att = s_att[:, h % 3, :]
                dve.wait_ge(sb_e, h + 1)
                nc.vector.tensor_tensor(att, att, mask, ALU.mult).then_inc(sb_att, 1)
        w_out_wait(dve, at)
        add_to_x(dve, x_sb, 1.0)

    QR, KVR, RD, IDX, IH = 384, 256, 32, 64, 8
    DIN, NOPE, TOPK = QR + KVR + RD + IDX + IH, P - RD, 64
    NEG, TAKEN = -1e30, -3e38
    O_KV, O_R, O_I, O_W = QR, QR + KVR, QR + KVR + RD, QR + KVR + RD + IDX
    car = Carve()
    d_p = car.take(TT, DIN)
    d_k = car.take(TT, P)
    d_cT = car.take(5, T)
    d_kT0 = car.take(T)
    d_q = car.take(TT, D)
    d_qT = car.take(GH, T)
    d_kT = car.take(GH, T)
    d_v = car.take(TT, D)
    d_qi = car.take(TT, IH * IDX)
    d_qiT = car.take(IH, T)
    d_sel = car.take(SC)
    d_score = car.take(SC)
    car = Carve()
    d_s = car.take(3, SC)
    d_pT = car.take(3, SC)
    car = Carve()
    car.take(TT * DIN + TT * P + 6 * T)
    d_relu = car.take(2, 2 * T)
    d_tmp = aT[:, :, :].rearrange("p a b -> p (a b)")
    d_small = sb("d_small", [P, 64])
    d_ss = d_small[:, 0:6]
    d_m8 = d_small[:, 8:16]
    d_w = d_small[:, 16:32]
    d_nm = d_small[:, 32:38]
    d_sum = d_small[:, 40:46]
    d_rec = d_small[:, 48:54]
    d_gk = sb("d_gk", [P, IDX])
    dsa_p = sem("dsa_p")
    dsa_ps = sem("dsa_ps")
    dsa_ss = sem("dsa_ss")
    dsa_rs = sem("dsa_rs")
    dsa_c = sem("dsa_c")
    dsa_cps = sem("dsa_cps")
    dsa_cT = sem("dsa_cT")
    dsa_q = sem("dsa_q")
    dsa_qs = sem("dsa_qs")
    dsa_qa = sem("dsa_qa")
    dsa_kps = sem("dsa_kps")
    dsa_ks = sem("dsa_ks")
    dsa_kr = sem("dsa_kr")
    dsa_v = sem("dsa_v")
    dsa_vs = sem("dsa_vs")
    dsa_qTps = sem("dsa_qTps")
    dsa_qT = sem("dsa_qT")
    dsa_log = sem("dsa_log")
    dsa_relu = sem("dsa_relu")
    dsa_sc = sem("dsa_sc")
    dsa_z = sem("dsa_z")
    dsa_m = sem("dsa_m")
    dsa_e = sem("dsa_e")
    dsa_pr = sem("dsa_pr")
    dsa_pt = sem("dsa_pt")
    dsa_pts = sem("dsa_pts")
    dsa_o = sem("dsa_o")

    def dsa_sp(sp, at):
        j = at["n"]

        def go(g, off, src, sem_by):
            v = src.rearrange("(k p) c -> p k c", p=P)
            n = v.shape[1] * v.shape[2]
            sp.dma_start(slot(g)[:, off:off + n].rearrange("p (k c) -> p k c", k=v.shape[1]), v)\
                .then_inc(load_done[g % RING], sem_by)

        g = at["load"]
        wait_slot_free(sp, g)
        go(g, 0, A["dsa_w_in"][j], 48)
        wait_slot_free(sp, g + 1)
        go(g + 1, 0, A["dsa_w_uq"][j], 32)
        go(g + 1, 3 * D, A["dsa_w_qidx"][j], 16)
        wait_slot_free(sp, g + 2)
        go(g + 2, 0, A["dsa_w_uk"][j], 32)
        go(g + 2, 2 * D, A["dsa_w_uv"][j], 16)
        w_out_sp(sp, at, 3, A["dsa_w_out"][j])

    def dsa_pe(pe, at):
        norm_pe(pe, at)
        pe.wait_ge(hT_ready, 2 * TT * (at["norm"] + 1))
        g = at["load"]
        wait_loaded(pe, g)
        w = slot(g)[:, 0:KD * DIN].rearrange("p (k c) -> p k c", k=KD)
        for t in range(TT):
            for bank, cols in ((2 * t, slice(0, O_KV)), (2 * t + 1, slice(O_KV, DIN))):
                for k in range(KD):
                    ins = nc.tensor.matmul(ps[:, bank, 0:cols.stop - cols.start], hT[:, k, t * P:(t + 1) * P],
                                           w[:, k, cols], start=(k == 0), stop=(k == KD - 1))
            ins.then_inc(dsa_p if t == 0 else load_used, 1)
        pe.wait_ge(dsa_c, 1)
        for n in range(6):
            src = d_p[:, :, n * P:(n + 1) * P] if n < 5 else d_k[:, :, :]
            for t in range(TT):
                ins = nc.tensor.transpose(ps[:, 4 + n // 2, (n % 2) * T + t * P:(n % 2) * T + (t + 1) * P],
                                          src[:, t, :], ident)
        ins.then_inc(dsa_cps, 1)
        pe.wait_ge(dsa_cT, 1)
        wait_loaded(pe, g + 1)
        wq = slot(g + 1)[:, 0:3 * D].rearrange("p (k c) -> p k c", k=3)
        wi = slot(g + 1)[:, 3 * D:3 * D + 3 * PB].rearrange("p (k c) -> p k c", k=3)
        for t in range(TT):
            for bank, src in ((2 * t, wq[:, :, 0:PB]), (2 * t + 1, wq[:, :, PB:D]), (4 + t, wi)):
                for k in range(3):
                    ins = nc.tensor.matmul(ps[:, bank, :], d_cT[:, k, t * P:(t + 1) * P], src[:, k, :],
                                           start=(k == 0), stop=(k == 2))
            ins.then_inc(dsa_q if t == 0 else load_used, 1)
        wait_loaded(pe, g + 2)
        wk = slot(g + 2)[:, 0:2 * GH * NOPE].rearrange("p (k c) -> p k c", k=2)
        wv = slot(g + 2)[:, 2 * D:4 * D].rearrange("p (k c) -> p k c", k=2)
        for n in range(4):
            if n >= 2:
                pe.wait_ge(dsa_ks, n - 1)
            for i in range(2):
                h = 2 * n + i
                for k in range(2):
                    ins = nc.tensor.matmul(ps[0:NOPE, 6 + n % 2, i * T:(i + 1) * T],
                                           wk[:, k, h * NOPE:(h + 1) * NOPE], d_cT[:, 3 + k, :],
                                           start=(k == 0), stop=(k == 1))
            ins.then_inc(dsa_kps, 1)
        for n in range(4):
            pe.wait_ge(dsa_ks, 3 + n % 2)
            if n >= 2:
                pe.wait_ge(dsa_vs, n - 1)
            for k in range(2):
                ins = nc.tensor.matmul(ps[:, 6 + n % 2, :], d_cT[:, 3 + k, (n // 2) * P:(n // 2 + 1) * P],
                                       wv[:, k, (n % 2) * PB:(n % 2 + 1) * PB], start=(k == 0), stop=(k == 1))
            ins.then_inc(dsa_v if n < 3 else load_used, 1)
        for t in range(TT):
            pe.wait_ge(dsa_qs, t + 1)
            pe.wait_ge(dsa_qa, t + 1)
        for n in range(8):
            t, half = n // 2 % 2, n % 2
            if n >= 4:
                pe.wait_ge(dsa_qT, n - 3)
            for c in range(4):
                h = 4 * half + c
                if n < 4:
                    ins = nc.tensor.transpose(ps[0:IDX, n % 4, c * P:(c + 1) * P],
                                              d_qi[:, t, h * IDX:(h + 1) * IDX], ident)
                else:
                    ins = nc.tensor.transpose(ps[:, n % 4, c * P:(c + 1) * P], d_q[:, t, h * P:(h + 1) * P], ident)
            ins.then_inc(dsa_qTps, 1)
        pe.wait_ge(dsa_qT, 4)
        for n in range(8):
            t = n // 4
            if n >= 2:
                pe.wait_ge(dsa_relu, n - 1)
            for i in range(2):
                h = 2 * (n % 4) + i
                ins = nc.tensor.matmul(ps[:, 4 + n % 2, i * T:i * T + (t + 1) * P],
                                       d_qiT[0:IDX, h, t * P:(t + 1) * P], d_kT0[0:IDX, 0:(t + 1) * P],
                                       start=True, stop=True)
            ins.then_inc(dsa_log, 1)
        pe.wait_ge(dsa_qT, 8)
        pe.wait_ge(dsa_relu, 8)
        pe.wait_ge(dsa_kr, 1)
        pe.wait_ge(dsa_vs, 4)
        for i in range(GH + 2):
            if i < GH:
                if i >= 2:
                    pe.wait_ge(dsa_m, i - 1)
                nc.tensor.matmul(ps[:, i % 2, 0:P], d_qT[:, i, 0:P], d_kT[:, i, 0:P], start=True, stop=True)
                nc.tensor.matmul(ps[:, i % 2, P:SC], d_qT[:, i, P:T], d_kT[:, i, :], start=True, stop=True)\
                    .then_inc(dsa_z, 1)
            if 1 <= i <= GH:
                h = i - 1
                pe.wait_ge(dsa_pr, h + 1)
                if h >= 2:
                    pe.wait_ge(dsa_pts, h - 1)
                for c in range(3):
                    ins = nc.tensor.transpose(ps[:, 2 + h % 2, c * P:(c + 1) * P],
                                              d_s[:, h % 3, c * P:(c + 1) * P], ident)
                ins.then_inc(dsa_pt, 1)
            if i >= 2:
                h = i - 2
                bank, pT = ps[:, 4 + h % 2, :], d_pT[:, h % 3, :]
                pe.wait_ge(dsa_pts, h + 1)
                if h >= 2:
                    pe.wait_ge(mix_in_ready, mix_in_before(at) + h - 1)
                v = [d_v[:, t, h * P:(h + 1) * P] for t in range(TT)]
                nc.tensor.matmul(bank[:, 0:T], v[0], pT[:, 0:T], start=True, stop=False)
                nc.tensor.matmul(bank[:, P:T], v[1], pT[:, T:SC], start=False, stop=True).then_inc(dsa_o, 1)
        w_out_pe(pe, at, 3, hT)

    def dsa_act(act, at):
        norm_act(act, at)
        for t in range(TT):
            if t == 0:
                act.wait_ge(dsa_p, 1)
            else:
                act.wait_ge(load_used, at["mixer_load"] + 1)
            nc.scalar.activation(d_p[:, t, 0:O_KV], ps[:, 2 * t, 0:O_KV], ACT.Copy)
            nc.scalar.activation(d_p[:, t, O_KV:DIN], ps[:, 2 * t + 1, 0:DIN - O_KV], ACT.Copy).then_inc(dsa_ps, 1)
            for s, (bank, cols) in enumerate(((2 * t, slice(0, QR)), (2 * t + 1, slice(0, KVR)),
                                              (2 * t + 1, slice(KVR + RD, KVR + RD + IDX)))):
                ins = nc.scalar.activation(silu[:, 0:2, :].rearrange("p a b -> p (a b)")[:, 0:cols.stop - cols.start],
                                           ps[:, bank, cols], ACT.Square,
                                           accum_out=d_ss[:, 2 * s + t:2 * s + t + 1])
                if s < 2:
                    act_steps.done(act, ins)
            ins.then_inc(dsa_ss, 1)
            act.wait_ge(dsa_ss, t + 1)
        for t in range(TT):
            act.wait_ge(dsa_qs, t + 1)
            for half in range(2):
                nc.scalar.activation(
                    d_q[:, t, half * PB:(half + 1) * PB].rearrange("p (h c) -> p h c", c=P)[:, :, 0:NOPE],
                    ps[:, 2 * t + half, :].rearrange("p (h c) -> p h c", c=P)[:, :, RD:P], ACT.Copy)
            nc.scalar.activation(d_qi[:, t, :].rearrange("p (h c) -> p h c", c=IDX)[:, :, 16:IDX],
                                 ps[:, 4 + t, :].rearrange("p (h c) -> p h c", c=IDX)[:, :, 16:IDX], ACT.Copy)\
                .then_inc(dsa_qa, 1)
        for n in range(4):
            act.wait_ge(dsa_kps, n + 1)
            nc.scalar.activation(d_kT[0:NOPE, 2 * n:2 * n + 2, :],
                                 ps[0:NOPE, 6 + n % 2, :].rearrange("p (h c) -> p h c", c=T), ACT.Copy)\
                .then_inc(dsa_ks, 1)
        for n in range(4):
            if n < 3:
                act.wait_ge(dsa_v, n + 1)
            else:
                act.wait_ge(load_used, at["mixer_load"] + 3)
            nc.scalar.activation(d_v[:, n // 2, (n % 2) * PB:(n % 2 + 1) * PB], ps[:, 6 + n % 2, :], ACT.Copy)\
                .then_inc(dsa_vs, 1)
        for n in range(8):
            t, half = n // 2 % 2, n % 2
            act.wait_ge(dsa_qTps, n + 1)
            rows, dst = (IDX, d_qiT) if n < 4 else (P, d_qT)
            nc.scalar.activation(dst[0:rows, 4 * half:4 * half + 4, t * P:(t + 1) * P],
                                 ps[0:rows, n % 4, :].rearrange("p (h c) -> p h c", c=P), ACT.Copy,
                                 scale=1.0 if n < 4 else float(P) ** -0.5).then_inc(dsa_qT, 1)
        for n in range(8):
            t = n // 4
            act.wait_ge(dsa_log, n + 1)
            if n >= 2:
                act.wait_ge(dsa_sc, n - 1)
            elif n == 0:
                act.wait_ge(dsa_qTps, 8)
            nc.scalar.activation(d_relu[:, n % 2, :].rearrange("p (i c) -> p i c", i=2)[:, :, 0:(t + 1) * P],
                                 ps[:, 4 + n % 2, :].rearrange("p (i c) -> p i c", i=2)[:, :, 0:(t + 1) * P],
                                 ACT.Relu).then_inc(dsa_relu, 1)
        for i in range(GH + 2):
            if i < GH:
                act.wait_ge(dsa_m, i + 1)
                for t, cols in ((0, slice(0, P)), (1, slice(P, SC))):
                    n = 2 * (i % 3) + t
                    s = d_s[:, i % 3, cols]
                    ins = nc.scalar.activation(s, s, ACT.Exp, bias=d_nm[:, n:n + 1], accum_out=d_sum[:, n:n + 1])
                ins.then_inc(dsa_e, 1)
            if i >= 2:
                h = i - 2
                act.wait_ge(dsa_o, h + 1)
                nc.scalar.activation(hT[:, h, :], ps[:, 4 + h % 2, 0:T], ACT.Copy).then_inc(mix_in_ready, 1)

    def rotate(dve, step, dst1, dst2, src1, src2, cos, sin, tmp, last):
        n, half = src1.shape[1], src1.shape[2]
        t = [tmp[:, i * n * half:(i + 1) * n * half].rearrange("p (n c) -> p n c", n=n) for i in range(4)]
        c, s = bc_mid(cos, n), bc_mid(sin, n)
        nc.vector.tensor_tensor(t[0], src1, c, ALU.mult)
        nc.vector.tensor_tensor(t[1], src2, s, ALU.mult)
        nc.vector.tensor_tensor(t[2], src2, c, ALU.mult)
        step(dve, nc.vector.tensor_tensor(t[3], src1, s, ALU.mult))
        step(dve, nc.vector.tensor_tensor(dst1, t[0], t[1], ALU.subtract))
        last(nc.vector.tensor_tensor(dst2, t[2], t[3], ALU.add))

    def dsa_dve(dve, at):
        norm_dve(dve, at, gain[:, :, 4 + at["layer"]])
        step = dve_steps.done

        def fin(ins):
            step(dve, ins)

        step(dve, nc.vector.memset(d_k, 0.0))
        dve.wait_ge(rows_loaded, ROWS_DMAS)
        dve.wait_ge(dsa_rs, 1)
        for t in range(TT):
            for s, (a, b) in enumerate(((0, QR), (O_KV, O_KV + KVR), (O_I, O_I + IDX))):
                v = d_p[:, t, a:b]
                step(dve, nc.vector.tensor_scalar(v, v, d_ss[:, 2 * s + t:2 * s + t + 1], None, ALU.mult))
            step(dve, nc.vector.tensor_tensor(d_k[:, t, 0:IDX], d_p[:, t, O_I:O_I + IDX], d_gk[:, :], ALU.mult))
            k = d_k[:, t, :][:, None, :]
            rotate(dve, step, k[:, :, 0:8], k[:, :, 8:16], k[:, :, 0:8], k[:, :, 8:16],
                   col(C_ROPE8 + 16 * t, 8), col(C_ROPE8 + 16 * t + 8, 8), d_tmp, fin)
            r = d_p[:, t, O_R:O_R + RD][:, None, :]
            rotate(dve, step, k[:, :, NOPE:NOPE + 16], k[:, :, NOPE + 16:P], r[:, :, 0:16], r[:, :, 16:32],
                   col(C_ROPE16 + 32 * t, 16), col(C_ROPE16 + 32 * t + 16, 16), d_tmp, fin)
            step(dve, nc.vector.tensor_scalar(d_w[:, 8 * t:8 * t + 8], d_p[:, t, O_W:O_W + IH],
                                              float(IH * IDX) ** -0.5, None, ALU.mult))
        nc.vector.tensor_scalar(d_w, d_w, 1.0, None, ALU.mult).then_inc(dsa_c, 1)
        dve.wait_ge(dsa_cps, 1)
        for n in range(5):
            g_col = 102 + n
            nc.vector.tensor_scalar(d_cT[:, n, :], ps[:, 4 + n // 2, (n % 2) * T:(n % 2 + 1) * T],
                                    cols_T[:, 0, g_col:g_col + 1], None, ALU.mult)
        nc.vector.tensor_copy(d_kT0, ps[:, 6, T:2 * T]).then_inc(dsa_cT, 1)
        for t in range(TT):
            if t == 0:
                dve.wait_ge(dsa_q, 1)
            else:
                dve.wait_ge(load_used, at["mixer_load"] + 2)
            for half in range(2):
                q = ps[:, 2 * t + half, :].rearrange("p (h c) -> p h c", c=P)
                dst = d_q[:, t, half * PB:(half + 1) * PB].rearrange("p (h c) -> p h c", c=P)
                rotate(dve, step, dst[:, :, NOPE:NOPE + 16], dst[:, :, NOPE + 16:P], q[:, :, 0:16], q[:, :, 16:32],
                       col(C_ROPE16 + 32 * t, 16), col(C_ROPE16 + 32 * t + 16, 16), d_tmp, fin)
            qi = ps[:, 4 + t, :].rearrange("p (h c) -> p h c", c=IDX)
            dst = d_qi[:, t, :].rearrange("p (h c) -> p h c", c=IDX)
            rotate(dve, step, dst[:, :, 0:8], dst[:, :, 8:16], qi[:, :, 0:8], qi[:, :, 8:16],
                   col(C_ROPE8 + 16 * t, 8), col(C_ROPE8 + 16 * t + 8, 8), d_tmp,
                   lambda ins: ins.then_inc(dsa_qs, 1))
            dve.wait_ge(dsa_qs, t + 1)
        for n in range(8):
            t = n // 4
            acc = d_score[:, 0:P] if t == 0 else d_score[:, P:SC]
            dve.wait_ge(dsa_relu, n + 1)
            for i in range(2):
                h = 2 * (n % 4) + i
                w = d_w[:, 8 * t + h:8 * t + h + 1]
                r = d_relu[:, n % 2, i * T:i * T + (t + 1) * P]
                if h == 0:
                    step(dve, nc.vector.tensor_scalar(acc, r, w, None, ALU.mult))
                else:
                    ins = nc.vector.scalar_tensor_tensor(out=acc, in0=r, scalar=w, in1=acc,
                                                         op0=ALU.mult, op1=ALU.add)
                    if i == 0:
                        step(dve, ins)
            ins.then_inc(dsa_sc, 1)
            dve.wait_ge(dsa_sc, n + 1)
        step(dve, nc.vector.tensor_tensor(d_score, d_score, col(C_CNEG, SC), ALU.add))
        for cols in (slice(0, P), slice(P, SC)):
            s = d_score[:, cols]
            for _ in range(TOPK // 8):
                step(dve, nc.vector.max(d_m8, s))
                step(dve, nc.vector.match_replace(out=s, in_to_replace=d_m8, in_values=s, imm_value=TAKEN))
        step(dve, nc.vector.tensor_scalar(d_sel, d_score, 0.5 * TAKEN, NEG, ALU.is_gt, ALU.mult))
        step(dve, nc.vector.tensor_tensor(d_sel, d_sel, col(C_CNEG, SC), ALU.add))
        for i in range(GH + 2):
            if i < GH:
                s = d_s[:, i % 3, :]
                dve.wait_ge(dsa_z, i + 1)
                if i >= 3:
                    dve.wait_ge(dsa_pt, i - 2)
                step(dve, nc.vector.tensor_tensor(s, ps[:, i % 2, 0:SC], d_sel, ALU.add))
                n = 2 * (i % 3)
                nc.vector.tensor_reduce(d_nm[:, n:n + 1], s[:, 0:P], AX.X, ALU.max, negate=True)
                nc.vector.tensor_reduce(d_nm[:, n + 1:n + 2], s[:, P:SC], AX.X, ALU.max, negate=True)\
                    .then_inc(dsa_m, 1)
            if 1 <= i <= GH:
                h = i - 1
                n = 2 * (h % 3)
                dve.wait_ge(dsa_e, h + 1)
                step(dve, nc.vector.reciprocal(d_rec[:, n:n + 2], d_sum[:, n:n + 2]))
                for t, cols in ((0, slice(0, P)), (1, slice(P, SC))):
                    s = d_s[:, h % 3, cols]
                    ins = nc.vector.tensor_scalar(s, s, d_rec[:, n + t:n + t + 1], None, ALU.mult)
                ins.then_inc(dsa_pr, 1)
            if i >= 1 and i - 1 < GH:
                h = i - 1
                dve.wait_ge(dsa_pt, h + 1)
                if h >= 3:
                    dve.wait_ge(dsa_o, h - 2)
                nc.vector.tensor_copy(d_pT[:, h % 3, :], ps[:, 2 + h % 2, 0:SC]).then_inc(dsa_pts, 1)
        w_out_wait(dve, at)
        add_to_x(dve, x_sb, 1.0)

    def dsa_pool(pool, at):
        norm_pool(pool, at)
        pool.wait_ge(dsa_ss, TT)
        for s, n in enumerate((QR, KVR, IDX)):
            v = d_ss[:, 2 * s:2 * s + 2]
            pool_steps.done(pool, nc.gpsimd.tensor_scalar(v, v, 1.0 / n, EPS, ALU.mult, ALU.add))
        nc.gpsimd.tensor_tensor(d_ss, d_ss, consts[:, C_NHALF:C_NHALF + 6], ALU.pow).then_inc(dsa_rs, 1)
        pool.wait_ge(dsa_cT, 1)
        nc.gpsimd.tensor_copy(d_kT[NOPE:P, :, :], d_kT0[NOPE:P, None, :].to_broadcast([RD, GH, T]))\
            .then_inc(dsa_kr, 1)

    NMOD = 9 * KD
    car = Carve()
    x_ctx = car.take(TT, D)
    m_rows = car.take(2, P)
    m_b = car.take(2, NMOD)
    m_s = car.take(KD, 2)
    f_row = car.take(D)
    mod = sb("mod", [P, 2, NMOD, 2])
    amp = sb("amp", [P, 8, KD])
    gate_row = sb("gate_row", [P, D])
    ctx_loaded = sem("ctx_loaded")
    mod_s = sem("mod_s")
    mod_bps = sem("mod_bps")
    mod_ready = sem("mod_ready")
    ctx_ready = sem("ctx_ready")
    gate_ps = sem("gate_ps")
    gate_ready = sem("gate_ready")
    fin_loaded = sem("fin_loaded")
    fin_ss = sem("fin_ss")
    fin_rs = sem("fin_rs")

    GATES = {("ffn", 8): (0, 0, 1, 0.5), ("ffn", 9): (0, 0, 0, 0.5), ("even", 0): (0, 1, 0, 1.0),
             ("ffn", 10): (0, 2, 0, 0.5), ("ffn", 11): (1, 0, 0, 0.5), ("sgu", 0): (1, 1, 0, 1.0),
             ("ffn", 12): (1, 2, 0, 0.5)}

    def gate_use(at):
        return list(GATES).index((at["kind"], at["n"]))

    def mod_cols(layer, vector, cond):
        return mod[:, layer, vector * KD:(vector + 1) * KD, cond]

    def gate_pe(pe, at):
        layer, j, cond, _ = GATES[at["kind"], at["n"]]
        for k in range(KD):
            c = mod_cols(layer, 3 * j + 2, cond)[:, k:k + 1]
            ins = nc.tensor.matmul(ps[:, k // 4, (k % 4) * P:(k % 4 + 1) * P], c.to_broadcast([P, P]), ident,
                                   start=True, stop=True)
        ins.then_inc(gate_ps, 1)
        pe.wait_ge(gate_ready, gate_use(at) + 1)

    def gate_act(act, at):
        n = gate_use(at)
        act.wait_ge(gate_ps, n + 1)
        nc.scalar.activation(gate_row[:, :], ps[:, 0:2, :].rearrange("p a b -> p (a b)"), ACT.Copy,
                             scale=GATES[at["kind"], at["n"]][3]).then_inc(gate_ready, 1)

    def mod_sp(sp, at):
        if at["update"]:
            sp.wait_ge(x_ready, TT * at["update"])
        sp.dma_start(x_ctx, A["ctx_2"][0].rearrange("(t p) d -> p t d", p=P)).then_inc(ctx_loaded, 16)
        for l in range(2):
            sp.dma_start(m_rows[0:NMOD, l, :], A["b_mod_2"][l].rearrange("(n p) -> n p", p=P)).then_inc(ctx_loaded, 16)
        for l in range(2):
            w = A["w_mod_2"][l].rearrange("(k p) (q c) -> q p k c", p=P, c=CH)

            def load(n, it=None):
                g = at["load"] + 12 * l + n
                if it is None:
                    wait_slot_free(sp, g)
                else:
                    sp.wait_ge(load_used, at["mixer_load"] + 12 * l + n - RING + 1 + it * RING)
                for m in range(3):
                    q = 3 * n + m if it is None else it * (3 * RING) + (3 * n + m)
                    sp.dma_start(part(g, m).rearrange("p (k c) -> p k c", k=KD),
                                 w[bass.ds(q, 1)].rearrange("a p k c -> p (a k) c")).then_inc(load_done[g % RING], 16)

            for n in range(RING):
                load(n)
            with sp.Fori(0, 12 // RING - 1) as it:
                for n in range(RING):
                    load(RING + n, it)

    def mod_pe(pe, at):
        pe.wait_ge(ctx_loaded, 48)
        if at["update"]:
            pe.wait_ge(x_ready, TT * at["update"])
        for l in range(2):
            ins = nc.tensor.transpose(ps[:, 4, l * P:l * P + NMOD], m_rows[0:NMOD, l, :],
                                      consts[0:NMOD, C_IDENT:C_IDENT + NMOD])
        ins.then_inc(mod_bps, 1)
        pe.wait_ge(mod_s, 1)
        for l in range(2):
            with pe.Fori(0, 12 // RING) as it:
                for n in range(RING):
                    g = at["load"] + 12 * l + n
                    pe.wait_ge(load_done[g % RING], 48 * (g // RING + 1) + it * 48)
                    for m in range(3):
                        w = part(g, m).rearrange("p (k c) -> p k c", k=KD)
                        for i in range(2):
                            column = (6 * n + 2 * m + i) * 2 + it * (12 * RING)
                            for k in range(KD):
                                ins = nc.tensor.matmul(ps[:, l, bass.ds(column, 2)], w[:, k, i * P:(i + 1) * P],
                                                       m_s[:, k, :], start=(k == 0), stop=(k == KD - 1))
                    ins.then_inc(load_used, 1)
        pe.wait_ge(mod_ready, 1)

    def mod_act(act, at):
        if at["update"]:
            act.wait_ge(x_ready, TT * at["update"])
        act.wait_ge(gains_ready, 3)
        nc.scalar.activation(m_s, gain[:, :, 18:20], ACT.Silu).then_inc(mod_s, 1)

    def mod_dve(dve, at):
        step = dve_steps.done
        dve.wait_ge(mod_bps, 1)
        step(dve, nc.vector.tensor_copy(m_b, ps[:, 4, 0:2 * P].rearrange("p (l n) -> p l n", n=P)[:, :, 0:NMOD]))
        dve.wait_ge(load_used, at["mixer_load"] + 24)
        for l in range(2):
            step(dve, nc.vector.tensor_tensor(
                mod[:, l, :, :], ps[:, l, 0:2 * NMOD].rearrange("p (n c) -> p n c", c=2), bc_last(m_b[:, l, :], 2),
                ALU.add))
        for n in range(8):
            l, j, cond = (n // 3, n % 3, 0) if n < 6 else (0, n - 6, 1)
            ins = nc.vector.scalar_tensor_tensor(out=amp[:, n, :], in0=mod_cols(l, 3 * j + 1, cond), scalar=1.0,
                                                 in1=gain[:, :, 12 + 3 * l + j], op0=ALU.add, op1=ALU.mult)
        ins.then_inc(mod_ready, 1)
        dve.wait_ge(mod_ready, 1)

    def final_sp(sp, at):
        n = at["n"]
        sp.wait_ge(x_ready, TT * at["update"])
        sp.dma_start(f_row, (A["final_g_2"] if n else A["final_norm"]).partition_broadcast(P)).then_inc(fin_loaded, 16)
        if n:
            for t in range(TT):
                sp.wait_ge(x_ready, TT * at["update"] + t + 1)
                sp.dma_start(out[0, t * P:(t + 1) * P, :], x_sb[:, t, :]).then_inc(out_done, 16)

    def final_act(act, at):
        for t in range(TT):
            act.wait_ge(x_ready, TT * (at["update"] - 1) + t + 1)
            nc.scalar.activation(xn[:, t, :], x_sb[:, t, :], ACT.Square, accum_out=sumsq[:, t:t + 1])\
                .then_inc(fin_ss, 1)

    def final_pool(pool, at):
        for t in range(TT):
            pool.wait_ge(fin_ss, TT * at["n"] + t + 1)
            inv_sqrt(pool, rstd[:, t:t + 1], sumsq[:, t:t + 1], 1.0 / D, EPS).then_inc(fin_rs, 1)

    def final_dve(dve, at):
        dve.wait_ge(fin_loaded, 16 * (at["n"] + 1))
        for t in range(TT):
            dve.wait_ge(fin_rs, TT * at["n"] + t + 1)
            nc.vector.scalar_tensor_tensor(out=x_sb[:, t, :], in0=x_sb[:, t, :], scalar=rstd[:, t:t + 1], in1=f_row,
                                           op0=ALU.mult, op1=ALU.mult).then_inc(x_ready, 1)

    def nothing(eng, at):
        pass

    SGW, SGT, SGG = 2048, 16, 8
    car = Carve()
    sg_v = car.take(TT, SGW)
    sg_u = car.take(SGT, T)
    sg_lng = car.take(SGW)
    sg_lnb = car.take(SGW)
    sg_ws = car.take(SGG, P)
    sg_wsT = car.take(SGG, P)
    sg_bs = car.take(SGG, P)
    sg_mean = sb("sg_mean", [P, 6])
    sgu_loaded = sem("sgu_loaded")
    sgu_ps = sem("sgu_ps")
    sgu_s = sem("sgu_s")
    sgu_wps = sem("sgu_wps")
    sgu_w = sem("sgu_w")
    sgu_cen = sem("sgu_cen")
    sgu_ss = sem("sgu_ss")
    sgu_rs = sem("sgu_rs")
    sgu_v = sem("sgu_v")
    sgu_mix = sem("sgu_mix")
    sgu_y = sem("sgu_y")

    SGU = [("v", 8 + q, t) for q in range(8) for t in range(TT)] + [("u", q, i) for q in range(8) for i in range(2)]

    def sgu_sp(sp, at):
        sp.wait_ge(x_ready, TT * at["update"])
        sp.dma_start(sg_lng, A["sg_ln_g_2"][0].partition_broadcast(P)).then_inc(sgu_loaded, 16)
        sp.dma_start(sg_lnb, A["sg_ln_b_2"][0].partition_broadcast(P)).then_inc(sgu_loaded, 16)
        sp.dma_start(sg_ws, A["sg_w_s_2"][0].rearrange("g t s -> t g s")).then_inc(sgu_loaded, 16)
        sp.dma_start(sg_bs[0:1, :, :], A["sg_b_s_2"]).then_inc(sgu_loaded, 16)

    def sgu_weights_sp(sp, at):
        w = A["sg_w_in_2"][0].rearrange("(k p) c -> p k c", p=P)
        chunks = [8 + q for q in range(8)] + list(range(8))
        for n in range(6):
            g = at["load"] + n
            wait_slot_free(sp, g)
            here = chunks[3 * n:3 * n + 3]
            for m, q in enumerate(here):
                sp.dma_start(part(g, m).rearrange("p (k c) -> p k c", k=KD), w[:, :, q * CH:(q + 1) * CH])\
                    .then_inc(load_done[g % RING], 48 // len(here))
        w_out_sp(sp, at, 6, A["sg_w_out_2"][0], tiles=SGT)

    def sgu_pe(pe, at):
        pe.wait_ge(sgu_loaded, 64)
        norm_pe(pe, at)
        gate_pe(pe, at)
        pe.wait_ge(hT_ready, 2 * TT * (at["norm"] + 1))
        for h in range(2):
            for c in range(4):
                ins = nc.tensor.transpose(ps[:, 4 + h, c * P:(c + 1) * P], sg_ws[:, 4 * h + c, :], ident)
            ins.then_inc(sgu_wps, 1)
        for n, (side, q, i) in enumerate(SGU):
            g = at["load"] + n // 6
            if n % 6 == 0:
                wait_loaded(pe, g)
            if n >= 4:
                pe.wait_ge(sgu_s, n - 3)
            w = part(g, n // 2 % 3).rearrange("p (k c) -> p k c", k=KD)
            for k in range(KD):
                if side == "v":
                    ins = nc.tensor.matmul(ps[:, n % 4, 0:CH], hT[:, k, i * P:(i + 1) * P], w[:, k, :],
                                           start=(k == 0), stop=(k == KD - 1))
                else:
                    ins = nc.tensor.matmul(ps[:, n % 4, 0:T], w[:, k, i * P:(i + 1) * P], hT[:, k, :],
                                           start=(k == 0), stop=(k == KD - 1))
            ins.then_inc(sgu_ps, 1)
        pe.wait_ge(sgu_v, TT)
        pe.wait_ge(sgu_w, 2)
        for n in range(SGG):
            bank = ps[:, 4 + n % 4, :]
            if n >= 4:
                pe.wait_ge(sgu_y, n - 3)
            for i in range(2):
                for t in range(TT):
                    o = bank[:, (2 * i + t) * P:(2 * i + t + 1) * P]
                    nc.tensor.matmul(o, sg_v[:, t, (2 * n + i) * P:(2 * n + i + 1) * P], sg_wsT[:, n, :],
                                     start=True, stop=False)
                    ins = nc.tensor.matmul(o, consts[0:1, C_ONES:C_ONES + P], sg_bs[0:1, n, :],
                                           start=False, stop=True)
            ins.then_inc(sgu_mix, 1)
        pe.wait_ge(sgu_s, len(SGU))
        pe.wait_ge(sgu_y, SGG)
        w_out_pe(pe, at, 6, sg_u, tiles=SGT)

    def sgu_act(act, at):
        norm_act(act, at)
        gate_act(act, at)

        def square(t):
            act.wait_ge(sgu_cen, t + 1)
            if t:
                act.wait_ge(sgu_ss, t)
            nc.scalar.activation(squares(t), sg_v[:, t, :], ACT.Square, accum_out=sg_mean[:, 4 + t:5 + t])\
                .then_inc(sgu_ss, 1)

        for n, (side, q, i) in enumerate(SGU):
            act.wait_ge(sgu_ps, n + 1)
            dst = sg_v[:, i, (q - 8) * CH:(q - 7) * CH] if side == "v" else sg_u[:, 2 * q + i, :]
            nc.scalar.activation(dst, ps[:, n % 4, 0:CH], ACT.Gelu_apprx_tanh).then_inc(sgu_s, 1)
            if n in (20, 24):
                square((n - 20) // 4)

    def squares(t):
        return xn[:, :, :].rearrange("p t d -> p (t d)")

    def sgu_dve(dve, at):
        step = dve_steps.done
        norm_dve(dve, at, amp[:, 4, :], mod_cols(1, 3, 0))
        for h in range(2):
            dve.wait_ge(sgu_wps, h + 1)
            nc.vector.tensor_copy(sg_wsT[:, 4 * h:4 * h + 4, :], ps[:, 4 + h, :].rearrange("p (g c) -> p g c", c=P))\
                .then_inc(sgu_w, 1)
        dve.wait_ge(sgu_s, 16)
        for t in range(TT):
            step(dve, nc.vector.tensor_reduce(sg_mean[:, t:t + 1], sg_v[:, t, :], AX.X, ALU.add))
            step(dve, nc.vector.tensor_scalar(sg_mean[:, 2 + t:3 + t], sg_mean[:, t:t + 1], 1.0 / SGW, None, ALU.mult))
            nc.vector.tensor_scalar(sg_v[:, t, :], sg_v[:, t, :], sg_mean[:, 2 + t:3 + t], None,
                                    ALU.subtract).then_inc(sgu_cen, 1)
        dve.wait_ge(sgu_loaded, 64)
        for t in range(TT):
            v = sg_v[:, t, :]
            dve.wait_ge(sgu_rs, t + 1)
            step(dve, nc.vector.scalar_tensor_tensor(out=v, in0=v, scalar=sg_mean[:, 4 + t:5 + t], in1=sg_lng,
                                                     op0=ALU.mult, op1=ALU.mult))
            nc.vector.tensor_tensor(v, v, sg_lnb, ALU.add).then_inc(sgu_v, 1)
        for n in range(SGG):
            dve.wait_ge(sgu_mix, n + 1)
            dve.wait_ge(sgu_s, 16 + 2 * n + 2)
            u = sg_u[:, 2 * n:2 * n + 2, :]
            nc.vector.tensor_tensor(u, u, ps[:, 4 + n % 4, :].rearrange("p (c i) -> p c i", c=2), ALU.mult)\
                .then_inc(sgu_y, 1)
        w_out_wait(dve, at)
        add_to_x(dve, x_sb, 1.0, gate_row)

    def sgu_pool(pool, at):
        norm_pool(pool, at)
        for t in range(TT):
            pool.wait_ge(sgu_ss, t + 1)
            v = sg_mean[:, 4 + t:5 + t]
            inv_sqrt(pool, v, v, 1.0 / SGW, EPS).then_inc(sgu_rs, 1)

    NH, NDH, GRID = 8, 64, 64
    MH, MW = 4, P
    MX = MW + 1
    car = Carve()
    car.take(TT, D)
    e_hx = car.take(KD, T)
    e_qaT = car.take(4, T)
    e_kaT = car.take(4, 2 * T)
    e_va = car.take(4, NH * NDH)
    e_qb = car.take(TT, MH * MW)
    e_kb = car.take(4, MH * MW)
    e_vb = car.take(4, MH, MX + 3)
    e_ob = car.take(TT, MH * MW)
    e_g = car.take(4, 16)
    after = car.at
    car = Carve()
    e_p = car.take(2, 2 * T)
    e_pT = car.take(2, 4 * P)
    e_bias = car.take(2, TT, T)
    car = Carve()
    e_rm = car.take(2, MH * P)
    e_sT = car.take(2, MH * P)
    e_ka = car.take(MH * P)
    e_o = car.take(MH, MX + 3)
    car.at = max(car.at, 0)
    assert car.at <= 4096
    car.at = after
    e_qT = car.take(MH, T)
    e_kT = car.take(MH, T)
    e_C = car.take(2 * MH, MX + 3)
    e_rot = aT[:, :, :].rearrange("p a b -> p (a b)")
    e_s = sb("e_s", [P, 576])
    e_gl = e_s[:, 0:64]
    e_ga = e_s[:, 64:128]
    e_li, e_lf, e_b, e_r, e_we, e_be, e_mb, e_t, e_ap, e_at = (
        e_s[:, 128 + 32 * i:160 + 32 * i] for i in range(10))
    e_mx = e_s[:, 448:456]
    e_wi = e_s[:, 456:464]
    e_em = e_s[:, 464:472]
    e_den = e_s[:, 472:480]
    e_nm = e_s[:, 480:482]
    e_sum = e_s[:, 482:484]
    e_rec = e_s[:, 484:486]
    e_hss = e_s[:, 488:496]
    e_rows = sb("e_rows", [8, 64])
    e_wmax, e_ber, e_m = e_rows[:, 0:4], e_rows[:, 4:8], e_rows[:, 8:12]
    e_md = e_rows[:, 16:48]
    e_gb = sb("e_gb", [P, 16])
    rpb_copies = nc.dram_tensor("rpb_copies", (GRID, math.prod(A["na_rpb_2"].shape)), FP32, kind="Internal").ap()
    TILE = [[2, 3, 0, 1], [3, 2, 1, 0]]

    even_ps = sem("even_ps")
    even_s = sem("even_s")
    even_copies = sem("even_copies")
    even_bias = [sem(f"even_bias_{i}") for i in range(2)]
    even_msk = sem("even_msk")
    even_z = sem("even_z")
    even_m = sem("even_m")
    even_e = sem("even_e")
    even_p = sem("even_p")
    even_pt = sem("even_pt")
    even_pts = sem("even_pts")
    even_o = sem("even_o")
    ml_gates = sem("ml_gates")
    ml_exps = sem("ml_exps")
    ml_sums = sem("ml_sums")
    ml_rot = sem("ml_rot")
    ml_T = sem("ml_T")
    ml_Ts = sem("ml_Ts")
    ml_ka = sem("ml_ka")
    ml_U = sem("ml_U")
    ml_C = sem("ml_C")
    ml_R = sem("ml_R")
    ml_w = sem("ml_w")
    ml_we2 = sem("ml_we2")
    ml_s = sem("ml_s")
    ml_sT = sem("ml_sT")
    ml_sTs = sem("ml_sTs")
    ml_o = sem("ml_o")
    ml_on = sem("ml_on")
    ml_ss = sem("ml_ss")
    ml_rs = sem("ml_rs")

    def even_products():
        made = []
        for q in range(14):
            name, c = ("qa", "ka", "va", "qb", "kb", "vb", "ob")[q // 2], q % 2
            for side in ((0, 1) if name in ("ka", "va", "kb", "vb") else (0,)):
                for i in range(2):
                    cols = slice(c * CH, (c + 1) * CH)
                    tile = 2 * side + i
                    if name == "qa":
                        to = (e_qaT[:, 2 * c + i, :], ACT.Copy, float(NDH) ** -0.5)
                    elif name == "ka":
                        to = (e_kaT[:, 2 * c + i, side * T:(side + 1) * T], ACT.Copy, 1.0)
                    elif name == "va":
                        to = (e_va[:, tile, cols], ACT.Copy, 1.0)
                    elif name == "qb":
                        to = (e_qb[:, i, cols], ACT.Copy, 1.0)
                    elif name == "kb":
                        to = (e_kb[:, tile, cols], ACT.Copy, float(MW) ** -0.5)
                    elif name == "vb":
                        to = (e_vb[:, tile, 2 * c:2 * c + 2, 0:MW], ACT.Copy, 1.0)
                    else:
                        to = (e_ob[:, i, cols], ACT.Sigmoid, 1.0)
                    made.append((q, name in ("qa", "ka"), side, i, *to))
        for side in range(2):
            for i in range(2):
                made.append((14, False, side, i, e_g[:, 2 * side + i, :], ACT.Copy, 1.0))
        return made

    EVEN = even_products()
    EVEN_ENDS = [sum(p[0] < 3 * (n + 1) for p in EVEN) for n in range(5)]

    def even_sp(sp, at):
        w = A["mix_w_in_2"][0].rearrange("(k p) c -> p k c", p=P)
        for n in range(5):
            g = at["load"] + n
            wait_slot_free(sp, g)
            for m in range(3):
                q = 3 * n + m
                width = CH if q < 14 else 16
                sp.dma_start(part(g, m)[:, 0:KD * width].rearrange("p (k c) -> p k c", k=KD),
                             w[:, :, q * CH:q * CH + width]).then_inc(load_done[g % RING], 16)
        w_out_sp(sp, at, 5, A["mix_w_out_2"][0])

    def even_pool(pool, at):
        norm_pool(pool, at, 0)
        norm_pool(pool, at, 1)
        rpb = A["na_rpb_2"]
        rel_rows, rel_cols = rpb.shape[2], rpb.shape[3]
        size = rpb_copies.shape[1]
        pool.dma_start(rpb_copies, rpb.rearrange("a h r c -> (a h r c)").partition_broadcast(GRID))\
            .then_inc(even_copies, 16)
        pool.wait_ge(even_copies, 16)
        for h in range(NH):
            if h == 0:
                pool.wait_ge(even_s, len(EVEN))
            if h >= 2:
                pool.wait_ge(even_m, 2 * (h - 1))
            for i in range(4):
                dst = e_bias[(i % 2) * GRID:(i % 2 + 1) * GRID, h % 2, i // 2, :].rearrange("p (a c) -> p a c", a=4)
                src = bass.AP(tensor=rpb_copies.tensor,
                              offset=(h * rel_rows + rel_rows // 2 - i) * rel_cols + rel_cols // 2,
                              ap=[[size - 1, GRID], [rel_cols, 4], [1, GRID]])
                pool.dma_start(dst, src).then_inc(even_bias[h % 2], 16)
        pool.wait_ge(ml_ss, 1)
        inv_sqrt(pool, e_hss, e_hss, 1.0 / MW, EPS).then_inc(ml_rs, 1)

    def even_pe(pe, at):
        norm_pe(pe, at, 0)
        pe.wait_ge(hT_ready, 2 * TT * (at["norm"] + 1))
        norm_pe(pe, at, 1)
        gate_pe(pe, at)
        pe.wait_ge(hT_ready, 2 * TT * (at["norm"] + 2))
        last = -1
        for n, (q, is_T, side, i, *_) in enumerate(EVEN):
            g = at["load"] + q // 3
            if q // 3 != last:
                wait_loaded(pe, g)
                last = q // 3
            if n >= 4:
                pe.wait_ge(even_s, n - 3)
            h = e_hx if side else hT
            width = CH if q < 14 else 16
            w = part(g, q % 3)[:, 0:KD * width].rearrange("p (k c) -> p k c", k=KD)
            for k in range(KD):
                if is_T:
                    ins = nc.tensor.matmul(ps[:, n % 4, 0:T], w[:, k, i * P:(i + 1) * P], h[:, k, :],
                                           start=(k == 0), stop=(k == KD - 1))
                else:
                    ins = nc.tensor.matmul(ps[:, n % 4, 0:width], h[:, k, i * P:(i + 1) * P], w[:, k, :],
                                           start=(k == 0), stop=(k == KD - 1))
            ins.then_inc(even_ps, 1)
        pe.wait_ge(even_s, len(EVEN))
        units = 2 * NH
        for u in range(units + 2):
            if u < units:
                h, t = divmod(u, 2)
                rows = slice((h % 2) * NDH, (h % 2 + 1) * NDH)
                if u >= 2:
                    pe.wait_ge(even_e, u - 1)
                nc.tensor.matmul(ps[:, u % 2, :], e_qaT[rows, h // 2, t * P:(t + 1) * P], e_kaT[rows, h // 2, :],
                                 start=True, stop=True).then_inc(even_z, 1)
            if 1 <= u <= units:
                v = u - 1
                pe.wait_ge(even_p, v + 1)
                if v >= 2:
                    pe.wait_ge(even_pts, v - 1)
                for c in range(4):
                    ins = nc.tensor.transpose(ps[:, 2 + v % 2, c * P:(c + 1) * P],
                                              e_p[:, v % 2, c * P:(c + 1) * P], ident)
                ins.then_inc(even_pt, 1)
            if u >= 2:
                v = u - 2
                h, t = divmod(v, 2)
                rows = slice((h % 2) * NDH, (h % 2 + 1) * NDH)
                pe.wait_ge(even_pts, v + 1)
                if v >= 2:
                    pe.wait_ge(mix_in_ready, mix_in_before(at) + v - 1)
                for c in range(4):
                    ins = nc.tensor.matmul(ps[rows, 4 + v % 2, 0:P], e_va[:, c, h * NDH:(h + 1) * NDH],
                                           e_pT[:, v % 2, c * P:(c + 1) * P], start=(c == 0), stop=(c == 3))
                ins.then_inc(even_o, 1)
        pe.wait_ge(mix_in_ready, mix_in_before(at) + units)
        pe.wait_ge(ml_gates, 2)
        lf = e_lf.rearrange("p (s d h) -> p s d h", s=4, d=2)
        b = ps[:, 6, 0:32].rearrange("p (s d h) -> p s d h", s=4, d=2)
        for d in range(2):
            nc.tensor.matmul(b[:, :, d, :], col(C_UPPER if d == 0 else C_FROM), lf[:, :, d, :], start=True, stop=True)
        nc.tensor.matmul(ps[:, 6, 32:64], col(C_ONES), e_lf, start=True, stop=True)
        for s in range(4):
            ins = nc.tensor.matmul(ps[0:8, 6, 64 + s:65 + s], e_lf[:, 8 * s:8 * s + 8], col(C_ONES, 1),
                                   start=True, stop=True)
        ins.then_inc(ml_sums, 1)
        pe.wait_ge(ml_gates, 3)
        for s in range(4):
            ins = nc.tensor.transpose(ps[0:8, 7, s * P:(s + 1) * P], e_we[:, 8 * s:8 * s + 8], ident)
        ins.then_inc(ml_sums, 1)
        pe.wait_ge(ml_gates, 4)
        nc.tensor.matmul(ps[:, 6, 128:160], consts[0:8, C_ONES:C_ONES + P], e_md, start=True, stop=True)\
            .then_inc(ml_sums, 1)
        for n, (src, t) in enumerate(((e_qb, 0), (e_qb, 1), (e_kb, 0), (e_kb, 1))):
            pe.wait_ge(ml_rot, n + 1)
            for c in range(MH):
                ins = nc.tensor.transpose(ps[:, n, c * P:(c + 1) * P], src[:, t, c * MW:(c + 1) * MW], ident)
            ins.then_inc(ml_T, 1)
        pe.wait_ge(ml_Ts, 4)

        def update(s, d):
            n = 2 * s + d
            pe.wait_ge(ml_ka, n + 1)
            for h in range(MH):
                ins = nc.tensor.matmul(ps[:, 4 + h // 2, (h % 2) * MX:(h % 2 + 1) * MX], e_ka[:, h * P:(h + 1) * P],
                                       e_vb[:, TILE[d][s], h, 0:MX], start=True, stop=True)
            ins.then_inc(ml_U, 1)

        for s in range(4):
            if s < 2:
                for d in range(2):
                    update(s, d)
                continue
            for d in range(2):
                n, tile = 2 * (s - 2) + d, TILE[d][s]
                q = [e_qT[:, h, tile * P:(tile + 1) * P] for h in range(MH)]
                if n:
                    pe.wait_ge(ml_on, n)
                pe.wait_ge(ml_C, 2 * (s - 1) + d + 1)
                for h in range(MH):
                    r = e_r[:, 8 * s + 4 * d + h:8 * s + 4 * d + h + 1]
                    nc.tensor.matmul(ps[:, 0, h * P:(h + 1) * P], r.to_broadcast([P, P]), ident, start=True, stop=True)
                    nc.tensor.matmul(ps[:, 1, h * P:(h + 1) * P], q[h], e_kT[:, h, tile * P:(tile + 1) * P],
                                     start=True, stop=True)
                    ins = nc.tensor.matmul(ps[:, 2 + h // 2, (h % 2) * MX:(h % 2 + 1) * MX], q[h],
                                           e_C[:, 4 * d + h, 0:MX], start=True, stop=True)
                ins.then_inc(ml_R, 1)
                pe.wait_ge(ml_s, n + 1)
                for h in range(MH):
                    ins = nc.tensor.transpose(ps[:, 7, h * P:(h + 1) * P], e_rm[:, d, h * P:(h + 1) * P], ident)
                ins.then_inc(ml_sT, 1)
                pe.wait_ge(ml_sTs, n + 1)
                for h in range(MH):
                    ins = nc.tensor.matmul(ps[:, 4 + h // 2, (h % 2) * MX:(h % 2 + 1) * MX],
                                           e_sT[:, d, h * P:(h + 1) * P], e_vb[:, tile, h, 0:MX], start=True, stop=True)
                ins.then_inc(ml_o, 1)
                if s == 2:
                    pe.wait_ge(ml_on, n + 1)
                    update(s, d)
        for t in range(TT):
            pe.wait_ge(ml_on, 4 + t + 1)
            for h in range(MH):
                ins = nc.tensor.transpose(ps[:, t, h * P:(h + 1) * P], xn[:, t, h * P:(h + 1) * P], ident)
            ins.then_inc(ml_T, 1)
        w_out_pe(pe, at, 5, hT)

    def even_act(act, at):
        norm_act(act, at, 0, src=x_ctx)
        norm_act(act, at, 1)
        gate_act(act, at)
        for n, (q, _, _, _, dst, func, factor) in enumerate(EVEN):
            width = CH if q < 14 else 16
            act.wait_ge(even_ps, n + 1)
            src = ps[:, n % 4, 0:width]
            if len(dst.shape) == 3:
                src = src.rearrange("p (h c) -> p h c", h=2)
            nc.scalar.activation(dst, src, func, scale=factor).then_inc(even_s, 1)
        act.wait_ge(ml_gates, 1)
        act_steps.done(act, nc.scalar.activation(e_gl, e_ga, ACT.Abs))
        act_steps.done(act, nc.scalar.activation(e_gl, e_gl, ACT.Exp, scale=-1.0))
        nc.scalar.activation(e_gl, e_gl, ACT.Ln, bias=1.0).then_inc(ml_exps, 1)
        units = 2 * NH
        for u in range(units + 2):
            if u < units:
                act.wait_ge(even_m, u + 1)
                if u >= 2:
                    act.wait_ge(even_pt, u - 1)
                nc.scalar.activation(e_p[:, u % 2, :], ps[:, u % 2, :], ACT.Exp, bias=e_nm[:, u % 2:u % 2 + 1],
                                     accum_out=e_sum[:, u % 2:u % 2 + 1]).then_inc(even_e, 1)
            if u >= 2:
                v = u - 2
                h, t = divmod(v, 2)
                rows = slice((h % 2) * NDH, (h % 2 + 1) * NDH)
                act.wait_ge(even_o, v + 1)
                nc.scalar.activation(hT[rows, h // 2, t * P:(t + 1) * P], ps[rows, 4 + v % 2, 0:P], ACT.Copy)\
                    .then_inc(mix_in_ready, 1)
        act.wait_ge(ml_gates, 5)
        nc.scalar.activation(e_ap[:, 0:24], e_ap[:, 0:24], ACT.Exp)
        nc.scalar.activation(e_at[:, 0:24], e_at[:, 0:24], ACT.Exp).then_inc(ml_exps, 1)
        for n in range(4):
            act.wait_ge(ml_T, n + 1)
            nc.scalar.activation((e_qT if n < 2 else e_kT)[:, :, (n % 2) * P:(n % 2 + 1) * P],
                                 ps[:, n, :].rearrange("p (h c) -> p h c", c=P), ACT.Copy).then_inc(ml_Ts, 1)
        for n in range(4):
            d = n % 2
            act.wait_ge(ml_w, n + 1)
            nc.scalar.activation(e_wi[:, 4 * d:4 * d + 4], e_wi[:, 4 * d:4 * d + 4], ACT.Exp)
            nc.scalar.activation(e_em[:, 4 * d:4 * d + 4], e_em[:, 4 * d:4 * d + 4], ACT.Exp, scale=-1.0)
            nc.scalar.activation(e_rm[:, d, :], e_rm[:, d, :], ACT.Exp).then_inc(ml_we2, 1)
            act.wait_ge(ml_sT, n + 1)
            nc.scalar.activation(e_sT[:, d, :], ps[:, 7, :], ACT.Copy).then_inc(ml_sTs, 1)

    def even_dve(dve, at):
        step = dve_steps.done
        norm_dve(dve, at, amp[:, 7, :], mod_cols(0, 3, 1), k=0, src=x_ctx, dst=e_hx)
        norm_dve(dve, at, amp[:, 1, :], mod_cols(0, 3, 0), k=1)
        step(dve, nc.vector.memset(e_vb[:, :, :, MW:MX], 1.0))
        dve.wait_ge(even_s, len(EVEN))
        dve.wait_ge(rows_loaded, ROWS_DMAS)
        nc.vector.tensor_tensor(e_ga.rearrange("p (t c) -> p t c", t=4), e_g, bc_mid(e_gb[:, :], 4),
                                ALU.add).then_inc(ml_gates, 1)
        units = 2 * NH
        window = col(C_WINDOW, 2 * T).rearrange("p (t k) -> p t k", t=TT)
        for u in range(units + 1):
            if u < units:
                h, t = divmod(u, 2)
                slot_ = u % 2
                if t == 0:
                    dve.wait_ge(even_bias[h % 2], 64 * (h // 2 + 1))
                    step(dve, nc.vector.tensor_tensor(e_bias[:, h % 2, :, :], e_bias[:, h % 2, :, :], window, ALU.add))
                dve.wait_ge(even_z, u + 1)
                step(dve, nc.vector.tensor_tensor(ps[:, slot_, 0:T], ps[:, slot_, 0:T], e_bias[:, h % 2, t, :],
                                                  ALU.add))
                nc.vector.tensor_reduce(e_nm[:, slot_:slot_ + 1], ps[:, slot_, :], AX.X, ALU.max,
                                        negate=True).then_inc(even_m, 1)
            if u >= 1:
                v = u - 1
                r = e_rec[:, v % 2:v % 2 + 1]
                dve.wait_ge(even_e, v + 1)
                step(dve, nc.vector.reciprocal(r, e_sum[:, v % 2:v % 2 + 1]))
                nc.vector.tensor_scalar(e_p[:, v % 2, :], e_p[:, v % 2, :], r, None, ALU.mult).then_inc(even_p, 1)
                dve.wait_ge(even_pt, v + 1)
                if v >= 2:
                    dve.wait_ge(even_o, v - 1)
                nc.vector.tensor_copy(e_pT[:, v % 2, :], ps[:, 2 + v % 2, :]).then_inc(even_pts, 1)
        dve.wait_ge(ml_exps, 1)
        dve.wait_ge(mix_in_ready, mix_in_before(at) + units)
        step(dve, nc.vector.scalar_tensor_tensor(out=e_gl, in0=e_ga, scalar=0.0, in1=e_gl,
                                                 op0=ALU.min, op1=ALU.subtract))
        gi, gf = (v.rearrange("p (t h d g) -> p t h d g", t=4, h=MH, d=2) for v in (e_ga, e_gl))
        for d in range(2):
            for s in range(4):
                c = slice(8 * s + 4 * d, 8 * s + 4 * d + 4)
                nc.vector.tensor_copy(e_li[:, c], gi[:, TILE[d][s], :, d, 0])
                ins = nc.vector.tensor_copy(e_lf[:, c], gf[:, TILE[d][s], :, d, 1])
                if d == 0 or s < 3:
                    step(dve, ins)
        ins.then_inc(ml_gates, 1)
        dve.wait_ge(ml_sums, 1)
        step(dve, nc.vector.tensor_copy(e_b, ps[:, 6, 0:32]))
        step(dve, nc.vector.tensor_tensor(e_r, e_li, e_b, ALU.subtract))
        step(dve, nc.vector.tensor_copy(e_be, ps[:, 6, 32:64]))
        step(dve, nc.vector.tensor_copy(e_ber, ps[0:8, 6, 64:68]))
        nc.vector.tensor_tensor(e_we, e_be, e_r, ALU.add).then_inc(ml_gates, 1)
        dve.wait_ge(ml_sums, 2)
        step(dve, nc.vector.tensor_reduce(e_wmax, ps[0:8, 7, :].rearrange("p (s c) -> p s c", c=P), AX.X, ALU.max))
        step(dve, nc.vector.memset(e_m, 0.0))
        for s in range(3):
            nxt = e_m[:, s + 1:s + 2]
            step(dve, nc.vector.tensor_tensor(nxt, e_ber[:, s:s + 1], e_m[:, s:s + 1], ALU.add))
            step(dve, nc.vector.tensor_tensor(nxt, nxt, e_wmax[:, s:s + 1], ALU.max))
        nc.vector.tensor_tensor(e_md.rearrange("p (s c) -> p s c", c=8), consts[0:8, None, C_IDENT:C_IDENT + 8].to_broadcast([8, 4, 8]),
                                e_m[:, :, None].to_broadcast([8, 4, 8]), ALU.mult).then_inc(ml_gates, 1)
        dve.wait_ge(ml_sums, 3)
        step(dve, nc.vector.tensor_copy(e_mb, ps[:, 6, 128:160]))
        step(dve, nc.vector.tensor_tensor(e_t[:, 0:24], e_be[:, 0:24], e_mb[:, 0:24], ALU.add))
        step(dve, nc.vector.tensor_tensor(e_ap[:, 0:24], e_t[:, 0:24], e_mb[:, 8:32], ALU.subtract))
        nc.vector.tensor_tensor(e_at[:, 0:24], e_we[:, 0:24], e_mb[:, 8:32], ALU.subtract).then_inc(ml_gates, 1)
        for n, (src, t) in enumerate(((e_qb, 0), (e_qb, 1), (e_kb, 0), (e_kb, 1))):
            v = src[:, t, :].rearrange("p (h c two) -> p h c two", h=MH, two=2)
            for h in range(MH):
                def fin(ins):
                    if h < MH - 1:
                        step(dve, ins)
                    else:
                        ins.then_inc(ml_rot, 1)
                        dve.wait_ge(ml_rot, n + 1)
                x1, x2 = v[:, h:h + 1, :, 0], v[:, h:h + 1, :, 1]
                rotate(dve, step, x1, x2, x1, x2, col(C_AXIAL + P * t, 64), col(C_AXIAL + P * t + 64, 64), e_rot, fin)
        dve.wait_ge(ml_exps, 2)

        def heads(ap, w=P):
            return ap.rearrange("p (h c) -> p h c", c=w)

        def two_banks(bank):
            return ps[:, bank:bank + 2, 0:2 * MX].rearrange("p b (h c) -> p b h c", c=MX)

        def pairs(ap):
            return ap.rearrange("p (b h) c -> p b h c", b=2)

        def bc4(cols_ap):
            return cols_ap.rearrange("p (b h) -> p b h", b=2)[:, :, :, None].to_broadcast([P, 2, 2, MX])

        def update(s, d):
            n = 2 * s + d
            c = slice(8 * s + 4 * d, 8 * s + 4 * d + 4)
            if n:
                dve.wait_ge(ml_U, n)
            nc.vector.tensor_tensor(heads(e_ka), heads(e_kb[:, TILE[d][s], :]), bc_last(e_at[:, c], P), ALU.mult)\
                .then_inc(ml_ka, 1)
            state = e_C[:, 4 * d:4 * d + 4, 0:MX]
            if s:
                step(dve, nc.vector.tensor_tensor(state, state, bc_last(e_ap[:, c], MX), ALU.mult))
            dve.wait_ge(ml_U, n + 1)
            if s:
                ins = nc.vector.tensor_tensor(pairs(state), pairs(state), two_banks(4), ALU.add)
            else:
                ins = nc.vector.tensor_copy(pairs(state), two_banks(4))
            ins.then_inc(ml_C, 1)
            dve.wait_ge(ml_C, n + 1)

        for s in range(4):
            for d in range(2):
                if s < 2:
                    update(s, d)
                    continue
                n, tile = 2 * (s - 2) + d, TILE[d][s]
                c, c4 = slice(8 * s + 4 * d, 8 * s + 4 * d + 4), slice(4 * d, 4 * d + 4)
                rm = e_rm[:, d, :]
                mask = col(C_CNEG) if d == 0 else col(C_EARLIER)
                dve.wait_ge(ml_R, n + 1)
                step(dve, nc.vector.tensor_tensor(heads(rm), heads(ps[:, 0, :]), bc_mid(mask, MH), ALU.add))
                step(dve, nc.vector.tensor_reduce(e_mx[:, c4], heads(rm), AX.X, ALU.max))
                step(dve, nc.vector.tensor_tensor(e_mx[:, c4], e_mx[:, c4], e_mb[:, c], ALU.max))
                step(dve, nc.vector.tensor_tensor(e_wi[:, c4], e_mb[:, c], e_mx[:, c4], ALU.subtract))
                step(dve, nc.vector.tensor_tensor(e_em[:, c4], e_b[:, c], e_mx[:, c4], ALU.add))
                nc.vector.tensor_tensor(heads(rm), heads(rm), bc_last(e_mx[:, c4], P), ALU.subtract)\
                    .then_inc(ml_w, 1)
                dve.wait_ge(ml_we2, n + 1)
                nc.vector.tensor_tensor(rm, rm, ps[:, 1, :], ALU.mult).then_inc(ml_s, 1)
                o = pairs(e_o[:, :, 0:MX])
                step(dve, nc.vector.tensor_tensor(o, two_banks(2), bc4(e_wi[:, c4]), ALU.mult))
                dve.wait_ge(ml_o, n + 1)
                step(dve, nc.vector.tensor_tensor(o, o, two_banks(4), ALU.add))
                den, raw = e_den[:, c4], e_o[:, :, MW]
                step(dve, nc.vector.tensor_scalar(den, raw, -1.0, None, ALU.mult))
                step(dve, nc.vector.tensor_tensor(den, den, raw, ALU.max))
                step(dve, nc.vector.tensor_tensor(den, den, e_em[:, c4], ALU.max))
                step(dve, nc.vector.reciprocal(den, den))
                h_t = heads(xn[:, tile, 0:MH * P])
                if s == 2:
                    ins = nc.vector.tensor_tensor(h_t, e_o[:, :, 0:MW], bc_last(den, MW), ALU.mult)
                else:
                    step(dve, nc.vector.tensor_tensor(e_o[:, :, 0:MW], e_o[:, :, 0:MW], bc_last(den, MW), ALU.mult))
                    ins = nc.vector.tensor_tensor(h_t, h_t, e_o[:, :, 0:MW], ALU.add)
                ins.then_inc(ml_on, 1)
                dve.wait_ge(ml_on, n + 1)
                if s == 2:
                    update(s, d)
        h_all = xn[:, :, 0:MH * P]
        sq = xn[:, :, MH * P:D]
        step(dve, nc.vector.tensor_tensor(sq, h_all, h_all, ALU.mult))
        for t in range(TT):
            ins = nc.vector.tensor_reduce(e_hss[:, 4 * t:4 * t + 4], heads(sq[:, t, :]), AX.X, ALU.add)
            if t == 0:
                step(dve, ins)
        ins.then_inc(ml_ss, 1)
        dve.wait_ge(ml_rs, 1)
        for t in range(TT):
            v = xn[:, t, 0:MH * P]
            step(dve, nc.vector.tensor_tensor(heads(v), heads(v), bc_last(e_hss[:, 4 * t:4 * t + 4], P), ALU.mult))
            nc.vector.tensor_tensor(v, v, e_ob[:, t, :], ALU.mult).then_inc(ml_on, 1)
        for t in range(TT):
            dve.wait_ge(ml_T, 4 + t + 1)
            for k in range(2):
                gains = cols_T[:, 0, 98 + 2 * k:100 + 2 * k]
                nc.vector.tensor_tensor(hT[:, 4 + 2 * k:6 + 2 * k, t * P:(t + 1) * P],
                                        heads(ps[:, t, k * T:(k + 1) * T]), bc_last(gains, P), ALU.mult)\
                    .then_inc(mix_in_ready, 1)
        w_out_wait(dve, at)
        add_to_x(dve, x_sb, 1.0, gate_row)

    def sgu_all_sp(sp, at):
        sgu_sp(sp, at)
        sgu_weights_sp(sp, at)

    SP = {"ffn": ffn_sp, "gdn": gdn_sp_, "sb": sb_sp, "dsa": dsa_sp, "mod": mod_sp, "even": even_sp,
          "sgu": sgu_all_sp, "final": final_sp}
    ACTS = {"ffn": ffn_act, "gdn": gdn_act, "sb": sb_act, "dsa": dsa_act, "mod": mod_act, "even": even_act,
            "sgu": sgu_act, "final": final_act}
    DVES = {"ffn": ffn_dve, "gdn": gdn_dve, "sb": sb_dve, "dsa": dsa_dve, "mod": mod_dve, "even": even_dve,
            "sgu": sgu_dve, "final": final_dve}
    PES = {"ffn": ffn_pe, "gdn": gdn_pe, "sb": sb_pe, "dsa": dsa_pe, "mod": mod_pe, "even": even_pe,
           "sgu": sgu_pe, "final": nothing}
    POOLS = {"ffn": norm_pool, "gdn": gdn_pool, "sb": norm_pool, "dsa": dsa_pool, "mod": nothing,
             "even": even_pool, "sgu": sgu_pool, "final": final_pool}

    last_update = PLACES[-1]["update"] + (PLAN[-1][0] != "mod" and PLAN[-1] != ("ffn", CTX_FFN))
    with nc.Block() as block:

        @block.sync
        def _(sp):
            sp.dma_start(consts[:, :], A["consts"]).then_inc(consts_loaded, 16)
            sp.dma_start(x_sb[:, :, :], A["x"][0].rearrange("(t p) d -> p t d", p=P)).then_inc(x_loaded, 16)
            r = 0
            for name, rows in (("ffn1_norm", 4), ("mix_norm", 4), ("ffn2_norm", 4)):
                sp.dma_start(gain_rows[r:r + rows, :], A[name]).then_inc(gains_loaded, 16)
                r += rows
            sp.dma_start(gain_rows[r:r + 6, :], A["norm_g_2"].rearrange("l j d -> (l j) d")).then_inc(gains_loaded, 16)
            sp.dma_start(gain_rows[18:19, :], A["c_2"]).then_inc(gains_loaded, 16)
            sp.dma_start(gain_rows[19:20, :], A["c_ctx_2"].rearrange("(a d) -> a d", a=1)).then_inc(gains_loaded, 16)
            for j in range(2):
                sp.dma_start(col_rows[0:96, j, :], A["gdn_conv"][j].rearrange("w (c p) -> (w c) p", p=P))\
                    .then_inc(gains_loaded, 16)
            for r, name in ((96, "gdn_norm"), (98, "ml_head_g_2"), (102, "dsa_cq_norm"), (105, "dsa_ckv_norm")):
                v = A[name].rearrange("l h d -> (l h) d") if name == "ml_head_g_2" else \
                    A[name].rearrange("l (c p) -> (l c) p", p=P)
                sp.dma_start(col_rows[r:r + v.shape[0], 0, :], v).then_inc(gains_loaded, 16)
            for j in range(2):
                for c, name in ((0, "gdn_dt_bias"), (8, "gdn_a_log")):
                    sp.dma_start(g_rows[:, j, c:c + 8], A[name][j].partition_broadcast(P)).then_inc(rows_loaded, 16)
            sp.dma_start(e_gb[:, :], A["ml_gate_b_2"].rearrange("a h d g -> (a h d g)").partition_broadcast(P))\
                .then_inc(rows_loaded, 16)
            sp.dma_start(d_gk[:, :], A["dsa_kidx_norm"][0].partition_broadcast(P)).then_inc(rows_loaded, 16)
            for at in PLACES:
                SP[at["kind"]](sp, at)
            if PLAN[-1] != ("final", 1):
                sp.wait_ge(x_ready, TT * last_update)
                sp.dma_start(out[0].rearrange("(t p) d -> p t d", p=P), x_sb[:, :, :]).then_inc(out_done, 16)
            sp.wait_ge(out_done, 16 * (1 + (PLAN[-1] == ("final", 1))))

        @block.scalar
        def _(act):
            for at in PLACES:
                ACTS[at["kind"]](act, at)

        @block.vector
        def _(dve):
            dve.wait_ge(gains_turned, 1)
            nc.vector.tensor_copy(gain[:, :, :], ps[:, 4, 0:KD * NGAIN].rearrange("p (k n) -> p k n", n=NGAIN))\
                .then_inc(gains_ready, 1)
            nc.vector.tensor_copy(cols_T[:, 0, 0:107], ps[:, 5, 0:107]).then_inc(gains_ready, 1)
            nc.vector.tensor_copy(cols_T[:, 1, 0:96], ps[:, 5, P:P + 96]).then_inc(gains_ready, 1)
            dve.wait_ge(gains_ready, 3)
            for at in PLACES:
                DVES[at["kind"]](dve, at)

        @block.gpsimd
        def _(pool):
            pool.wait_ge(consts_loaded, 16)
            for at in PLACES:
                POOLS[at["kind"]](pool, at)

        @block.tensor
        def _(pe):
            pe.wait_ge(consts_loaded, 16)
            pe.wait_ge(gains_loaded, 16 * 12)
            for k in range(KD):
                ins = nc.tensor.transpose(ps[:, 4, k * NGAIN:(k + 1) * NGAIN], gain_rows[:, k * P:(k + 1) * P],
                                          consts[0:NGAIN, C_IDENT:C_IDENT + NGAIN])
            for j, rows in ((0, 107), (1, 96)):
                ins = nc.tensor.transpose(ps[:, 5, j * P:j * P + rows], col_rows[0:rows, j, :],
                                          consts[0:rows, C_IDENT:C_IDENT + rows])
            ins.then_inc(gains_turned, 1)
            pe.wait_ge(gains_ready, 3)
            for at in PLACES:
                PES[at["kind"]](pe, at)

    ctx.close()


def kernel(**inputs):
    import numpy as _np
    import concourse.bacc as _bacc
    from concourse import mybir as _mybir
    from concourse.bass_utils import run_bass_kernel_spmd as _run

    nc = _bacc.Bacc("TRN2", target_bir_lowering=False, num_devices=1)
    arrays, A = {}, {}
    given = {name: inputs[name] for name in INPUTS}
    given["consts"] = constants(_np)
    for name, a in given.items():
        a = _np.ascontiguousarray(a)
        arrays[f"in_{name}"] = a
        A[name] = nc.dram_tensor(f"in_{name}", a.shape, _mybir.dt.from_np(a.dtype), kind="ExternalInput").ap()
    out = nc.dram_tensor("out_x", (1, T, D), FP32, kind="ExternalOutput").ap()
    build(nc, A, out)
    r = _run(nc, [arrays], core_ids=[0])
    return r.results[0]["out_x"]
```

```python
import math
import concourse.bass as bass
from concourse import mybir
from contextlib import ExitStack

FP32 = mybir.dt.float32
FP32R = mybir.dt.float32r
ALU = mybir.AluOpType
ACT = mybir.ActivationFunctionType
AX = mybir.AxisListType

P = 128
D = 1024
KD = D // P
T = 256
TT = T // P
FF = 2816
EPS = 1e-6
CH = 256
NCH = FF // CH
NFT = FF // P
RING = 3
SLOT = 3 * KD * CH
PART = KD * CH
PEEL = NCH % RING
ITERS = NCH // RING
GU_SLOTS = 2
UPB = 3
PB = 512

PLAN = [("ffn", 0), ("gdn", 0), ("ffn", 1), ("ffn", 2), ("sb", 0), ("ffn", 3), ("ffn", 4), ("dsa", 0),
        ("ffn", 5), ("ffn", 6), ("gdn", 1), ("ffn", 7), ("final", 0), ("ctx", 0), ("ffn", 8), ("ffn", 9), ("even", 0),
        ("ffn", 10), ("ffn", 11), ("sgu", 0), ("ffn", 12), ("final", 1)]
LOADS = {"ffn": NCH, "gdn": 8, "sb": 6, "dsa": 5, "ctx": 0, "even": 7, "sgu": 10, "final": 0}
OWN_SIGNAL = {"gdn": 4, "sb": 2, "even": 5, "sgu": 6}
CTX_FFN = 8
NORMS = {"ffn": 1, "gdn": 1, "sb": 1, "dsa": 1, "ctx": 0, "even": 2, "sgu": 1, "final": 0}


def places():
    out, loads, mixer_loads, norms, ffns, updates = [], 0, 0, 0, 0, 0
    for kind, n in PLAN:
        layer = sum(k in ("gdn", "sb", "dsa") for k, _ in PLAN[:len(out)])
        out.append(dict(kind=kind, n=n, load=loads, mixer_load=mixer_loads, norm=norms, layer=layer, ffn=ffns,
                        update=updates))
        loads += LOADS[kind]
        mixer_loads += LOADS[kind] - OWN_SIGNAL.get(kind, 0) if kind != "ffn" else 0
        norms += NORMS[kind]
        ffns += kind == "ffn"
        updates += kind != "ctx" and not (kind == "ffn" and n == CTX_FFN)
    return out


PLACES = places()

INPUTS = ["x", "ffn1_norm", "ffn1_w_gu", "ffn1_w_down", "mix_norm", "ffn2_norm", "ffn2_w_gu", "ffn2_w_down",
          "gdn_w_in", "gdn_conv", "gdn_a_log", "gdn_dt_bias", "gdn_norm", "gdn_w_out", "sb_w_in", "sb_w_out",
          "dsa_w_in", "dsa_cq_norm", "dsa_ckv_norm", "dsa_kidx_norm", "dsa_w_uq", "dsa_w_qidx", "dsa_w_uk",
          "dsa_w_uv", "dsa_w_out", "final_norm", "c_2", "ctx_2", "c_ctx_2", "w_mod_2", "b_mod_2", "norm_g_2",
          "ffn_w_in_2", "ffn_w_out_2", "mix_w_in_2", "na_rpb_2", "ml_gate_b_2", "ml_head_g_2", "mix_w_out_2",
          "sg_w_in_2", "sg_ln_g_2", "sg_ln_b_2", "sg_w_s_2", "sg_b_s_2", "sg_w_out_2", "final_g_2"]

NGAIN = 20

ARENA = 19456
ROWS_DMAS = 16 * 7

C_IDENT = 0
C_NHALF = 128
C_ONES = 192
C_UPPER = 320
C_LOWER = 448
C_BLOCK = 576
C_SB = C_BLOCK + 7 * P
C_CNEG = C_SB + 384
C_ROPE16 = C_CNEG + 384
C_ROPE8 = C_ROPE16 + 64
C_AXIAL = C_ROPE8 + 32
C_FROM = C_AXIAL + 256
C_EARLIER = C_FROM + P
C_WINDOW = C_EARLIER + P
NCONST = C_WINDOW + 512


def rope_table(np, rot):
    half = rot // 2
    inv = np.float32(500000.0) ** (-np.arange(half, dtype=np.float32) * np.float32(2.0 / rot))
    ang = (np.arange(T, dtype=np.float32)[:, None] * inv[None, :]).astype(np.float32)
    return np.concatenate([np.cos(ang), np.sin(ang)], axis=1)


def constants(np):
    c = np.zeros((P, NCONST), np.float32)
    r, k = np.arange(P)[:, None], np.arange(P)[None, :]
    c[:, C_IDENT:C_IDENT + P] = r == k
    c[:, C_NHALF:C_NHALF + 64] = -0.5
    c[:, C_ONES:C_ONES + P] = 1
    c[:, C_UPPER:C_UPPER + P] = r <= k
    c[:, C_LOWER:C_LOWER + P] = r > k
    for n in range(7):
        m = 2 ** n
        c[:, C_BLOCK + n * P:C_BLOCK + (n + 1) * P] = (r // m % 2 == 1) & (k // m == r // m - 1)
    upper = (r < k).astype(np.float32)
    c[:, C_SB:C_SB + 384] = np.concatenate([upper, np.ones((P, P)), upper], axis=1)
    later = np.where(k > r, np.float32(-1e30), np.float32(0))
    c[:, C_CNEG:C_CNEG + 384] = np.concatenate([later, np.zeros((P, P)), later], axis=1)
    for t in range(TT):
        rows = slice(t * P, (t + 1) * P)
        c[:, C_ROPE16 + 32 * t:C_ROPE16 + 32 * t + 32] = rope_table(np, 32)[rows]
        c[:, C_ROPE8 + 16 * t:C_ROPE8 + 16 * t + 16] = rope_table(np, 16)[rows]
    c[:, C_FROM:C_FROM + P] = r >= k
    c[:, C_EARLIER:C_EARLIER + P] = np.where(k < r, np.float32(-1e30), np.float32(0))
    token = np.arange(T)
    inv = np.float32(10000.0) ** (-np.arange(32, dtype=np.float32) / np.float32(32))
    ang = np.concatenate([(token // 64).astype(np.float32)[:, None] * inv,
                          (token % 64).astype(np.float32)[:, None] * inv], axis=1)
    start = np.clip(token % 64 - 8, 0, 48)[:, None]
    inside = (token[None, :] % 64 >= start) & (token[None, :] % 64 < start + 16)
    for t in range(TT):
        rows = slice(t * P, (t + 1) * P)
        c[:, C_AXIAL + 128 * t:C_AXIAL + 128 * t + 64] = np.cos(ang)[rows]
        c[:, C_AXIAL + 128 * t + 64:C_AXIAL + 128 * t + 128] = np.sin(ang)[rows]
        c[:, C_WINDOW + T * t:C_WINDOW + T * (t + 1)] = np.where(inside[rows], np.float32(0), np.float32(-1e30))
    return c


def build(nc, A, out):
    ctx = ExitStack()

    def sb(name, shape):
        return ctx.enter_context(nc.sbuf_tensor(name, shape, FP32))

    def sem(name):
        return ctx.enter_context(nc.semaphore(name))

    with ExitStack() as shared:
        xn = shared.enter_context(nc.sbuf_tensor("xn", [P, TT, D], FP32))
        arena = shared.enter_context(nc.sbuf_tensor("arena", [P, ARENA], FP32))
        aT = shared.enter_context(nc.sbuf_tensor("aT", [P, UPB, T], FP32))

    def parts(name, shape):
        return ctx.enter_context(nc.sbuf_tensor(name, shape, FP32R))

    GU = 2 * KD * P
    h_hi = parts("h_hi", [P, KD, T])
    sb("kept", [P, ARENA - 2 * GU_SLOTS * GU - 2 * UPB * D - UPB * T - KD * T])
    gu_hi = parts("gu_hi", [P, GU_SLOTS, GU])
    gu_lo = parts("gu_lo", [P, GU_SLOTS, GU])
    down_hi = parts("down_hi", [P, UPB, D])
    down_lo = parts("down_lo", [P, UPB, D])
    h_lo = parts("h_lo", [P, KD, T])
    a_hi = parts("a_hi", [P, UPB, T])
    a_lo = parts("a_lo", [P, UPB, T])
    hT = sb("hT", [P, KD, T])
    ring = sb("ring", [P, RING, SLOT])
    x_sb = sb("x_sb", [P, TT, D])
    silu = sb("silu", [P, UPB, T])
    sumsq = sb("sumsq", [P, TT])
    rstd = sb("rstd", [P, TT])
    consts = sb("consts", [P, NCONST])
    h_flat = hT[:, :, :].rearrange("p k t -> p (k t)")
    gain_rows = h_flat[0:NGAIN, 0:D]
    col_rows = h_flat[:, D:D + 2 * P].rearrange("p (j c) -> p j c", j=2)
    cols_T = sb("cols_T", [P, 2, P])
    gain = sb("gain", [P, KD, NGAIN])
    ps = ctx.enter_context(nc.psum_tensor("ps", [P, 8, PB], FP32))
    ident = consts[:, C_IDENT:C_IDENT + P]

    x_loaded = sem("x_loaded")
    rows_loaded = sem("rows_loaded")
    consts_loaded = sem("consts_loaded")
    gains_loaded = sem("gains_loaded")
    gains_turned = sem("gains_turned")
    gains_ready = sem("gains_ready")
    load_done = [sem(f"load_done{i}") for i in range(RING)]
    load_used = sem("load_used")
    x_ready = sem("x_ready")
    sumsq_ready = sem("sumsq_ready")
    rstd_ready = sem("rstd_ready")
    xn_ready = sem("xn_ready")
    turned = sem("turned")
    hT_ready = sem("hT_ready")
    up_done = sem("up_done")
    silu_done = sem("silu_done")
    act_done = sem("act_done")
    down_done = sem("down_done")
    gu_upper = sem("gu_upper")
    gu_lower = sem("gu_lower")
    down_upper = sem("down_upper")
    down_lower = sem("down_lower")
    h_upper = sem("h_upper")
    h_split = sem("h_split")
    a_parts = sem("a_parts")
    out_done = sem("out_done")
    dve_step = sem("dve_step")
    act_step = sem("act_step")
    pool_step = sem("pool_step")

    class Steps:

        def __init__(self, sem):
            self.sem, self.count = sem, 0

        def done(self, eng, ins):
            self.count += 1
            ins.then_inc(self.sem, 1)
            eng.wait_ge(self.sem, self.count)

    dve_steps, act_steps, pool_steps = Steps(dve_step), Steps(act_step), Steps(pool_step)

    def wait_loaded(pe, load):
        pe.wait_ge(load_done[load % RING], 48 * (load // RING + 1))

    def wait_slot_free(sp, load):
        before = load - RING
        if before < 0:
            return
        at = [at for at in PLACES if at["load"] <= before and LOADS[at["kind"]]][-1]
        if at["kind"] == "ffn":
            sp.wait_ge(down_lower, NFT * at["ffn"] + 2 * (before - at["load"] + 1))
        elif before - at["load"] < OWN_SIGNAL.get(at["kind"], 0):
            n = before - at["load"] + 1
            if at["kind"] == "gdn":
                sp.wait_ge(gdn_qkv, NQKV * at["n"] + 6 * n)
            elif at["kind"] == "sb":
                sp.wait_ge(sb_qk, 6 * n)
            elif at["kind"] == "even":
                sp.wait_ge(even_ps, EVEN_ENDS[n - 1])
            else:
                sp.wait_ge(sgu_ps, min(6 * n, len(SGU)))
        else:
            before -= OWN_SIGNAL.get(at["kind"], 0)
            sp.wait_ge(load_used, at["mixer_load"] + before - at["load"] + 1)

    def slot(load):
        return ring[:, load % RING, :]

    def part(load, n):
        return ring[:, load % RING, n * PART:(n + 1) * PART]

    def norm_act(act, at, k=0, src=x_sb):
        n = at["norm"] + k
        for t in range(TT):
            if src is not x_sb:
                if at["kind"] == "ffn":
                    act.wait_ge(ctx_loaded, 16)
                    act.wait_ge(x_ready, TT * at["update"])
                else:
                    act.wait_ge(ctx_ready, t + 1)
                    if at["update"]:
                        act.wait_ge(x_ready, TT * at["update"])
            elif at["update"]:
                act.wait_ge(x_ready, TT * (at["update"] - 1) + t + 1)
            else:
                act.wait_ge(x_loaded, 16)
            if n:
                act.wait_ge(turned, 2 * TT * n)
            if at["kind"] == "ffn" and at["n"] == CTX_FFN + 1:
                act.wait_ge(ctx_ready, TT)
            nc.scalar.activation(xn[:, t, :], src[:, t, :], ACT.Square,
                                 accum_out=sumsq[:, t:t + 1]).then_inc(sumsq_ready, 1)

    def inv_sqrt(pool, dst, src, factor, eps):
        pool_steps.done(pool, nc.gpsimd.tensor_scalar(dst, src, factor, eps, ALU.mult, ALU.add))
        return nc.gpsimd.tensor_tensor(dst, dst, consts[:, C_NHALF:C_NHALF + dst.shape[-1]], ALU.pow)

    def norm_pool(pool, at, k=0):
        for t in range(TT):
            pool.wait_ge(sumsq_ready, TT * (at["norm"] + k) + t + 1)
            inv_sqrt(pool, rstd[:, t:t + 1], sumsq[:, t:t + 1], 1.0 / D, EPS).then_inc(rstd_ready, 1)

    def norm_dve(dve, at, scale, shift=None, k=0, src=x_sb, dst=hT):
        n = at["norm"] + k
        for t in range(TT):
            dve.wait_ge(rstd_ready, TT * n + t + 1)
            nc.vector.tensor_scalar(xn[:, t, :], src[:, t, :], rstd[:, t:t + 1], None,
                                    ALU.mult).then_inc(xn_ready, 1)
        for t in range(TT):
            for h in range(2):
                dve.wait_ge(turned, 2 * TT * n + 2 * t + h + 1)
                src_ps = ps[:, 4 + 2 * t + h, :].rearrange("p (k c) -> p k c", c=P)
                dst_h = dst[:, 4 * h:4 * h + 4, t * P:(t + 1) * P]
                g = scale[:, 4 * h:4 * h + 4, None].to_broadcast([P, 4, P])
                ins = nc.vector.tensor_tensor(dst_h, src_ps, g, ALU.mult)
                if shift is not None:
                    dve_steps.done(dve, ins)
                    s = shift[:, 4 * h:4 * h + 4, None].to_broadcast([P, 4, P])
                    ins = nc.vector.tensor_tensor(dst_h, dst_h, s, ALU.add)
                ins.then_inc(hT_ready, 1)

    def norm_pe(pe, at, k=0):
        n = at["norm"] + k
        for t in range(TT):
            pe.wait_ge(xn_ready, TT * n + t + 1)
            for h in range(2):
                for c in range(4):
                    col = (4 * h + c) * P
                    ins = nc.tensor.transpose(ps[:, 4 + 2 * t + h, c * P:(c + 1) * P],
                                              xn[:, t, col:col + P], ident)
                ins.then_inc(turned, 1)

    def ffn_weights(n):
        if n < 8:
            i, second = divmod(n, 2)
            gu, down = (A["ffn2_w_gu"], A["ffn2_w_down"]) if second else (A["ffn1_w_gu"], A["ffn1_w_down"])
            return gu[i], down[i]
        l, j = {8: (0, 0), 9: (0, 0), 10: (0, 1), 11: (1, 0), 12: (1, 1)}[n]
        return A["ffn_w_in_2"][l, j], A["ffn_w_out_2"][l, j]

    def ffn_sp(sp, at):
        gu, down = ffn_weights(at["n"])
        gu_v = gu.rearrange("(k p) f -> p k f", p=P)
        down_v = down.rearrange("(c j p) d -> c p j d", p=P, j=CH // P)

        def load(first, it=None):
            g = at["load"] + first
            s = g % RING
            if it is None:
                wait_slot_free(sp, g)
                col, chunk = first * CH, first
            else:
                sp.wait_ge(down_lower, NFT * at["ffn"] + 2 * (first - RING + 1) + it * (2 * RING))
                col, chunk = first * CH + it * (RING * CH), it * RING + first
            for side in range(2):
                sp.dma_start(part(g, side).rearrange("p (k f) -> p k f", k=KD),
                             gu_v[:, :, bass.ds(col + side * FF, CH)]).then_inc(load_done[s], 16)
            sp.dma_start(part(g, 2).rearrange("p (j d) -> p j d", d=D),
                         down_v[bass.ds(chunk, 1)].rearrange("a p j d -> p (a j) d")).then_inc(load_done[s], 16)

        first_loop = PEEL + RING
        for c in range(first_loop):
            load(c)
        with sp.Fori(0, (NCH - first_loop) // RING) as it:
            for u in range(RING):
                load(first_loop + u, it)

    def next_step(at):
        n = PLACES.index(at) + 1
        return PLACES[n] if n < len(PLACES) else None

    def last_step(at):
        n = PLACES.index(at)
        return PLACES[n - 1] if n else None

    def is_ffn(at):
        return at is not None and at["kind"] == "ffn"

    def gu_raw(g, j):
        return ring[:, g % RING, 0:2 * PART].rearrange("p (m f) -> p m f", f=CH)[:, :, (j % 2) * P:(j % 2 + 1) * P]

    def down_raw(g, j):
        return ring[:, g % RING, 2 * PART + (j % 2) * D:2 * PART + (j % 2 + 1) * D]

    def blocks(ap):
        return ap.rearrange("p (m f) -> p m f", f=P)

    def count(n, it, step):
        return n if it is None else n + step * it

    def gu_upper_act(act, at, j, it=None):
        g, f = at["load"] + j // 2, NFT * at["ffn"] + j
        if j % 2 == 0:
            act.wait_ge(load_done[g % RING], count(48 * (g // RING + 1), it, 48))
        if f >= GU_SLOTS:
            act.wait_ge(up_done, count(f - GU_SLOTS + 1, it, 2 * RING))
        nc.scalar.activation(blocks(gu_hi[:, f % GU_SLOTS, :]), gu_raw(g, j), ACT.Copy).then_inc(gu_upper, 1)

    def down_upper_act(act, at, j, it=None):
        g, f = at["load"] + j // 2, NFT * at["ffn"] + j
        if f >= UPB:
            act.wait_ge(down_done, count(f - UPB + 1, it, 2 * RING))
        nc.scalar.activation(down_hi[:, f % UPB, :], down_raw(g, j), ACT.Copy).then_inc(down_upper, 1)

    def gu_lower_dve(dve, at, j, it=None):
        g, f = at["load"] + j // 2, NFT * at["ffn"] + j
        dve.wait_ge(gu_upper, count(f + 1, it, 2 * RING))
        nc.vector.tensor_tensor(blocks(gu_lo[:, f % GU_SLOTS, :]), gu_raw(g, j), blocks(gu_hi[:, f % GU_SLOTS, :]),
                                ALU.subtract).then_inc(gu_lower, 1)

    def down_lower_dve(dve, at, j, it=None):
        g, f = at["load"] + j // 2, NFT * at["ffn"] + j
        dve.wait_ge(down_upper, count(f + 1, it, 2 * RING))
        nc.vector.tensor_tensor(down_lo[:, f % UPB, :], down_raw(g, j), down_hi[:, f % UPB, :], ALU.subtract)\
            .then_inc(down_lower, 1)

    def split_first_act(act, at):
        last = last_step(at)
        if is_ffn(last):
            return
        if last in MIXERS:
            if MIX_IN[last["kind"]]:
                act.wait_ge(mix_in_ready, mix_in_before(last) + MIX_IN[last["kind"]])
            else:
                act.wait_ge(load_used, at["mixer_load"])
        elif last is not None and last["kind"] == "ctx":
            act.wait_ge(mod_ready, 1)
        for j in range(GU_SLOTS):
            gu_upper_act(act, at, j)

    def split_first_dve(dve, at):
        if is_ffn(at) and not is_ffn(last_step(at)):
            for j in range(GU_SLOTS):
                gu_lower_dve(dve, at, j)

    def ffn_pe(pe, at):
        norm_pe(pe, at)
        if at["n"] >= 8:
            gate_pe(pe, at)
        f0 = NFT * at["ffn"]
        pe.wait_ge(h_split, 2 * TT * (at["ffn"] + 1))
        step = 2 * RING

        def up(i, it=None):
            f = f0 + i
            pe.wait_ge(gu_lower, count(f + 1, it, step))
            if f >= UPB:
                pe.wait_ge(act_done, count(f - UPB + 1, it, step))
            w_u, w_l = blocks(gu_hi[:, f % GU_SLOTS, :]), blocks(gu_lo[:, f % GU_SLOTS, :])
            for side in range(2):
                dst = ps[:, 4 + i % UPB, side * T:(side + 1) * T]
                for k in range(KD):
                    m = side * KD + k
                    nc.tensor.matmul(dst, w_u[:, m, :], h_hi[:, k, :], start=(k == 0), stop=False)
                    nc.tensor.matmul(dst, w_u[:, m, :], h_lo[:, k, :], start=False, stop=False)
                    ins = nc.tensor.matmul(dst, w_l[:, m, :], h_hi[:, k, :], start=False, stop=(k == KD - 1))
            ins.then_inc(up_done, 1)

        def down(i, it=None, first=False, last=False, only=None):
            f = f0 + i
            pe.wait_ge(act_done, count(f + 1, it, step))
            pe.wait_ge(down_lower, count(f + 1, it, step))
            w_u, w_l = down_hi[:, f % UPB, :], down_lo[:, f % UPB, :]
            for t in range(TT) if only is None else (only,):
                tokens = slice(t * P, (t + 1) * P)
                a_u, a_l = a_hi[:, i % UPB, tokens], a_lo[:, i % UPB, tokens]
                for h in range(2):
                    cols = slice(h * PB, (h + 1) * PB)
                    dst = ps[:, 2 * t + h, :]
                    nc.tensor.matmul(dst, a_u, w_u[:, cols], start=first, stop=False, skip_group_check=True)
                    nc.tensor.matmul(dst, a_u, w_l[:, cols], start=False, stop=False, skip_group_check=True)
                    ins = nc.tensor.matmul(dst, a_l, w_u[:, cols], start=False, stop=last, skip_group_check=True)
            if only is None or last:
                ins.then_inc(down_done, 1)

        tiles0 = 2 * PEEL
        for i in range(tiles0):
            up(i)
            if i >= 2:
                down(i - 2, first=(i == 2))
        with pe.Fori(0, ITERS) as it:
            for u in range(step):
                up(tiles0 + u, it)
                down(tiles0 + u - 2, it)
                if at["n"] < 8:
                    mod_pe(pe, at, u, it)
        for t in range(TT):
            for i in (NFT - 2, NFT - 1):
                down(i, last=(i == NFT - 1), only=t)

    def ffn_act(act, at):
        split_first_act(act, at)
        norm_act(act, at, src=x_ctx if at["n"] == CTX_FFN else x_sb)
        if at["n"] >= 8:
            gate_act(act, at)
        act.wait_ge(turned, 2 * TT * (at["norm"] + 1))
        for t in range(TT):
            for h in range(2):
                act.wait_ge(hT_ready, 2 * TT * at["norm"] + 2 * t + h + 1)
                part_ = (slice(None), slice(4 * h, 4 * h + 4), slice(t * P, (t + 1) * P))
                nc.scalar.activation(h_hi[part_], hT[part_], ACT.Copy).then_inc(h_upper, 1)
        f0 = NFT * at["ffn"]

        def tile(i, it):
            act.wait_ge(up_done, count(f0 + i + 1, it, 2 * RING))
            if f0 + i >= UPB:
                act.wait_ge(act_done, count(f0 + i - UPB + 1, it, 2 * RING))
            nc.scalar.activation(silu[:, i % UPB, :], ps[:, 4 + i % UPB, 0:T], ACT.Silu).then_inc(silu_done, 1)

        ffn_tiles(act, at, tile, gu_upper_act, down_upper_act)

    def ffn_tiles(eng, at, tile, gu_split, down_split):
        end = NFT + GU_SLOTS * is_ffn(next_step(at))

        def both(i, it=None):
            tile(i, it)
            if it is not None or i + GU_SLOTS < end:
                gu_split(eng, at, i + GU_SLOTS, it)
            down_split(eng, at, i, it)

        for i in range(2 * PEEL):
            both(i)
        with eng.Fori(0, ITERS - 1) as it:
            for u in range(2 * RING):
                both(2 * PEEL + u, it)
        for i in range(NFT - 2 * RING, NFT):
            both(i)

    def ffn_dve(dve, at):
        n, f0 = at["n"], NFT * at["ffn"]
        if not (last_step(at) in MIXERS):
            split_first_dve(dve, at)
        if n < 8:
            norm_dve(dve, at, gain[:, :, 8 * (n % 2) + n // 2])
        else:
            layer, j, cond, _ = GATES["ffn", n]
            norm_dve(dve, at, amp[:, 3 * layer + j + 6 * cond, :], mod_cols(layer, 3 * j, cond),
                     src=x_ctx if cond else x_sb)
        for t in range(TT):
            for h in range(2):
                dve.wait_ge(h_upper, 2 * TT * at["ffn"] + 2 * t + h + 1)
                part_ = (slice(None), slice(4 * h, 4 * h + 4), slice(t * P, (t + 1) * P))
                nc.vector.tensor_tensor(h_lo[part_], hT[part_], h_hi[part_], ALU.subtract).then_inc(h_split, 1)

        def tile(i, it):
            a, f, step = silu[:, i % UPB, :], f0 + i, 2 * RING
            dve.wait_ge(silu_done, count(f + 1, it, step))
            nc.vector.tensor_tensor(a, a, ps[:, 4 + i % UPB, T:2 * T], ALU.mult).then_inc(a_parts, 1)
            if f >= UPB:
                dve.wait_ge(down_done, count(f - UPB + 1, it, step))
            dve.wait_ge(a_parts, count(2 * f + 1, it, 2 * step))
            nc.vector.tensor_copy(a_hi[:, i % UPB, :], a).then_inc(a_parts, 1)
            dve.wait_ge(a_parts, count(2 * f + 2, it, 2 * step))
            nc.vector.tensor_tensor(a_lo[:, i % UPB, :], a, a_hi[:, i % UPB, :], ALU.subtract).then_inc(act_done, 1)

        ffn_tiles(dve, at, tile, gu_lower_dve, down_lower_dve)
        if n < 8:
            mod_dve(dve, at)
        done = [(down_done, f0 + NFT - TT + t + 1) for t in range(TT)]
        if n < 8:
            add_to_x(dve, done, x_sb, 0.5)
        elif n == CTX_FFN:
            add_to_x(dve, done, x_ctx, 1.0, gate_row, ctx_ready)
        else:
            add_to_x(dve, done, x_sb, 1.0, gate_row)

    def ffn_pool(pool, at):
        norm_pool(pool, at)
        if at["n"] < 8:
            mod_pool(pool, at)

    def add_to_x(dve, done, dst, factor, row=None, signal=None):
        for t in range(TT):
            dve.wait_ge(*done[t])
            for h in range(2):
                cols = slice(h * PB, (h + 1) * PB)
                src = ps[:, 2 * t + h, :]
                if row is not None:
                    dve_steps.done(dve, nc.vector.tensor_tensor(xn[:, t, cols], src, row[:, cols], ALU.mult))
                    src = xn[:, t, cols]
                ins = nc.vector.scalar_tensor_tensor(out=dst[:, t, cols], in0=src, scalar=factor,
                                                     in1=dst[:, t, cols], op0=ALU.mult, op1=ALU.add)
                if h == 1:
                    ins.then_inc(signal or x_ready, 1)
                else:
                    dve_steps.done(dve, ins)

    GH = 8

    mix_out_done = sem("mix_out_done")
    mix_in_ready = sem("mix_in_ready")

    class Carve:

        def __init__(self):
            self.at = 0

        def take(self, *shape):
            n = 1
            for s in shape:
                n *= s
            ap = arena[:, self.at:self.at + n]
            self.at += n
            assert self.at <= ARENA
            if len(shape) == 2:
                ap = ap.rearrange("p (a b) -> p a b", b=shape[1])
            if len(shape) == 3:
                ap = ap.rearrange("p (a b c) -> p a b c", b=shape[1], c=shape[2])
            return ap

    MIXERS = [a for a in PLACES if a["kind"] in ("gdn", "sb", "dsa", "even", "sgu")]

    MIX_IN = {"gdn": 4, "sb": GH, "dsa": GH, "even": 20, "sgu": 0}

    def mix_in_before(at):
        return sum(MIX_IN[a["kind"]] for a in MIXERS[:MIXERS.index(at)])

    def w_out_sp(sp, at, first, w, tiles=KD, per_load=4):
        w_v = w.rearrange("(k p) d -> p k d", p=P)
        for n in range(tiles // per_load):
            g = at["load"] + first + n
            wait_slot_free(sp, g)
            for m, (a, b) in enumerate(((0, 1), (1, 2), (2, per_load))):
                sp.dma_start(slot(g)[:, a * D:b * D].rearrange("p (k d) -> p k d", d=D),
                             w_v[:, per_load * n + a:per_load * n + b, :]).then_inc(load_done[g % RING], 16)

    def w_out_pe(pe, at, first, lhs, tiles=KD, per_load=4):
        if lhs is hT:
            pe.wait_ge(mix_in_ready, mix_in_before(at) + MIX_IN[at["kind"]])
        def row_tile(k, tokens):
            g = at["load"] + first + k // per_load
            if k % per_load == 0:
                wait_loaded(pe, g)
            for t in tokens:
                for h in range(2):
                    col = (k % per_load) * D + h * PB
                    ins = nc.tensor.matmul(ps[:, 2 * t + h, :], lhs[:, k, t * P:(t + 1) * P],
                                           slot(g)[:, col:col + PB], start=(k == 0), stop=(k == tiles - 1),
                                           skip_group_check=True)
            if k % per_load == per_load - 1 and TT - 1 in tokens:
                ins.then_inc(load_used, 1)
            return ins

        if tiles == KD:
            for t in range(TT):
                for k in range(tiles):
                    ins = row_tile(k, (t,))
                if t == 0:
                    ins.then_inc(mix_out_done, 1)
        else:
            for k in range(tiles):
                row_tile(k, range(TT))

    def w_out_done(dve, at, tiles=KD):
        split_first_dve(dve, next_step(at))
        end = (load_used, at["mixer_load"] + LOADS[at["kind"]] - OWN_SIGNAL.get(at["kind"], 0))
        early = [m for m in MIXERS if m["kind"] != "sgu"]
        return [(mix_out_done, early.index(at) + 1) if tiles == KD else end, end]

    def bc_last(ap, n):
        return ap[:, :, None].to_broadcast([P, ap.shape[1], n])

    def bc_mid(ap, n):
        return ap[:, None, :].to_broadcast([P, n, ap.shape[1]])

    def col(name, n=P):
        return consts[:, name:name + n]

    NQKV, LEVELS = 24, 7
    HG = 2
    GW = 4 * P
    car = Carve()
    g_tok = car.take(TT, 3 * D)
    g_T = car.take(16, T)
    g_z = car.take(TT, D)
    g_L, g_C, g_Ti, g_V, g_W, g_QK = (car.take(HG, GW) for _ in range(6))
    g_S = car.take(GH, P)
    g_sq = g_T[:, 0:8, :].rearrange("p c t -> p (c t)")
    g_small = sb("g_small", [P, 256])
    g_in = g_small[:, 0:16]
    g_g = g_small[:, 16:32]
    g_beta = g_small[:, 32:48]
    g_gc = g_small[:, 48:64]
    g_eg = g_small[:, 64:80]
    g_kd = g_small[:, 80:88]
    g_nb = g_small[:, 88:96]
    g_t1 = g_small[:, 96:112]
    g_t2 = g_small[:, 112:128]
    g_ss = g_small[:, 128:160]
    g_oss = g_small[:, 160:176]
    g_A = g_small[:, 176:184]
    g_rows = sb("g_rows", [P, 2, 16])
    g_cw = cols_T[:, :, 0:96]
    g_ng = cols_T[:, 0, 96:98]

    gdn_qkv = sem("gdn_qkv")
    gdn_tap = sem("gdn_tap")
    gdn_conv = sem("gdn_conv")
    gdn_silu = sem("gdn_silu")
    gdn_flip = sem("gdn_flip")
    gdn_tok = sem("gdn_tok")
    gdn_zps = sem("gdn_zps")
    gdn_z = sem("gdn_z")
    gdn_gps = sem("gdn_gps")
    gdn_y = sem("gdn_y")
    gdn_sp = sem("gdn_sp")
    gdn_g = sem("gdn_g")
    gdn_gcps = sem("gdn_gcps")
    gdn_gc = sem("gdn_gc")
    gdn_eg = sem("gdn_eg")
    gdn_ss = sem("gdn_ss")
    gdn_rs = sem("gdn_rs")
    gdn_n = sem("gdn_n")
    gdn_Tps = sem("gdn_Tps")
    gdn_T = sem("gdn_T")
    gdn_kd = sem("gdn_kd")
    gdn_prep = sem("gdn_prep")
    gdn_D = sem("gdn_D")
    gdn_E = sem("gdn_E")
    gdn_L = sem("gdn_L")
    gdn_C = sem("gdn_C")
    gdn_Wps = sem("gdn_Wps")
    gdn_W = sem("gdn_W")
    gdn_TV = sem("gdn_TV")
    gdn_V = sem("gdn_V")
    gdn_ks = sem("gdn_ks")
    gdn_r = sem("gdn_r")
    gdn_ups = sem("gdn_ups")
    gdn_u = sem("gdn_u")
    gdn_Sps = sem("gdn_Sps")
    gdn_S = sem("gdn_S")
    gdn_ops = sem("gdn_ops")
    gdn_o = sem("gdn_o")
    gdn_on = sem("gdn_on")
    gdn_oT = sem("gdn_oT")

    def gdn_sp_(sp, at):
        w = A["gdn_w_in"][at["n"]].rearrange("(k p) c -> p k c", p=P)

        def cols(g, n, c, width=CH):
            return sp.dma_start(part(g, n)[:, 0:KD * width].rearrange("p (k c) -> p k c", k=KD),
                                w[:, :, c:c + width])

        for n in range(4):
            g = at["load"] + n
            wait_slot_free(sp, g)
            for m in range(3):
                cols(g, m, (3 * n + m) * CH).then_inc(load_done[g % RING], 16)
        g = at["load"] + 4
        wait_slot_free(sp, g)
        for m in range(3):
            cols(g, m, 3 * D + m * CH).then_inc(load_done[g % RING], 16)
        g = at["load"] + 5
        wait_slot_free(sp, g)
        cols(g, 0, 3 * D + 3 * CH).then_inc(load_done[g % RING], 16)
        cols(g, 1, 4 * D, 16).then_inc(load_done[g % RING], 32)
        w_out_sp(sp, at, 6, A["gdn_w_out"][at["n"]])

    def gdn_pe(pe, at):
        j = at["n"]
        norm_pe(pe, at)
        pe.wait_ge(hT_ready, 2 * TT * (at["norm"] + 1))

        def turn(c):
            pe.wait_ge(gdn_silu, NQKV * j + c + 1)
            if NQKV * j + c >= 3:
                pe.wait_ge(gdn_tok, NQKV * j + c - 2)
            for t in range(TT):
                ins = nc.tensor.transpose(ps[:, 4 + c % 3, t * P:(t + 1) * P],
                                          silu[:, c % 3, t * P:(t + 1) * P], ident)
            ins.then_inc(gdn_flip, 1)

        for c in range(NQKV):
            g = at["load"] + c // 6
            if c % 6 == 0:
                wait_loaded(pe, g)
            if NQKV * j + c >= 3:
                pe.wait_ge(gdn_conv, NQKV * j + c - 2)
            w = part(g, c % 6 // 2).rearrange("p (k c) -> p k c", k=KD)
            for k in range(KD):
                ins = nc.tensor.matmul(ps[:, c % 3, 0:T], w[:, k, (c % 2) * P:(c % 2 + 1) * P], hT[:, k, :],
                                       start=(k == 0), stop=(k == KD - 1))
            ins.then_inc(gdn_qkv, 1)
            if c >= 2:
                turn(c - 2)
        turn(NQKV - 2)
        turn(NQKV - 1)
        pe.wait_ge(gdn_conv, NQKV * (j + 1))
        pe.wait_ge(gdn_tok, NQKV * (j + 1))
        for q in range(4):
            g = at["load"] + 4 + q // 3
            if q % 3 == 0:
                wait_loaded(pe, g)
            w = part(g, q % 3).rearrange("p (k c) -> p k c", k=KD)
            for t in range(TT):
                for k in range(KD):
                    ins = nc.tensor.matmul(ps[:, 2 * t + q // 2, (q % 2) * CH:(q % 2 + 1) * CH],
                                           hT[:, k, t * P:(t + 1) * P], w[:, k, :],
                                           start=(k == 0), stop=(k == KD - 1))
                if q % 2:
                    ins.then_inc(gdn_zps, 1)
            if q == 2:
                ins.then_inc(load_used, 1)
        w = part(g, 1)[:, 0:16 * KD].rearrange("p (k c) -> p k c", k=KD)
        for t in range(TT):
            for k in range(KD):
                ins = nc.tensor.matmul(ps[:, 7, t * 16:(t + 1) * 16], hT[:, k, t * P:(t + 1) * P], w[:, k, :],
                                       start=(k == 0), stop=(k == KD - 1))
        ins.then_inc(load_used, 1)
        pe.wait_ge(gdn_g, j + 1)
        for t in range(TT):
            nc.tensor.matmul(ps[:, 7, 64 + 8 * t:72 + 8 * t], col(C_UPPER), g_g[:, 8 * t:8 * t + 8],
                             start=True, stop=True)
        nc.tensor.matmul(ps[:, 7, 80:88], col(C_ONES), g_g[:, 0:8], start=True, stop=True).then_inc(gdn_gcps, 1)
        for t in range(TT):
            pe.wait_ge(gdn_n, TT * j + t + 1)
            for q in range(4):
                if t == 0 and q == 0:
                    pe.wait_ge(gdn_z, 4 * (j + 1))
                if t == 1:
                    pe.wait_ge(gdn_T, 8 * j + q + 1)
                for c in range(4):
                    ins = nc.tensor.transpose(ps[:, q, c * P:(c + 1) * P],
                                              g_tok[:, t, (4 * q + c) * P:(4 * q + c + 1) * P], ident)
                ins.then_inc(gdn_Tps, 1)
        pe.wait_ge(gdn_T, 8 * (j + 1))
        for t in range(TT):
            for hg in range(HG):
                if t == 1:
                    pe.wait_ge(gdn_u, 4 * j + hg + 1)
                    pe.wait_ge(gdn_S, 2 * j + hg + 1)
                    pe.wait_ge(gdn_o, 4 * j + hg + 1)
                for h4 in range(4):
                    h, cs = 4 * hg + h4, slice(h4 * P, (h4 + 1) * P)
                    q_h, k_h = (g_T[:, h + o, t * P:(t + 1) * P] for o in (0, GH))
                    nc.tensor.matmul(ps[:, hg, cs], k_h, k_h, start=True, stop=True)
                    nc.tensor.matmul(ps[:, 2 + hg, cs], k_h, q_h, start=True, stop=True)
                    ins = nc.tensor.matmul(ps[:, 4 + hg, cs],
                                           g_g[:, 8 * t + h:8 * t + h + 1].to_broadcast([P, P]), col(C_UPPER),
                                           start=True, stop=True)
                ins.then_inc(gdn_prep, 1)
            for lv in range(LEVELS):
                for hg in range(HG):
                    pe.wait_ge(gdn_C, 28 * j + (LEVELS * t + lv) * HG + hg + 1)
                    if lv:
                        pe.wait_ge(gdn_V, 28 * j + (LEVELS * t + lv - 1) * HG + hg + 1)
                    for h4 in range(4):
                        cs = slice(h4 * P, (h4 + 1) * P)
                        if lv == 0:
                            ins = nc.tensor.transpose(ps[:, hg, cs], g_C[:, hg, cs], ident)
                        else:
                            ins = nc.tensor.matmul(ps[:, hg, cs], g_C[:, hg, cs], g_V[:, hg, cs],
                                                   start=True, stop=True)
                    ins.then_inc(gdn_Wps, 1)
                if lv == 0:
                    continue
                for hg in range(HG):
                    pe.wait_ge(gdn_W, 24 * j + ((LEVELS - 1) * t + lv - 1) * HG + hg + 1)
                    for h4 in range(4):
                        cs = slice(h4 * P, (h4 + 1) * P)
                        if lv < LEVELS - 1:
                            nc.tensor.matmul(ps[:, 2 + hg, cs], g_W[:, hg, cs], g_Ti[:, hg, cs],
                                             start=True, stop=True)
                        ins = nc.tensor.matmul(ps[:, 4 + hg, cs], g_Ti[:, hg, cs], g_W[:, hg, cs],
                                               start=True, stop=True)
                    ins.then_inc(gdn_TV, 1)
            for hg in range(HG):
                heads = [(4 * hg + h4, slice(h4 * P, (h4 + 1) * P)) for h4 in range(4)]
                pe.wait_ge(gdn_kd, j + 1)
                pe.wait_ge(gdn_V, 28 * j + (LEVELS * t + LEVELS - 1) * HG + hg + 1)
                if t == 1:
                    for h, cs in heads:
                        nc.tensor.matmul(ps[:, 6 + hg, cs], g_T[:, h, P:T], g_S[:, h, :], start=True, stop=True)
                        ins = nc.tensor.matmul(ps[:, 2 + hg, cs], g_T[:, GH + h, P:T], g_S[:, h, :],
                                               start=True, stop=True)
                    ins.then_inc(gdn_ks, 1)
                    pe.wait_ge(gdn_r, 2 * j + hg + 1)
                for h, cs in heads:
                    ins = nc.tensor.matmul(ps[:, hg, cs], g_V[:, hg, cs],
                                           g_tok[:, t, 2 * D + h * P:2 * D + (h + 1) * P], start=True, stop=True)
                ins.then_inc(gdn_ups, 1)
                pe.wait_ge(gdn_u, 4 * j + 2 * t + hg + 1)
                if t == 0:
                    for h, cs in heads:
                        ins = nc.tensor.matmul(ps[:, 2 + hg, cs], g_tok[:, 0, D + h * P:D + (h + 1) * P],
                                               g_tok[:, 0, 2 * D + h * P:2 * D + (h + 1) * P],
                                               start=True, stop=True)
                    ins.then_inc(gdn_Sps, 1)
                for h, cs in heads:
                    ins = nc.tensor.matmul(ps[:, 4 + hg, cs], g_QK[:, hg, cs],
                                           g_tok[:, t, 2 * D + h * P:2 * D + (h + 1) * P], start=True, stop=True)
                ins.then_inc(gdn_ops, 1)
        heads_to_hT_pe(pe, xn, gdn_on, TT * j, gdn_oT)
        w_out_pe(pe, at, 6, hT)

    def heads_to_hT_pe(pe, src, ready, before, turned_sem):
        for t in range(TT):
            pe.wait_ge(ready, before + t + 1)
            for h in range(2):
                for c in range(4):
                    ins = nc.tensor.transpose(ps[:, 4 + 2 * t + h, c * P:(c + 1) * P],
                                              src[:, t, (4 * h + c) * P:(4 * h + c + 1) * P], ident)
                ins.then_inc(turned_sem, 1)

    def gdn_act(act, at):
        j = at["n"]
        act.wait_ge(gains_ready, 6)
        act.wait_ge(rows_loaded, ROWS_DMAS)
        norm_act(act, at)

        def tap(c):
            act.wait_ge(gdn_qkv, NQKV * j + c + 1)
            if NQKV * j + c >= 3:
                act.wait_ge(gdn_silu, NQKV * j + c - 2)
            nc.scalar.activation(aT[:, c % 3, :], ps[:, c % 3, 0:T], ACT.Copy,
                                 scale=g_cw[:, j, 3 * NQKV + c:3 * NQKV + c + 1]).then_inc(gdn_tap, 1)

        def silu_of(c):
            act.wait_ge(gdn_conv, NQKV * j + c + 1)
            if NQKV * j + c >= 3:
                act.wait_ge(gdn_flip, NQKV * j + c - 2)
            nc.scalar.activation(silu[:, c % 3, :], aT[:, c % 3, :], ACT.Silu).then_inc(gdn_silu, 1)

        def to_tok(c):
            act.wait_ge(gdn_flip, NQKV * j + c + 1)
            nc.scalar.activation(g_tok[:, :, c * P:(c + 1) * P],
                                 ps[:, 4 + c % 3, 0:T].rearrange("p (t c) -> p t c", t=TT), ACT.Copy)\
                .then_inc(gdn_tok, 1)

        for c in range(NQKV + 2):
            if c < NQKV:
                tap(c)
            if 1 <= c <= NQKV:
                silu_of(c - 1)
            if c >= 2:
                to_tok(c - 2)
        for n, (h, t) in enumerate(((0, 0), (0, 1), (1, 0), (1, 1))):
            act.wait_ge(gdn_zps, 4 * j + n + 1)
            nc.scalar.activation(g_z[:, t, h * PB:(h + 1) * PB], ps[:, 2 * t + h, :], ACT.Silu).then_inc(gdn_z, 1)
        act.wait_ge(gdn_y, j + 1)
        nc.scalar.activation(g_beta, ps[:, 7, 0:32].rearrange("p (t c) -> p t c", t=TT)[:, :, 0:8], ACT.Exp,
                             scale=-1.0)
        act_steps.done(act, nc.scalar.activation(g_t1, g_in, ACT.Abs))
        act_steps.done(act, nc.scalar.activation(g_t2, g_t1, ACT.Exp, scale=-1.0))
        nc.scalar.activation(g_A, g_rows[:, j, 8:16], ACT.Exp)
        nc.scalar.activation(g_t1, g_t2, ACT.Ln, bias=1.0).then_inc(gdn_sp, 1)
        act.wait_ge(gdn_gc, j + 1)
        nc.scalar.activation(g_kd, g_t2[:, 0:8], ACT.Exp)
        nc.scalar.activation(g_eg, g_gc, ACT.Exp).then_inc(gdn_eg, 1)
        for t in range(TT):
            for q in range(4):
                act.wait_ge(gdn_Tps, 8 * j + 4 * t + q + 1)
                nc.scalar.activation(g_T[:, 4 * q:4 * q + 4, t * P:(t + 1) * P],
                                     ps[:, q, :].rearrange("p (c i) -> p c i", c=4), ACT.Copy).then_inc(gdn_T, 1)
        for t in range(TT):
            for hg in range(HG):
                act.wait_ge(gdn_D, 4 * j + 2 * t + hg + 1)
                nc.scalar.activation(g_QK[:, hg, :], g_QK[:, hg, :], ACT.Exp)
                nc.scalar.activation(g_L[:, hg, :], g_L[:, hg, :], ACT.Exp, scale=-1.0).then_inc(gdn_E, 1)
            for lv in range(1, LEVELS):
                for hg in range(HG):
                    act.wait_ge(gdn_Wps, 28 * j + (LEVELS * t + lv) * HG + hg + 1)
                    if lv > 1:
                        act.wait_ge(gdn_TV, 24 * j + ((LEVELS - 1) * t + lv - 2) * HG + hg + 1)
                    nc.scalar.activation(g_W[:, hg, :], ps[:, hg, :], ACT.Copy).then_inc(gdn_W, 1)
            for hg in range(HG):
                act.wait_ge(gdn_ups, 4 * j + 2 * t + hg + 1)
                nc.scalar.activation(g_tok[:, t, 2 * D + hg * GW:2 * D + (hg + 1) * GW], ps[:, hg, :], ACT.Copy)\
                    .then_inc(gdn_u, 1)
                if t == 0:
                    act.wait_ge(gdn_Sps, 2 * j + hg + 1)
                    nc.scalar.activation(g_S[:, 4 * hg:4 * hg + 4, :],
                                         ps[:, 2 + hg, :].rearrange("p (h c) -> p h c", c=P), ACT.Copy)\
                        .then_inc(gdn_S, 1)

    def gdn_dve(dve, at):
        j = at["n"]
        dve.wait_ge(rows_loaded, ROWS_DMAS)
        norm_dve(dve, at, gain[:, :, 4 + at["layer"]])
        step = dve_steps.done
        for c in range(NQKV):
            dve.wait_ge(gdn_tap, NQKV * j + c + 1)
            w = [g_cw[:, j, tap * NQKV + c:tap * NQKV + c + 1] for tap in range(4)]
            acc, x_c = aT[:, c % 3, :], ps[:, c % 3, 0:T]
            for back in (1, 2, 3):
                ins = nc.vector.scalar_tensor_tensor(out=acc[:, back:T], in0=x_c[:, 0:T - back],
                                                     scalar=w[3 - back], in1=acc[:, back:T],
                                                     op0=ALU.mult, op1=ALU.add)
                if back < 3:
                    step(dve, ins)
            ins.then_inc(gdn_conv, 1)
        dve.wait_ge(load_used, at["mixer_load"] + 2)
        gates = ps[:, 7, 0:32].rearrange("p (t c) -> p t c", t=TT)
        nc.vector.tensor_tensor(g_in.rearrange("p (t h) -> p t h", t=TT), gates[:, :, 8:16],
                                bc_mid(g_rows[:, j, 0:8], TT), ALU.add).then_inc(gdn_y, 1)
        dve.wait_ge(gdn_sp, j + 1)
        step(dve, nc.vector.tensor_scalar(g_beta, g_beta, 1.0, None, ALU.add))
        step(dve, nc.vector.reciprocal(g_beta, g_beta))
        step(dve, nc.vector.scalar_tensor_tensor(out=g_g, in0=g_in, scalar=0.0, in1=g_t1, op0=ALU.max, op1=ALU.add))
        nc.vector.scalar_tensor_tensor(out=g_g.rearrange("p (t h) -> p t h", t=TT),
                                       in0=g_g.rearrange("p (t h) -> p t h", t=TT), scalar=-1.0,
                                       in1=bc_mid(g_A, TT), op0=ALU.mult, op1=ALU.mult).then_inc(gdn_g, 1)
        for t in range(TT):
            dve.wait_ge(gdn_tok, NQKV * (j + 1))
            step(dve, nc.vector.tensor_tensor(g_sq, g_tok[:, t, 0:2 * D], g_tok[:, t, 0:2 * D], ALU.mult))
            nc.vector.tensor_reduce(g_ss[:, 16 * t:16 * t + 16], g_sq.rearrange("p (c d) -> p c d", d=P), AX.X,
                                    ALU.add).then_inc(gdn_ss, 1)
            dve.wait_ge(gdn_ss, 3 * j + t + 1)
        dve.wait_ge(gdn_gcps, j + 1)
        step(dve, nc.vector.tensor_copy(g_gc, ps[:, 7, 64:80]))
        nc.vector.tensor_tensor(g_t2[:, 0:8], ps[:, 7, 80:88], g_gc[:, 0:8], ALU.subtract).then_inc(gdn_gc, 1)
        for t in range(TT):
            dve.wait_ge(gdn_rs, 3 * j + t + 1)
            qk = g_tok[:, t, 0:2 * D].rearrange("p (c d) -> p c d", d=P)
            nc.vector.tensor_tensor(qk, qk, bc_last(g_ss[:, 16 * t:16 * t + 16], P), ALU.mult).then_inc(gdn_n, 1)
        for t in range(TT):
            v = g_tok[:, t, 2 * D:3 * D].rearrange("p (h d) -> p h d", d=P)
            step(dve, nc.vector.tensor_tensor(v, v, bc_last(g_beta[:, 8 * t:8 * t + 8], P), ALU.mult))
        dve.wait_ge(gdn_eg, j + 1)
        step(dve, nc.vector.scalar_tensor_tensor(out=g_nb, in0=g_beta[:, 8:16], scalar=-1.0, in1=g_eg[:, 8:16],
                                                 op0=ALU.mult, op1=ALU.mult))
        dve.wait_ge(gdn_Tps, 8 * j + 4)
        k0 = g_tok[:, 0, D:2 * D].rearrange("p (h d) -> p h d", d=P)
        nc.vector.tensor_tensor(k0, k0, bc_last(g_kd, P), ALU.mult).then_inc(gdn_kd, 1)

        def wide(ap):
            return ap.rearrange("p (h c) -> p h c", c=P)

        for t in range(TT):
            for hg in range(HG):
                cols = slice(8 * t + 4 * hg, 8 * t + 4 * hg + 4)
                dve.wait_ge(gdn_prep, 4 * j + 2 * t + hg + 1)
                if t or j:
                    dve.wait_ge(gdn_C, 28 * j + LEVELS * t * HG)
                step(dve, nc.vector.tensor_tensor(wide(g_W[:, hg, :]), wide(ps[:, 4 + hg, :]),
                                                  bc_last(g_gc[:, cols], P), ALU.subtract))
                step(dve, nc.vector.tensor_scalar(g_QK[:, hg, :], g_W[:, hg, :], 0.0, None, ALU.min))
                nc.vector.tensor_scalar(g_L[:, hg, :], g_W[:, hg, :], 0.0, None, ALU.max).then_inc(gdn_D, 1)
            for hg in range(HG):
                cols = slice(8 * t + 4 * hg, 8 * t + 4 * hg + 4)
                qk, lo = wide(g_QK[:, hg, :]), wide(g_L[:, hg, :])
                dve.wait_ge(gdn_E, 4 * j + 2 * t + hg + 1)
                step(dve, nc.vector.tensor_tensor(qk, qk, bc_mid(col(C_UPPER), 4), ALU.mult))
                step(dve, nc.vector.tensor_tensor(g_QK[:, hg, :], g_QK[:, hg, :], ps[:, 2 + hg, :], ALU.mult))
                step(dve, nc.vector.tensor_tensor(lo, lo, bc_mid(col(C_LOWER), 4), ALU.mult))
                step(dve, nc.vector.tensor_tensor(lo, lo, bc_last(g_beta[:, cols], P), ALU.mult))
                nc.vector.tensor_tensor(g_L[:, hg, :], g_L[:, hg, :], ps[:, hg, :], ALU.mult).then_inc(gdn_L, 1)
            for lv in range(LEVELS):
                for hg in range(HG):
                    Ti, V = g_Ti[:, hg, :], g_V[:, hg, :]
                    if lv == 0:
                        dve.wait_ge(gdn_Wps, 28 * j + LEVELS * t * HG + hg + 1)
                        step(dve, nc.vector.tensor_tensor(wide(Ti), bc_mid(ident, 4), wide(g_C[:, hg, :]),
                                                          ALU.subtract))
                        nc.vector.tensor_tensor(wide(V), bc_mid(ident, 4), wide(ps[:, hg, :]),
                                                ALU.subtract).then_inc(gdn_V, 1)
                    else:
                        dve.wait_ge(gdn_TV, 24 * j + ((LEVELS - 1) * t + lv - 1) * HG + hg + 1)
                        if lv < LEVELS - 1:
                            step(dve, nc.vector.tensor_tensor(Ti, Ti, ps[:, 2 + hg, :], ALU.subtract))
                        nc.vector.tensor_tensor(V, V, ps[:, 4 + hg, :], ALU.subtract).then_inc(gdn_V, 1)
                    dve.wait_ge(gdn_V, 28 * j + (LEVELS * t + lv) * HG + hg + 1)
            for hg in range(HG):
                o = xn[:, t, hg * GW:(hg + 1) * GW]
                if t == 1:
                    dve.wait_ge(gdn_ks, 2 * j + hg + 1)
                    v = wide(g_tok[:, 1, 2 * D + hg * GW:2 * D + (hg + 1) * GW])
                    step(dve, nc.vector.tensor_tensor(wide(g_C[:, hg, :]), wide(ps[:, 2 + hg, :]),
                                                      bc_last(g_nb[:, 4 * hg:4 * hg + 4], P), ALU.mult))
                    nc.vector.tensor_tensor(v, v, wide(g_C[:, hg, :]), ALU.add).then_inc(gdn_r, 1)
                    step(dve, nc.vector.tensor_tensor(wide(o), wide(ps[:, 6 + hg, :]),
                                                      bc_last(g_eg[:, 8 + 4 * hg:12 + 4 * hg], P), ALU.mult))
                dve.wait_ge(gdn_ops, 4 * j + 2 * t + hg + 1)
                if t == 0:
                    ins = nc.vector.tensor_copy(o, ps[:, 4 + hg, :])
                else:
                    ins = nc.vector.tensor_tensor(o, o, ps[:, 4 + hg, :], ALU.add)
                ins.then_inc(gdn_o, 1)
        dve.wait_ge(gdn_o, 4 * (j + 1))
        for t in range(TT):
            step(dve, nc.vector.tensor_tensor(g_sq[:, t * D:(t + 1) * D], xn[:, t, :], xn[:, t, :], ALU.mult))
        nc.vector.tensor_reduce(g_oss, g_sq.rearrange("p (c d) -> p c d", d=P), AX.X, ALU.add).then_inc(gdn_ss, 1)
        dve.wait_ge(gdn_rs, 3 * j + 3)
        for t in range(TT):
            o = wide(xn[:, t, :])
            step(dve, nc.vector.tensor_tensor(o, o, bc_last(g_oss[:, 8 * t:8 * t + 8], P), ALU.mult))
            nc.vector.tensor_tensor(xn[:, t, :], xn[:, t, :], g_z[:, t, :], ALU.mult).then_inc(gdn_on, 1)
        for t in range(TT):
            for h in range(2):
                dve.wait_ge(gdn_oT, 4 * j + 2 * t + h + 1)
                nc.vector.tensor_scalar(hT[:, 4 * h:4 * h + 4, t * P:(t + 1) * P], wide(ps[:, 4 + 2 * t + h, :]),
                                        g_ng[:, j:j + 1], None, ALU.mult).then_inc(mix_in_ready, 1)
        add_to_x(dve, w_out_done(dve, at), x_sb, 1.0)

    def gdn_pool(pool, at):
        j = at["n"]
        norm_pool(pool, at)
        for t in range(TT):
            pool.wait_ge(gdn_ss, 3 * j + t + 1)
            ss = g_ss[:, 16 * t:16 * t + 16]
            pool_steps.done(pool, nc.gpsimd.tensor_scalar(ss[:, 0:8], ss[:, 0:8], float(P), P * EPS, ALU.mult, ALU.add))
            pool_steps.done(pool, nc.gpsimd.tensor_scalar(ss[:, 8:16], ss[:, 8:16], EPS, None, ALU.add))
            nc.gpsimd.tensor_tensor(ss, ss, consts[:, C_NHALF:C_NHALF + 16], ALU.pow).then_inc(gdn_rs, 1)
        for t in range(TT):
            for lv in range(LEVELS):
                for hg in range(HG):
                    pool.wait_ge(gdn_L, 4 * j + 2 * t + hg + 1)
                    if lv == 1:
                        pool.wait_ge(gdn_V, 28 * j + (LEVELS * t + lv - 1) * HG + hg + 1)
                    if lv:
                        pool.wait_ge(gdn_Wps, 28 * j + (LEVELS * t + lv - 1) * HG + hg + 1)
                    nc.gpsimd.tensor_tensor(g_C[:, hg, :].rearrange("p (h c) -> p h c", c=P),
                                            g_L[:, hg, :].rearrange("p (h c) -> p h c", c=P),
                                            bc_mid(col(C_BLOCK + lv * P), 4), ALU.mult).then_inc(gdn_C, 1)
        pool.wait_ge(gdn_ss, 3 * j + 3)
        inv_sqrt(pool, g_oss, g_oss, 1.0 / P, EPS).then_inc(gdn_rs, 1)

    SC = 3 * P
    car = Carve()
    s_qk = car.take(16, T)
    s_v = car.take(TT, D)
    s_t, s_lb, s_lf, s_att = (car.take(3, SC) for _ in range(4))
    sb_qk = sem("sb_qk")
    sb_qks = sem("sb_qks")
    sb_vs = sem("sb_vs")
    sb_z = sem("sb_z")
    sb_t = sem("sb_t")
    sb_lf = sem("sb_lf")
    sb_cum = sem("sb_cum")
    sb_la = sem("sb_la")
    sb_e = sem("sb_e")
    sb_att = sem("sb_att")
    sb_o = sem("sb_o")

    def sb_sp(sp, at):
        w = A["sb_w_in"][at["n"]].rearrange("(k p) c -> p k c", p=P)
        for n in range(4):
            g = at["load"] + n
            wait_slot_free(sp, g)
            for m in range(3):
                c = (3 * n + m) * CH
                sp.dma_start(part(g, m).rearrange("p (k c) -> p k c", k=KD), w[:, :, c:c + CH])\
                    .then_inc(load_done[g % RING], 16)
        w_out_sp(sp, at, 4, A["sb_w_out"][at["n"]])

    def sb_pe(pe, at):
        norm_pe(pe, at)
        pe.wait_ge(hT_ready, 2 * TT * (at["norm"] + 1))
        for q in range(12):
            g = at["load"] + q // 3
            if q % 3 == 0:
                wait_loaded(pe, g)
            w = part(g, q % 3).rearrange("p (k c) -> p k c", k=KD)
            for i in range(2):
                if q < 8:
                    c = 2 * q + i
                    if c >= 4:
                        pe.wait_ge(sb_qks, c - 3)
                    for k in range(KD):
                        ins = nc.tensor.matmul(ps[:, c % 4, 0:T], w[:, k, i * P:(i + 1) * P], hT[:, k, :],
                                               start=(k == 0), stop=(k == KD - 1))
                    ins.then_inc(sb_qk, 1)
                else:
                    for k in range(KD):
                        ins = nc.tensor.matmul(ps[:, 4 + 2 * i + (q - 8) // 2, (q % 2) * CH:(q % 2 + 1) * CH],
                                               hT[:, k, i * P:(i + 1) * P], w[:, k, :],
                                               start=(k == 0), stop=(k == KD - 1))
                    if i == 1 and q in (8, 11):
                        ins.then_inc(load_used, 1)
        pe.wait_ge(sb_qks, 16)
        for i in range(GH + 2):
            if i < GH:
                if i >= 2:
                    pe.wait_ge(sb_lf, i - 1)
                nc.tensor.matmul(ps[:, i % 2, 0:T], s_qk[:, GH + i, 0:P], s_qk[:, i, :], start=True, stop=True)
                nc.tensor.matmul(ps[:, i % 2, T:SC], s_qk[:, GH + i, P:T], s_qk[:, i, P:T],
                                 start=True, stop=True).then_inc(sb_z, 1)
            if 1 <= i <= GH:
                h = i - 1
                lf, bank = s_lf[:, h % 3, :], ps[:, 2 + h % 2, :]
                pe.wait_ge(sb_lf, h + 1)
                if h >= 2:
                    pe.wait_ge(sb_la, h - 1)
                nc.tensor.matmul(bank[:, T:SC], col(C_LOWER), lf[:, T:SC], start=True, stop=True)
                nc.tensor.matmul(bank[:, 0:T], col(C_LOWER), lf[:, 0:T], start=True, stop=False)
                nc.tensor.matmul(bank[:, P:T], col(C_ONES), lf[:, T:SC], start=False, stop=True)\
                    .then_inc(sb_cum, 1)
            if i >= 2:
                h = i - 2
                att, bank = s_att[:, h % 3, :], ps[:, 4 + h % 2, :]
                pe.wait_ge(sb_att, h + 1)
                pe.wait_ge(sb_vs, 4)
                if h >= 2:
                    pe.wait_ge(mix_in_ready, mix_in_before(at) + h - 1)
                v = [s_v[:, t, h * P:(h + 1) * P] for t in range(TT)]
                nc.tensor.matmul(bank[:, 0:T], v[0], att[:, 0:T], start=True, stop=False)
                nc.tensor.matmul(bank[:, P:T], v[1], att[:, T:SC], start=False, stop=True).then_inc(sb_o, 1)
        w_out_pe(pe, at, 4, hT)

    def sb_act(act, at):
        norm_act(act, at)
        for c in range(16):
            act.wait_ge(sb_qk, c + 1)
            nc.scalar.activation(s_qk[:, c, :], ps[:, c % 4, 0:T], ACT.Copy,
                                 scale=float(P) ** -0.5 if c < GH else 1.0).then_inc(sb_qks, 1)
        for i in range(GH + 3):
            if i < GH:
                t = s_t[:, i % 3, :]
                act.wait_ge(sb_z, i + 1)
                if i >= 3:
                    act.wait_ge(sb_lf, i - 2)
                act_steps.done(act, nc.scalar.activation(t, ps[:, i % 2, 0:SC], ACT.Abs))
                act_steps.done(act, nc.scalar.activation(t, t, ACT.Exp, scale=-1.0))
                nc.scalar.activation(t, t, ACT.Ln, bias=1.0).then_inc(sb_t, 1)
            if 1 <= i <= GH:
                h = i - 1
                act.wait_ge(sb_la, h + 1)
                nc.scalar.activation(s_att[:, h % 3, :], s_att[:, h % 3, :], ACT.Exp).then_inc(sb_e, 1)
            if i >= 3:
                h = i - 3
                act.wait_ge(sb_o, h + 1)
                nc.scalar.activation(hT[:, h, :], ps[:, 4 + h % 2, 0:T], ACT.Copy).then_inc(mix_in_ready, 1)

    def sb_dve(dve, at):
        norm_dve(dve, at, gain[:, :, 4 + at["layer"]])
        dve.wait_ge(load_used, at["mixer_load"] + 2)
        for b in range(4):
            nc.vector.tensor_copy(s_v[:, b // 2, (b % 2) * PB:(b % 2 + 1) * PB], ps[:, 4 + b, :])\
                .then_inc(sb_vs, 1)
        mask = col(C_SB, SC)
        for i in range(GH + 2):
            if i < GH:
                z, t = ps[:, i % 2, 0:SC], s_t[:, i % 3, :]
                lf, lb = s_lf[:, i % 3, :], s_lb[:, i % 3, :]
                dve.wait_ge(sb_t, i + 1)
                if i >= 3:
                    dve.wait_ge(sb_cum, i - 2)
                dve_steps.done(dve, nc.vector.scalar_tensor_tensor(out=lf, in0=z, scalar=0.0, in1=t,
                                                                   op0=ALU.max, op1=ALU.add))
                dve_steps.done(dve, nc.vector.scalar_tensor_tensor(out=lf, in0=lf, scalar=-1.0, in1=mask,
                                                                   op0=ALU.mult, op1=ALU.mult))
                nc.vector.scalar_tensor_tensor(out=lb, in0=z, scalar=0.0, in1=t,
                                               op0=ALU.min, op1=ALU.subtract).then_inc(sb_lf, 1)
            if 1 <= i <= GH:
                h = i - 1
                dve.wait_ge(sb_cum, h + 1)
                dve.wait_ge(sb_lf, h + 1)
                if h >= 3:
                    dve.wait_ge(sb_o, h - 2)
                nc.vector.tensor_tensor(s_att[:, h % 3, :], ps[:, 2 + h % 2, 0:SC], s_lb[:, h % 3, :],
                                        ALU.add).then_inc(sb_la, 1)
            if i >= 2:
                h = i - 2
                att = s_att[:, h % 3, :]
                dve.wait_ge(sb_e, h + 1)
                nc.vector.tensor_tensor(att, att, mask, ALU.mult).then_inc(sb_att, 1)
        add_to_x(dve, w_out_done(dve, at), x_sb, 1.0)

    QR, KVR, RD, IDX, IH = 384, 256, 32, 64, 8
    DIN, NOPE, TOPK = QR + KVR + RD + IDX + IH, P - RD, 64
    NEG, TAKEN = -1e30, -3e38
    O_KV, O_R, O_I, O_W = QR, QR + KVR, QR + KVR + RD, QR + KVR + RD + IDX
    car = Carve()
    d_p = car.take(TT, DIN)
    d_k = car.take(TT, P)
    d_cT = car.take(5, T)
    d_kT0 = car.take(T)
    d_q = car.take(TT, D)
    d_qT = car.take(GH, T)
    d_kT = car.take(GH, T)
    d_v = car.take(TT, D)
    d_qi = car.take(TT, IH * IDX)
    d_qiT = car.take(IH, T)
    d_sel = car.take(SC)
    d_score = car.take(SC)
    car = Carve()
    d_s = car.take(3, SC)
    d_pT = car.take(3, SC)
    car = Carve()
    car.take(TT * DIN + TT * P + 6 * T)
    d_relu = car.take(2, 2 * T)
    d_tmp = aT[:, :, :].rearrange("p a b -> p (a b)")
    d_small = sb("d_small", [P, 64])
    d_ss = d_small[:, 0:6]
    d_m8 = d_small[:, 8:16]
    d_w = d_small[:, 16:32]
    d_nm = d_small[:, 32:38]
    d_sum = d_small[:, 40:46]
    d_rec = d_small[:, 48:54]
    d_gk = sb("d_gk", [P, IDX])
    dsa_p = sem("dsa_p")
    dsa_ps = sem("dsa_ps")
    dsa_ss = sem("dsa_ss")
    dsa_rs = sem("dsa_rs")
    dsa_c = sem("dsa_c")
    dsa_cps = sem("dsa_cps")
    dsa_cT = sem("dsa_cT")
    dsa_q = sem("dsa_q")
    dsa_qs = sem("dsa_qs")
    dsa_qa = sem("dsa_qa")
    dsa_kps = sem("dsa_kps")
    dsa_ks = sem("dsa_ks")
    dsa_kr = sem("dsa_kr")
    dsa_v = sem("dsa_v")
    dsa_vs = sem("dsa_vs")
    dsa_qTps = sem("dsa_qTps")
    dsa_qT = sem("dsa_qT")
    dsa_log = sem("dsa_log")
    dsa_relu = sem("dsa_relu")
    dsa_sc = sem("dsa_sc")
    dsa_z = sem("dsa_z")
    dsa_m = sem("dsa_m")
    dsa_e = sem("dsa_e")
    dsa_pr = sem("dsa_pr")
    dsa_pt = sem("dsa_pt")
    dsa_pts = sem("dsa_pts")
    dsa_o = sem("dsa_o")

    def dsa_sp(sp, at):
        j = at["n"]

        def go(g, off, src, sem_by):
            v = src.rearrange("(k p) c -> p k c", p=P)
            n = v.shape[1] * v.shape[2]
            sp.dma_start(slot(g)[:, off:off + n].rearrange("p (k c) -> p k c", k=v.shape[1]), v)\
                .then_inc(load_done[g % RING], sem_by)

        g = at["load"]
        wait_slot_free(sp, g)
        go(g, 0, A["dsa_w_in"][j], 48)
        wait_slot_free(sp, g + 1)
        go(g + 1, 0, A["dsa_w_uq"][j], 32)
        go(g + 1, 3 * D, A["dsa_w_qidx"][j], 16)
        wait_slot_free(sp, g + 2)
        go(g + 2, 0, A["dsa_w_uk"][j], 32)
        go(g + 2, 2 * D, A["dsa_w_uv"][j], 16)
        w_out_sp(sp, at, 3, A["dsa_w_out"][j])

    def dsa_pe(pe, at):
        norm_pe(pe, at)
        pe.wait_ge(hT_ready, 2 * TT * (at["norm"] + 1))
        g = at["load"]
        wait_loaded(pe, g)
        w = slot(g)[:, 0:KD * DIN].rearrange("p (k c) -> p k c", k=KD)
        for t in range(TT):
            for bank, cols in ((2 * t, slice(0, O_KV)), (2 * t + 1, slice(O_KV, DIN))):
                for k in range(KD):
                    ins = nc.tensor.matmul(ps[:, bank, 0:cols.stop - cols.start], hT[:, k, t * P:(t + 1) * P],
                                           w[:, k, cols], start=(k == 0), stop=(k == KD - 1))
            ins.then_inc(dsa_p if t == 0 else load_used, 1)
        pe.wait_ge(dsa_c, 1)
        for n in range(6):
            src = d_p[:, :, n * P:(n + 1) * P] if n < 5 else d_k[:, :, :]
            for t in range(TT):
                ins = nc.tensor.transpose(ps[:, 4 + n // 2, (n % 2) * T + t * P:(n % 2) * T + (t + 1) * P],
                                          src[:, t, :], ident)
        ins.then_inc(dsa_cps, 1)
        pe.wait_ge(dsa_cT, 1)
        wait_loaded(pe, g + 1)
        wq = slot(g + 1)[:, 0:3 * D].rearrange("p (k c) -> p k c", k=3)
        wi = slot(g + 1)[:, 3 * D:3 * D + 3 * PB].rearrange("p (k c) -> p k c", k=3)
        for t in range(TT):
            for bank, src in ((2 * t, wq[:, :, 0:PB]), (2 * t + 1, wq[:, :, PB:D]), (4 + t, wi)):
                for k in range(3):
                    ins = nc.tensor.matmul(ps[:, bank, :], d_cT[:, k, t * P:(t + 1) * P], src[:, k, :],
                                           start=(k == 0), stop=(k == 2))
            ins.then_inc(dsa_q if t == 0 else load_used, 1)
        wait_loaded(pe, g + 2)
        wk = slot(g + 2)[:, 0:2 * GH * NOPE].rearrange("p (k c) -> p k c", k=2)
        wv = slot(g + 2)[:, 2 * D:4 * D].rearrange("p (k c) -> p k c", k=2)
        for n in range(4):
            if n >= 2:
                pe.wait_ge(dsa_ks, n - 1)
            for i in range(2):
                h = 2 * n + i
                for k in range(2):
                    ins = nc.tensor.matmul(ps[0:NOPE, 6 + n % 2, i * T:(i + 1) * T],
                                           wk[:, k, h * NOPE:(h + 1) * NOPE], d_cT[:, 3 + k, :],
                                           start=(k == 0), stop=(k == 1))
            ins.then_inc(dsa_kps, 1)
        for n in range(4):
            pe.wait_ge(dsa_ks, 3 + n % 2)
            if n >= 2:
                pe.wait_ge(dsa_vs, n - 1)
            for k in range(2):
                ins = nc.tensor.matmul(ps[:, 6 + n % 2, :], d_cT[:, 3 + k, (n // 2) * P:(n // 2 + 1) * P],
                                       wv[:, k, (n % 2) * PB:(n % 2 + 1) * PB], start=(k == 0), stop=(k == 1))
            ins.then_inc(dsa_v if n < 3 else load_used, 1)
        for t in range(TT):
            pe.wait_ge(dsa_qs, t + 1)
            pe.wait_ge(dsa_qa, t + 1)
        for n in range(8):
            t, half = n // 2 % 2, n % 2
            if n >= 4:
                pe.wait_ge(dsa_qT, n - 3)
            for c in range(4):
                h = 4 * half + c
                if n < 4:
                    ins = nc.tensor.transpose(ps[0:IDX, n % 4, c * P:(c + 1) * P],
                                              d_qi[:, t, h * IDX:(h + 1) * IDX], ident)
                else:
                    ins = nc.tensor.transpose(ps[:, n % 4, c * P:(c + 1) * P], d_q[:, t, h * P:(h + 1) * P], ident)
            ins.then_inc(dsa_qTps, 1)
        pe.wait_ge(dsa_qT, 4)
        for n in range(8):
            t = n // 4
            if n >= 2:
                pe.wait_ge(dsa_relu, n - 1)
            for i in range(2):
                h = 2 * (n % 4) + i
                ins = nc.tensor.matmul(ps[:, 4 + n % 2, i * T:i * T + (t + 1) * P],
                                       d_qiT[0:IDX, h, t * P:(t + 1) * P], d_kT0[0:IDX, 0:(t + 1) * P],
                                       start=True, stop=True)
            ins.then_inc(dsa_log, 1)
        pe.wait_ge(dsa_qT, 8)
        pe.wait_ge(dsa_relu, 8)
        pe.wait_ge(dsa_kr, 1)
        pe.wait_ge(dsa_vs, 4)
        for i in range(GH + 2):
            if i < GH:
                if i >= 2:
                    pe.wait_ge(dsa_m, i - 1)
                nc.tensor.matmul(ps[:, i % 2, 0:P], d_qT[:, i, 0:P], d_kT[:, i, 0:P], start=True, stop=True)
                nc.tensor.matmul(ps[:, i % 2, P:SC], d_qT[:, i, P:T], d_kT[:, i, :], start=True, stop=True)\
                    .then_inc(dsa_z, 1)
            if 1 <= i <= GH:
                h = i - 1
                pe.wait_ge(dsa_pr, h + 1)
                if h >= 2:
                    pe.wait_ge(dsa_pts, h - 1)
                for c in range(3):
                    ins = nc.tensor.transpose(ps[:, 2 + h % 2, c * P:(c + 1) * P],
                                              d_s[:, h % 3, c * P:(c + 1) * P], ident)
                ins.then_inc(dsa_pt, 1)
            if i >= 2:
                h = i - 2
                bank, pT = ps[:, 4 + h % 2, :], d_pT[:, h % 3, :]
                pe.wait_ge(dsa_pts, h + 1)
                if h >= 2:
                    pe.wait_ge(mix_in_ready, mix_in_before(at) + h - 1)
                v = [d_v[:, t, h * P:(h + 1) * P] for t in range(TT)]
                nc.tensor.matmul(bank[:, 0:T], v[0], pT[:, 0:T], start=True, stop=False)
                nc.tensor.matmul(bank[:, P:T], v[1], pT[:, T:SC], start=False, stop=True).then_inc(dsa_o, 1)
        w_out_pe(pe, at, 3, hT)

    def dsa_act(act, at):
        norm_act(act, at)
        for t in range(TT):
            if t == 0:
                act.wait_ge(dsa_p, 1)
            else:
                act.wait_ge(load_used, at["mixer_load"] + 1)
            nc.scalar.activation(d_p[:, t, 0:O_KV], ps[:, 2 * t, 0:O_KV], ACT.Copy)
            nc.scalar.activation(d_p[:, t, O_KV:DIN], ps[:, 2 * t + 1, 0:DIN - O_KV], ACT.Copy).then_inc(dsa_ps, 1)
            for s, (bank, cols) in enumerate(((2 * t, slice(0, QR)), (2 * t + 1, slice(0, KVR)),
                                              (2 * t + 1, slice(KVR + RD, KVR + RD + IDX)))):
                ins = nc.scalar.activation(silu[:, 0:2, :].rearrange("p a b -> p (a b)")[:, 0:cols.stop - cols.start],
                                           ps[:, bank, cols], ACT.Square,
                                           accum_out=d_ss[:, 2 * s + t:2 * s + t + 1])
                if s < 2:
                    act_steps.done(act, ins)
            ins.then_inc(dsa_ss, 1)
            act.wait_ge(dsa_ss, t + 1)
        for t in range(TT):
            act.wait_ge(dsa_qs, t + 1)
            for half in range(2):
                nc.scalar.activation(
                    d_q[:, t, half * PB:(half + 1) * PB].rearrange("p (h c) -> p h c", c=P)[:, :, 0:NOPE],
                    ps[:, 2 * t + half, :].rearrange("p (h c) -> p h c", c=P)[:, :, RD:P], ACT.Copy)
            nc.scalar.activation(d_qi[:, t, :].rearrange("p (h c) -> p h c", c=IDX)[:, :, 16:IDX],
                                 ps[:, 4 + t, :].rearrange("p (h c) -> p h c", c=IDX)[:, :, 16:IDX], ACT.Copy)\
                .then_inc(dsa_qa, 1)
        for n in range(4):
            act.wait_ge(dsa_kps, n + 1)
            nc.scalar.activation(d_kT[0:NOPE, 2 * n:2 * n + 2, :],
                                 ps[0:NOPE, 6 + n % 2, :].rearrange("p (h c) -> p h c", c=T), ACT.Copy)\
                .then_inc(dsa_ks, 1)
        for n in range(4):
            if n < 3:
                act.wait_ge(dsa_v, n + 1)
            else:
                act.wait_ge(load_used, at["mixer_load"] + 3)
            nc.scalar.activation(d_v[:, n // 2, (n % 2) * PB:(n % 2 + 1) * PB], ps[:, 6 + n % 2, :], ACT.Copy)\
                .then_inc(dsa_vs, 1)
        for n in range(8):
            t, half = n // 2 % 2, n % 2
            act.wait_ge(dsa_qTps, n + 1)
            rows, dst = (IDX, d_qiT) if n < 4 else (P, d_qT)
            nc.scalar.activation(dst[0:rows, 4 * half:4 * half + 4, t * P:(t + 1) * P],
                                 ps[0:rows, n % 4, :].rearrange("p (h c) -> p h c", c=P), ACT.Copy,
                                 scale=1.0 if n < 4 else float(P) ** -0.5).then_inc(dsa_qT, 1)
        for n in range(8):
            t = n // 4
            act.wait_ge(dsa_log, n + 1)
            if n >= 2:
                act.wait_ge(dsa_sc, n - 1)
            elif n == 0:
                act.wait_ge(dsa_qTps, 8)
            nc.scalar.activation(d_relu[:, n % 2, :].rearrange("p (i c) -> p i c", i=2)[:, :, 0:(t + 1) * P],
                                 ps[:, 4 + n % 2, :].rearrange("p (i c) -> p i c", i=2)[:, :, 0:(t + 1) * P],
                                 ACT.Relu).then_inc(dsa_relu, 1)
        for i in range(GH + 2):
            if i < GH:
                act.wait_ge(dsa_m, i + 1)
                for t, cols in ((0, slice(0, P)), (1, slice(P, SC))):
                    n = 2 * (i % 3) + t
                    s = d_s[:, i % 3, cols]
                    ins = nc.scalar.activation(s, s, ACT.Exp, bias=d_nm[:, n:n + 1], accum_out=d_sum[:, n:n + 1])
                ins.then_inc(dsa_e, 1)
            if i >= 2:
                h = i - 2
                act.wait_ge(dsa_o, h + 1)
                nc.scalar.activation(hT[:, h, :], ps[:, 4 + h % 2, 0:T], ACT.Copy).then_inc(mix_in_ready, 1)

    def rotate(dve, step, dst1, dst2, src1, src2, cos, sin, tmp, last):
        n, half = src1.shape[1], src1.shape[2]
        t = [tmp[:, i * n * half:(i + 1) * n * half].rearrange("p (n c) -> p n c", n=n) for i in range(4)]
        c, s = bc_mid(cos, n), bc_mid(sin, n)
        nc.vector.tensor_tensor(t[0], src1, c, ALU.mult)
        nc.vector.tensor_tensor(t[1], src2, s, ALU.mult)
        nc.vector.tensor_tensor(t[2], src2, c, ALU.mult)
        step(dve, nc.vector.tensor_tensor(t[3], src1, s, ALU.mult))
        step(dve, nc.vector.tensor_tensor(dst1, t[0], t[1], ALU.subtract))
        last(nc.vector.tensor_tensor(dst2, t[2], t[3], ALU.add))

    def dsa_dve(dve, at):
        norm_dve(dve, at, gain[:, :, 4 + at["layer"]])
        step = dve_steps.done

        def fin(ins):
            step(dve, ins)

        step(dve, nc.vector.memset(d_k, 0.0))
        dve.wait_ge(rows_loaded, ROWS_DMAS)
        dve.wait_ge(dsa_rs, 1)
        for t in range(TT):
            for s, (a, b) in enumerate(((0, QR), (O_KV, O_KV + KVR), (O_I, O_I + IDX))):
                v = d_p[:, t, a:b]
                step(dve, nc.vector.tensor_scalar(v, v, d_ss[:, 2 * s + t:2 * s + t + 1], None, ALU.mult))
            step(dve, nc.vector.tensor_tensor(d_k[:, t, 0:IDX], d_p[:, t, O_I:O_I + IDX], d_gk[:, :], ALU.mult))
            k = d_k[:, t, :][:, None, :]
            rotate(dve, step, k[:, :, 0:8], k[:, :, 8:16], k[:, :, 0:8], k[:, :, 8:16],
                   col(C_ROPE8 + 16 * t, 8), col(C_ROPE8 + 16 * t + 8, 8), d_tmp, fin)
            r = d_p[:, t, O_R:O_R + RD][:, None, :]
            rotate(dve, step, k[:, :, NOPE:NOPE + 16], k[:, :, NOPE + 16:P], r[:, :, 0:16], r[:, :, 16:32],
                   col(C_ROPE16 + 32 * t, 16), col(C_ROPE16 + 32 * t + 16, 16), d_tmp, fin)
            step(dve, nc.vector.tensor_scalar(d_w[:, 8 * t:8 * t + 8], d_p[:, t, O_W:O_W + IH],
                                              float(IH * IDX) ** -0.5, None, ALU.mult))
        nc.vector.tensor_scalar(d_w, d_w, 1.0, None, ALU.mult).then_inc(dsa_c, 1)
        dve.wait_ge(dsa_cps, 1)
        for n in range(5):
            g_col = 102 + n
            nc.vector.tensor_scalar(d_cT[:, n, :], ps[:, 4 + n // 2, (n % 2) * T:(n % 2 + 1) * T],
                                    cols_T[:, 0, g_col:g_col + 1], None, ALU.mult)
        nc.vector.tensor_copy(d_kT0, ps[:, 6, T:2 * T]).then_inc(dsa_cT, 1)
        for t in range(TT):
            if t == 0:
                dve.wait_ge(dsa_q, 1)
            else:
                dve.wait_ge(load_used, at["mixer_load"] + 2)
            for half in range(2):
                q = ps[:, 2 * t + half, :].rearrange("p (h c) -> p h c", c=P)
                dst = d_q[:, t, half * PB:(half + 1) * PB].rearrange("p (h c) -> p h c", c=P)
                rotate(dve, step, dst[:, :, NOPE:NOPE + 16], dst[:, :, NOPE + 16:P], q[:, :, 0:16], q[:, :, 16:32],
                       col(C_ROPE16 + 32 * t, 16), col(C_ROPE16 + 32 * t + 16, 16), d_tmp, fin)
            qi = ps[:, 4 + t, :].rearrange("p (h c) -> p h c", c=IDX)
            dst = d_qi[:, t, :].rearrange("p (h c) -> p h c", c=IDX)
            rotate(dve, step, dst[:, :, 0:8], dst[:, :, 8:16], qi[:, :, 0:8], qi[:, :, 8:16],
                   col(C_ROPE8 + 16 * t, 8), col(C_ROPE8 + 16 * t + 8, 8), d_tmp,
                   lambda ins: ins.then_inc(dsa_qs, 1))
            dve.wait_ge(dsa_qs, t + 1)
        for n in range(8):
            t = n // 4
            acc = d_score[:, 0:P] if t == 0 else d_score[:, P:SC]
            dve.wait_ge(dsa_relu, n + 1)
            for i in range(2):
                h = 2 * (n % 4) + i
                w = d_w[:, 8 * t + h:8 * t + h + 1]
                r = d_relu[:, n % 2, i * T:i * T + (t + 1) * P]
                if h == 0:
                    step(dve, nc.vector.tensor_scalar(acc, r, w, None, ALU.mult))
                else:
                    ins = nc.vector.scalar_tensor_tensor(out=acc, in0=r, scalar=w, in1=acc,
                                                         op0=ALU.mult, op1=ALU.add)
                    if i == 0:
                        step(dve, ins)
            ins.then_inc(dsa_sc, 1)
            dve.wait_ge(dsa_sc, n + 1)
        step(dve, nc.vector.tensor_tensor(d_score, d_score, col(C_CNEG, SC), ALU.add))
        for cols in (slice(0, P), slice(P, SC)):
            s = d_score[:, cols]
            for _ in range(TOPK // 8):
                step(dve, nc.vector.max(d_m8, s))
                step(dve, nc.vector.match_replace(out=s, in_to_replace=d_m8, in_values=s, imm_value=TAKEN))
        step(dve, nc.vector.tensor_scalar(d_sel, d_score, 0.5 * TAKEN, NEG, ALU.is_gt, ALU.mult))
        step(dve, nc.vector.tensor_tensor(d_sel, d_sel, col(C_CNEG, SC), ALU.add))
        for i in range(GH + 2):
            if i < GH:
                s = d_s[:, i % 3, :]
                dve.wait_ge(dsa_z, i + 1)
                if i >= 3:
                    dve.wait_ge(dsa_pt, i - 2)
                step(dve, nc.vector.tensor_tensor(s, ps[:, i % 2, 0:SC], d_sel, ALU.add))
                n = 2 * (i % 3)
                nc.vector.tensor_reduce(d_nm[:, n:n + 1], s[:, 0:P], AX.X, ALU.max, negate=True)
                nc.vector.tensor_reduce(d_nm[:, n + 1:n + 2], s[:, P:SC], AX.X, ALU.max, negate=True)\
                    .then_inc(dsa_m, 1)
            if 1 <= i <= GH:
                h = i - 1
                n = 2 * (h % 3)
                dve.wait_ge(dsa_e, h + 1)
                step(dve, nc.vector.reciprocal(d_rec[:, n:n + 2], d_sum[:, n:n + 2]))
                for t, cols in ((0, slice(0, P)), (1, slice(P, SC))):
                    s = d_s[:, h % 3, cols]
                    ins = nc.vector.tensor_scalar(s, s, d_rec[:, n + t:n + t + 1], None, ALU.mult)
                ins.then_inc(dsa_pr, 1)
            if i >= 1 and i - 1 < GH:
                h = i - 1
                dve.wait_ge(dsa_pt, h + 1)
                if h >= 3:
                    dve.wait_ge(dsa_o, h - 2)
                nc.vector.tensor_copy(d_pT[:, h % 3, :], ps[:, 2 + h % 2, 0:SC]).then_inc(dsa_pts, 1)
        add_to_x(dve, w_out_done(dve, at), x_sb, 1.0)

    def dsa_pool(pool, at):
        norm_pool(pool, at)
        pool.wait_ge(dsa_ss, TT)
        for s, n in enumerate((QR, KVR, IDX)):
            v = d_ss[:, 2 * s:2 * s + 2]
            pool_steps.done(pool, nc.gpsimd.tensor_scalar(v, v, 1.0 / n, EPS, ALU.mult, ALU.add))
        nc.gpsimd.tensor_tensor(d_ss, d_ss, consts[:, C_NHALF:C_NHALF + 6], ALU.pow).then_inc(dsa_rs, 1)
        pool.wait_ge(dsa_cT, 1)
        nc.gpsimd.tensor_copy(d_kT[NOPE:P, :, :], d_kT0[NOPE:P, None, :].to_broadcast([RD, GH, T]))\
            .then_inc(dsa_kr, 1)

    NMOD = 9 * KD
    MT = 2 * NMOD // 8
    MTI = MT // ITERS
    M_STEPS = 4
    M_TURN = [(0, 0, 6, 2, 2, 0), (1, 0, 9, 3, 1, 15), (0, 1, 6, 2, 2, 1), (1, 1, 9, 3, 1, 16),
              (0, 48, 3, 1, 1, 12), (1, 2, 9, 3, 1, 17)]
    M_BEFORE = [M_STEPS * sum(t[4] for t in M_TURN[:n]) for n in range(MTI + 1)]
    M_ALL = M_BEFORE[MTI]
    x_ctx = arena[:, 0:TT * D].rearrange("p (t d) -> p t d", t=TT)
    f_row = sb("f_row", [P, D])
    m_w = x_ctx
    m_rows = arena[:, TT * D:TT * D + 2 * P].rearrange("p (l c) -> p l c", l=2)
    m_s = sb("m_s", [P, KD, 2])
    mod = sb("mod", [P, 2, NMOD, 2])
    amp = sb("amp", [P, 8, KD])
    gate_row = sb("gate_row", [P, D])
    m_p = hT[:, 0:KD // 2, :].rearrange("p k t -> p (k t)")
    m_acc = gate_row[:, 0:4 * P].rearrange("p (s c k) -> p s c k", s=2, c=2)
    m_loaded = [sem(f"m_loaded{i}") for i in range(2)]
    m_step = sem("m_step")
    m_sum = sem("m_sum")
    ctx_loaded = sem("ctx_loaded")
    mod_ready = sem("mod_ready")
    ctx_ready = sem("ctx_ready")
    gate_ps = sem("gate_ps")
    gate_ready = sem("gate_ready")
    fin_ss = sem("fin_ss")
    fin_rs = sem("fin_rs")

    GATES = {("ffn", 8): (0, 0, 1, 0.5), ("ffn", 9): (0, 0, 0, 0.5), ("even", 0): (0, 1, 0, 1.0),
             ("ffn", 10): (0, 2, 0, 0.5), ("ffn", 11): (1, 0, 0, 0.5), ("sgu", 0): (1, 1, 0, 1.0),
             ("ffn", 12): (1, 2, 0, 0.5)}

    def gate_use(at):
        return list(GATES).index((at["kind"], at["n"]))

    def mod_cols(layer, vector, cond):
        return mod[:, layer, vector * KD:(vector + 1) * KD, cond]

    def gate_pe(pe, at):
        layer, j, cond, _ = GATES[at["kind"], at["n"]]
        for k in range(KD):
            c = mod_cols(layer, 3 * j + 2, cond)[:, k:k + 1]
            ins = nc.tensor.matmul(ps[:, k // 4, (k % 4) * P:(k % 4 + 1) * P], c.to_broadcast([P, P]), ident,
                                   start=True, stop=True)
        ins.then_inc(gate_ps, 1)
        pe.wait_ge(gate_ready, gate_use(at) + 1)

    def gate_act(act, at):
        n = gate_use(at)
        act.wait_ge(gate_ps, n + 1)
        nc.scalar.activation(gate_row[:, :], ps[:, 0:2, :].rearrange("p a b -> p (a b)"), ACT.Copy,
                             scale=GATES[at["kind"], at["n"]][3]).then_inc(gate_ready, 1)

    def mod_pool(pool, at):
        steps0 = M_ALL * ITERS * at["ffn"]
        f0 = MT * at["ffn"]

        def load(turn, n, it=None):
            layer, tile, per_ffn, per_turn, _, _ = M_TURN[n]
            first = tile + per_ffn * at["ffn"] + per_turn * turn
            q = first if it is None else it * per_turn + first
            w = A["w_mod_2"][layer].rearrange("(k p) (q c) -> q p k c", p=P, c=P)
            pool.dma_start(m_w[:, n % 2, :].rearrange("p (k c) -> p k c", k=KD),
                           w[bass.ds(q, 1)].rearrange("a p k c -> p (a k) c")).then_inc(m_loaded[n % 2], 16)

        def tile(turn, n, it=None):
            before = f0 + MTI * turn + n
            pool.wait_ge(m_loaded[n % 2], count(8 * (before - n % 2) + 16, it, 8 * MTI))
            pool.wait_ge(m_sum, count(before + 1, it, MTI))
            at_step = steps0 + M_ALL * turn + M_BEFORE[n]
            for c in reversed(range(M_TURN[n][4])):
                w_t, to = m_w[:, n % 2, :], m_p if c else m_w[:, n % 2, :]
                half = KD * P
                ins = nc.gpsimd.tensor_tensor(to.rearrange("p (k c) -> p k c", k=KD),
                                              w_t.rearrange("p (k c) -> p k c", k=KD), bc_last(m_s[:, :, c], P),
                                              ALU.mult)
                for step in range(M_STEPS):
                    ins.then_inc(m_step, 1)
                    at_step += 1
                    if step < M_STEPS - 1:
                        pool.wait_ge(m_step, count(at_step, it, M_ALL))
                        half //= 2
                        dst = to[:, 0:half] if half > P else m_acc[:, n % 2, c, :]
                        ins = nc.gpsimd.tensor_tensor(dst, to[:, 0:half], to[:, half:2 * half], ALU.add)
            if turn < ITERS - 1 or n + 2 < MTI:
                pool.wait_ge(m_step, count(at_step, it, M_ALL))
                load(turn + (n + 2) // MTI, (n + 2) % MTI, it)

        if at["update"]:
            pool.wait_ge(x_ready, TT * at["update"])
        elif at["ffn"] == 0:
            pool.wait_ge(gains_ready, 6)
        pool.wait_ge(h_split, 2 * TT * (at["ffn"] + 1))
        for n in range(2):
            load(0, n)
        with pool.Fori(0, ITERS - 1) as it:
            for n in range(MTI):
                tile(0, n, it)
        for n in range(MTI):
            tile(ITERS - 1, n)

    def mod_pe(pe, at, n, it):
        _, _, _, per_turn, conds, first = M_TURN[n]
        pe.wait_ge(m_step, count(M_ALL * ITERS * at["ffn"] + M_BEFORE[n + 1], it, M_ALL))
        for c in range(conds):
            ins = nc.tensor.matmul(ps[:, 7, bass.ds(it * per_turn + (first + 6 * c), 1)], m_acc[:, n % 2, c, :],
                                   col(C_ONES, 1), start=True, stop=True)
        ins.then_inc(m_sum, 1)

    def mod_dve(dve, at):
        f = at["ffn"]
        dve.wait_ge(m_sum, 2 + MT * (f + 1))
        add_columns(mod[:, 0, 6 * f:6 * f + 6, :], ps[:, 7, 0:12].rearrange("p (c n) -> p n c", c=2))
        add_columns(mod[:, 0, 48 + 3 * f:51 + 3 * f, 0], ps[:, 7, 12:15])
        dve_steps.done(dve, add_columns(mod[:, 1, 9 * f:9 * f + 9, 0], ps[:, 7, 15:24]))

        if f == 7:
            for n in range(8):
                l, j, cond = (n // 3, n % 3, 0) if n < 6 else (0, n - 6, 1)
                ins = nc.vector.scalar_tensor_tensor(out=amp[:, n, :], in0=mod_cols(l, 3 * j + 1, cond), scalar=1.0,
                                                     in1=gain[:, :, 12 + 3 * l + j], op0=ALU.add, op1=ALU.mult)
            ins.then_inc(mod_ready, 1)
            dve.wait_ge(mod_ready, 1)

    def add_columns(to, columns):
        return nc.vector.tensor_tensor(to, to, columns, ALU.add)

    def ctx_sp(sp, at):
        sp.wait_ge(m_sum, 2 + 8 * MT)
        sp.dma_start(x_ctx, A["ctx_2"][0].rearrange("(t p) d -> p t d", p=P)).then_inc(ctx_loaded, 16)

    def ctx_pe(pe, at):
        pe.wait_ge(mod_ready, 1)

    def final_sp(sp, at):
        if at["n"]:
            for t in range(TT):
                sp.wait_ge(x_ready, TT * at["update"] + t + 1)
                sp.dma_start(out[0, t * P:(t + 1) * P, :], x_sb[:, t, :]).then_inc(out_done, 16)

    def final_act(act, at):
        for t in range(TT):
            act.wait_ge(x_ready, TT * (at["update"] - 1) + t + 1)
            nc.scalar.activation(xn[:, t, :], x_sb[:, t, :], ACT.Square, accum_out=sumsq[:, t:t + 1])\
                .then_inc(fin_ss, 1)

    def final_pool(pool, at):
        for t in range(TT):
            pool.wait_ge(fin_ss, TT * at["n"] + t + 1)
            inv_sqrt(pool, rstd[:, t:t + 1], sumsq[:, t:t + 1], 1.0 / D, EPS).then_inc(fin_rs, 1)

    def final_dve(dve, at):
        dve.wait_ge(*((x_loaded, 32) if at["n"] else (rows_loaded, ROWS_DMAS)))
        for t in range(TT):
            dve.wait_ge(fin_rs, TT * at["n"] + t + 1)
            nc.vector.scalar_tensor_tensor(out=x_sb[:, t, :], in0=x_sb[:, t, :], scalar=rstd[:, t:t + 1], in1=f_row[:, :],
                                           op0=ALU.mult, op1=ALU.mult).then_inc(x_ready, 1)

    def nothing(eng, at):
        pass

    SGW, SGT, SGG = 2048, 16, 8
    car = Carve()
    sg_v = car.take(TT, SGW)
    sg_u = car.take(SGT, T)
    sg_lng = car.take(SGW)
    sg_lnb = car.take(SGW)
    sg_ws = car.take(SGG, P)
    sg_wsT = car.take(SGG, P)
    sg_bs = car.take(SGG, P)
    sg_mean = sb("sg_mean", [P, 6])
    sgu_loaded = sem("sgu_loaded")
    sgu_ps = sem("sgu_ps")
    sgu_s = sem("sgu_s")
    sgu_wps = sem("sgu_wps")
    sgu_cen = sem("sgu_cen")
    sgu_ss = sem("sgu_ss")
    sgu_rs = sem("sgu_rs")
    sgu_mix = sem("sgu_mix")
    sgu_y = sem("sgu_y")

    SGU = [("v", 8 + q, t) for q in range(8) for t in range(TT)] + [("u", q, i) for q in range(8) for i in range(2)]

    def sgu_sp(sp, at):
        sp.wait_ge(x_ready, TT * at["update"])
        sp.dma_start(sg_lng, A["sg_ln_g_2"][0].partition_broadcast(P)).then_inc(sgu_loaded, 16)
        sp.dma_start(sg_lnb, A["sg_ln_b_2"][0].partition_broadcast(P)).then_inc(sgu_loaded, 16)
        sp.dma_start(sg_ws, A["sg_w_s_2"][0].rearrange("g t s -> t g s")).then_inc(sgu_loaded, 16)
        sp.dma_start(sg_bs[0:1, :, :], A["sg_b_s_2"]).then_inc(sgu_loaded, 16)

    def sgu_weights_sp(sp, at):
        w = A["sg_w_in_2"][0].rearrange("(k p) c -> p k c", p=P)
        chunks = [8 + q for q in range(8)] + list(range(8))
        for n in range(6):
            g = at["load"] + n
            wait_slot_free(sp, g)
            here = chunks[3 * n:3 * n + 3]
            for m, q in enumerate(here):
                sp.dma_start(part(g, m).rearrange("p (k c) -> p k c", k=KD), w[:, :, q * CH:(q + 1) * CH])\
                    .then_inc(load_done[g % RING], 48 // len(here))
        w_out_sp(sp, at, 6, A["sg_w_out_2"][0], tiles=SGT)

    def sgu_pe(pe, at):
        pe.wait_ge(sgu_loaded, 64)
        norm_pe(pe, at)
        gate_pe(pe, at)
        pe.wait_ge(hT_ready, 2 * TT * (at["norm"] + 1))
        for h in range(2):
            for c in range(4):
                ins = nc.tensor.transpose(ps[:, 4 + h, c * P:(c + 1) * P], sg_ws[:, 4 * h + c, :], ident)
            ins.then_inc(sgu_wps, 1)
        for n, (side, q, i) in enumerate(SGU):
            g = at["load"] + n // 6
            if n % 6 == 0:
                wait_loaded(pe, g)
            if n >= 4:
                pe.wait_ge(sgu_s, n - 3)
            w = part(g, n // 2 % 3).rearrange("p (k c) -> p k c", k=KD)
            for k in range(KD):
                if side == "v":
                    ins = nc.tensor.matmul(ps[:, n % 4, 0:CH], hT[:, k, i * P:(i + 1) * P], w[:, k, :],
                                           start=(k == 0), stop=(k == KD - 1))
                else:
                    ins = nc.tensor.matmul(ps[:, n % 4, 0:T], w[:, k, i * P:(i + 1) * P], hT[:, k, :],
                                           start=(k == 0), stop=(k == KD - 1))
            ins.then_inc(sgu_ps, 1)
        pe.wait_ge(sgu_cen, 2 + 2 * TT)
        for n in range(SGG):
            bank = ps[:, 4 + n % 4, :]
            if n >= 4:
                pe.wait_ge(sgu_y, n - 3)
            for i in range(2):
                for t in range(TT):
                    o = bank[:, (2 * i + t) * P:(2 * i + t + 1) * P]
                    nc.tensor.matmul(o, sg_v[:, t, (2 * n + i) * P:(2 * n + i + 1) * P], sg_wsT[:, n, :],
                                     start=True, stop=False)
                    ins = nc.tensor.matmul(o, consts[0:1, C_ONES:C_ONES + P], sg_bs[0:1, n, :],
                                           start=False, stop=True)
            ins.then_inc(sgu_mix, 1)
        pe.wait_ge(sgu_s, len(SGU))
        pe.wait_ge(sgu_y, SGG)
        w_out_pe(pe, at, 6, sg_u, tiles=SGT)

    def sgu_act(act, at):
        norm_act(act, at)
        gate_act(act, at)

        def square(t):
            act.wait_ge(sgu_cen, 2 + t + 1)
            if t:
                act.wait_ge(sgu_ss, t)
            nc.scalar.activation(squares(t), sg_v[:, t, :], ACT.Square, accum_out=sg_mean[:, 4 + t:5 + t])\
                .then_inc(sgu_ss, 1)

        for n, (side, q, i) in enumerate(SGU):
            act.wait_ge(sgu_ps, n + 1)
            dst = sg_v[:, i, (q - 8) * CH:(q - 7) * CH] if side == "v" else sg_u[:, 2 * q + i, :]
            nc.scalar.activation(dst, ps[:, n % 4, 0:CH], ACT.Gelu_apprx_tanh).then_inc(sgu_s, 1)
            if n in (20, 24):
                square((n - 20) // 4)

    def squares(t):
        return xn[:, :, :].rearrange("p t d -> p (t d)")

    def sgu_dve(dve, at):
        step = dve_steps.done
        norm_dve(dve, at, amp[:, 4, :], mod_cols(1, 3, 0))
        for h in range(2):
            dve.wait_ge(sgu_wps, h + 1)
            nc.vector.tensor_copy(sg_wsT[:, 4 * h:4 * h + 4, :], ps[:, 4 + h, :].rearrange("p (g c) -> p g c", c=P))\
                .then_inc(sgu_cen, 1)
        dve.wait_ge(sgu_s, 16)
        for t in range(TT):
            step(dve, nc.vector.tensor_reduce(sg_mean[:, t:t + 1], sg_v[:, t, :], AX.X, ALU.add))
            step(dve, nc.vector.tensor_scalar(sg_mean[:, 2 + t:3 + t], sg_mean[:, t:t + 1], 1.0 / SGW, None, ALU.mult))
            nc.vector.tensor_scalar(sg_v[:, t, :], sg_v[:, t, :], sg_mean[:, 2 + t:3 + t], None,
                                    ALU.subtract).then_inc(sgu_cen, 1)
        dve.wait_ge(sgu_loaded, 64)
        for t in range(TT):
            v = sg_v[:, t, :]
            dve.wait_ge(sgu_rs, t + 1)
            step(dve, nc.vector.scalar_tensor_tensor(out=v, in0=v, scalar=sg_mean[:, 4 + t:5 + t], in1=sg_lng,
                                                     op0=ALU.mult, op1=ALU.mult))
            nc.vector.tensor_tensor(v, v, sg_lnb, ALU.add).then_inc(sgu_cen, 1)
        for n in range(SGG):
            dve.wait_ge(sgu_mix, n + 1)
            dve.wait_ge(sgu_s, 16 + 2 * n + 2)
            u = sg_u[:, 2 * n:2 * n + 2, :]
            nc.vector.tensor_tensor(u, u, ps[:, 4 + n % 4, :].rearrange("p (c i) -> p c i", c=2), ALU.mult)\
                .then_inc(sgu_y, 1)
        add_to_x(dve, w_out_done(dve, at, tiles=SGT), x_sb, 1.0, gate_row)

    def sgu_pool(pool, at):
        norm_pool(pool, at)
        for t in range(TT):
            pool.wait_ge(sgu_ss, t + 1)
            v = sg_mean[:, 4 + t:5 + t]
            inv_sqrt(pool, v, v, 1.0 / SGW, EPS).then_inc(sgu_rs, 1)

    NH, NDH, GRID = 8, 64, 64
    MH, MW = 4, P
    MX = MW + 1
    car = Carve()
    car.take(TT, D)
    e_hx = car.take(KD, T)
    e_qaT = car.take(4, T)
    e_kaT = car.take(4, 2 * T)
    e_va = car.take(4, NH * NDH)
    e_qb = car.take(TT, MH * MW)
    e_kb = car.take(4, MH * MW)
    e_vb = car.take(4, MH, MX + 3)
    e_ob = car.take(TT, MH * MW)
    e_g = car.take(4, 16)
    after = car.at
    car = Carve()
    e_p = car.take(2, 2 * T)
    e_pT = car.take(2, 4 * P)
    e_bias = car.take(2, TT, T)
    car = Carve()
    e_rm = car.take(2, MH * P)
    e_sT = car.take(2, MH * P)
    e_ka = car.take(MH * P)
    e_o = car.take(MH, MX + 3)
    car.at = max(car.at, 0)
    assert car.at <= 4096
    car.at = after
    e_qT = car.take(MH, T)
    e_kT = car.take(MH, T)
    e_C = car.take(2 * MH, MX + 3)
    e_rot = aT[:, :, :].rearrange("p a b -> p (a b)")
    e_s = sb("e_s", [P, 576])
    e_gl = e_s[:, 0:64]
    e_ga = e_s[:, 64:128]
    e_li, e_lf, e_b, e_r, e_we, e_be, e_mb, e_t, e_ap, e_at = (
        e_s[:, 128 + 32 * i:160 + 32 * i] for i in range(10))
    e_mx = e_s[:, 448:456]
    e_wi = e_s[:, 456:464]
    e_em = e_s[:, 464:472]
    e_den = e_s[:, 472:480]
    e_nm = e_s[:, 480:482]
    e_sum = e_s[:, 482:484]
    e_rec = e_s[:, 484:486]
    e_hss = e_s[:, 488:496]
    e_rows = sb("e_rows", [8, 64])
    e_wmax, e_ber, e_m = e_rows[:, 0:4], e_rows[:, 4:8], e_rows[:, 8:12]
    e_md = e_rows[:, 16:48]
    e_gb = sb("e_gb", [P, 16])
    rpb_copies = nc.dram_tensor("rpb_copies", (GRID, math.prod(A["na_rpb_2"].shape)), FP32, kind="Internal").ap()
    TILE = [[2, 3, 0, 1], [3, 2, 1, 0]]

    even_ps = sem("even_ps")
    even_s = sem("even_s")
    even_copies = sem("even_copies")
    even_bias = [sem(f"even_bias_{i}") for i in range(2)]
    even_z = sem("even_z")
    even_m = sem("even_m")
    even_e = sem("even_e")
    even_p = sem("even_p")
    even_pt = sem("even_pt")
    even_pts = sem("even_pts")
    even_o = sem("even_o")
    ml_gates = sem("ml_gates")
    ml_exps = sem("ml_exps")
    ml_sums = sem("ml_sums")
    ml_rot = sem("ml_rot")
    ml_T = sem("ml_T")
    ml_Ts = sem("ml_Ts")
    ml_ka = sem("ml_ka")
    ml_U = sem("ml_U")
    ml_C = sem("ml_C")
    ml_R = sem("ml_R")
    ml_w = sem("ml_w")
    ml_we2 = sem("ml_we2")
    ml_on = sem("ml_on")
    ml_rs = sem("ml_rs")

    def even_products():
        made = []
        for q in range(14):
            name, c = ("qa", "ka", "va", "qb", "kb", "vb", "ob")[q // 2], q % 2
            for side in ((0, 1) if name in ("ka", "va", "kb", "vb") else (0,)):
                for i in range(2):
                    cols = slice(c * CH, (c + 1) * CH)
                    tile = 2 * side + i
                    if name == "qa":
                        to = (e_qaT[:, 2 * c + i, :], ACT.Copy, float(NDH) ** -0.5)
                    elif name == "ka":
                        to = (e_kaT[:, 2 * c + i, side * T:(side + 1) * T], ACT.Copy, 1.0)
                    elif name == "va":
                        to = (e_va[:, tile, cols], ACT.Copy, 1.0)
                    elif name == "qb":
                        to = (e_qb[:, i, cols], ACT.Copy, 1.0)
                    elif name == "kb":
                        to = (e_kb[:, tile, cols], ACT.Copy, float(MW) ** -0.5)
                    elif name == "vb":
                        to = (e_vb[:, tile, 2 * c:2 * c + 2, 0:MW], ACT.Copy, 1.0)
                    else:
                        to = (e_ob[:, i, cols], ACT.Sigmoid, 1.0)
                    made.append((q, name in ("qa", "ka"), side, i, *to))
        for side in range(2):
            for i in range(2):
                made.append((14, False, side, i, e_g[:, 2 * side + i, :], ACT.Copy, 1.0))
        return made

    EVEN = even_products()
    EVEN_ENDS = [sum(p[0] < 3 * (n + 1) for p in EVEN) for n in range(5)]

    def even_sp(sp, at):
        final = [a for a in PLACES if a["kind"] == "final"][0]
        sp.wait_ge(x_ready, TT * (final["update"] + 1))
        sp.dma_start(f_row[:, :], A["final_g_2"].partition_broadcast(P)).then_inc(x_loaded, 16)
        w = A["mix_w_in_2"][0].rearrange("(k p) c -> p k c", p=P)
        for n in range(5):
            g = at["load"] + n
            wait_slot_free(sp, g)
            for m in range(3):
                q = 3 * n + m
                width = CH if q < 14 else 16
                sp.dma_start(part(g, m)[:, 0:KD * width].rearrange("p (k c) -> p k c", k=KD),
                             w[:, :, q * CH:q * CH + width]).then_inc(load_done[g % RING], 16)
        w_out_sp(sp, at, 5, A["mix_w_out_2"][0])

    def even_pool(pool, at):
        norm_pool(pool, at, 0)
        norm_pool(pool, at, 1)
        rpb = A["na_rpb_2"]
        rel_rows, rel_cols = rpb.shape[2], rpb.shape[3]
        size = rpb_copies.shape[1]
        pool.dma_start(rpb_copies, rpb.rearrange("a h r c -> (a h r c)").partition_broadcast(GRID))\
            .then_inc(even_copies, 16)
        pool.wait_ge(even_copies, 16)
        for h in range(NH):
            if h == 0:
                pool.wait_ge(even_s, len(EVEN))
            if h >= 2:
                pool.wait_ge(even_m, 2 * (h - 1))
            for i in range(4):
                dst = e_bias[(i % 2) * GRID:(i % 2 + 1) * GRID, h % 2, i // 2, :].rearrange("p (a c) -> p a c", a=4)
                src = bass.AP(tensor=rpb_copies.tensor,
                              offset=(h * rel_rows + rel_rows // 2 - i) * rel_cols + rel_cols // 2,
                              ap=[[size - 1, GRID], [rel_cols, 4], [1, GRID]])
                pool.dma_start(dst, src).then_inc(even_bias[h % 2], 16)
        pool.wait_ge(ml_gates, 6)
        inv_sqrt(pool, e_hss, e_hss, 1.0 / MW, EPS).then_inc(ml_rs, 1)

    def even_pe(pe, at):
        norm_pe(pe, at, 0)
        pe.wait_ge(hT_ready, 2 * TT * (at["norm"] + 1))
        norm_pe(pe, at, 1)
        gate_pe(pe, at)
        pe.wait_ge(hT_ready, 2 * TT * (at["norm"] + 2))
        last = -1
        for n, (q, is_T, side, i, *_) in enumerate(EVEN):
            g = at["load"] + q // 3
            if q // 3 != last:
                wait_loaded(pe, g)
                last = q // 3
            if n >= 4:
                pe.wait_ge(even_s, n - 3)
            h = e_hx if side else hT
            width = CH if q < 14 else 16
            w = part(g, q % 3)[:, 0:KD * width].rearrange("p (k c) -> p k c", k=KD)
            for k in range(KD):
                if is_T:
                    ins = nc.tensor.matmul(ps[:, n % 4, 0:T], w[:, k, i * P:(i + 1) * P], h[:, k, :],
                                           start=(k == 0), stop=(k == KD - 1))
                else:
                    ins = nc.tensor.matmul(ps[:, n % 4, 0:width], h[:, k, i * P:(i + 1) * P], w[:, k, :],
                                           start=(k == 0), stop=(k == KD - 1))
            ins.then_inc(even_ps, 1)
        pe.wait_ge(even_s, len(EVEN))
        units = 2 * NH
        for u in range(units + 2):
            if u < units:
                h, t = divmod(u, 2)
                rows = slice((h % 2) * NDH, (h % 2 + 1) * NDH)
                if u >= 2:
                    pe.wait_ge(even_e, u - 1)
                nc.tensor.matmul(ps[:, u % 2, :], e_qaT[rows, h // 2, t * P:(t + 1) * P], e_kaT[rows, h // 2, :],
                                 start=True, stop=True).then_inc(even_z, 1)
            if 1 <= u <= units:
                v = u - 1
                pe.wait_ge(even_p, v + 1)
                if v >= 2:
                    pe.wait_ge(even_pts, v - 1)
                for c in range(4):
                    ins = nc.tensor.transpose(ps[:, 2 + v % 2, c * P:(c + 1) * P],
                                              e_p[:, v % 2, c * P:(c + 1) * P], ident)
                ins.then_inc(even_pt, 1)
            if u >= 2:
                v = u - 2
                h, t = divmod(v, 2)
                rows = slice((h % 2) * NDH, (h % 2 + 1) * NDH)
                pe.wait_ge(even_pts, v + 1)
                if v >= 2:
                    pe.wait_ge(mix_in_ready, mix_in_before(at) + v - 1)
                for c in range(4):
                    ins = nc.tensor.matmul(ps[rows, 4 + v % 2, 0:P], e_va[:, c, h * NDH:(h + 1) * NDH],
                                           e_pT[:, v % 2, c * P:(c + 1) * P], start=(c == 0), stop=(c == 3))
                ins.then_inc(even_o, 1)
        pe.wait_ge(mix_in_ready, mix_in_before(at) + units)
        pe.wait_ge(ml_gates, 2)
        lf = e_lf.rearrange("p (s d h) -> p s d h", s=4, d=2)
        b = ps[:, 6, 0:32].rearrange("p (s d h) -> p s d h", s=4, d=2)
        for d in range(2):
            nc.tensor.matmul(b[:, :, d, :], col(C_UPPER if d == 0 else C_FROM), lf[:, :, d, :], start=True, stop=True)
        nc.tensor.matmul(ps[:, 6, 32:64], col(C_ONES), e_lf, start=True, stop=True)
        for s in range(4):
            ins = nc.tensor.matmul(ps[0:8, 6, 64 + s:65 + s], e_lf[:, 8 * s:8 * s + 8], col(C_ONES, 1),
                                   start=True, stop=True)
        ins.then_inc(ml_sums, 1)
        pe.wait_ge(ml_gates, 3)
        for s in range(4):
            ins = nc.tensor.transpose(ps[0:8, 7, s * P:(s + 1) * P], e_we[:, 8 * s:8 * s + 8], ident)
        ins.then_inc(ml_sums, 1)
        pe.wait_ge(ml_gates, 4)
        nc.tensor.matmul(ps[:, 6, 128:160], consts[0:8, C_ONES:C_ONES + P], e_md, start=True, stop=True)\
            .then_inc(ml_sums, 1)
        for n, (src, t) in enumerate(((e_qb, 0), (e_qb, 1), (e_kb, 0), (e_kb, 1))):
            pe.wait_ge(ml_rot, n + 1)
            for c in range(MH):
                ins = nc.tensor.transpose(ps[:, n, c * P:(c + 1) * P], src[:, t, c * MW:(c + 1) * MW], ident)
            ins.then_inc(ml_T, 1)
        pe.wait_ge(ml_Ts, 4)

        def update(s, d):
            n = 2 * s + d
            pe.wait_ge(ml_ka, n + 1)
            for h in range(MH):
                ins = nc.tensor.matmul(ps[:, 4 + h // 2, (h % 2) * MX:(h % 2 + 1) * MX], e_ka[:, h * P:(h + 1) * P],
                                       e_vb[:, TILE[d][s], h, 0:MX], start=True, stop=True)
            ins.then_inc(ml_U, 1)

        for s in range(4):
            if s < 2:
                for d in range(2):
                    update(s, d)
                continue
            for d in range(2):
                n, tile = 2 * (s - 2) + d, TILE[d][s]
                q = [e_qT[:, h, tile * P:(tile + 1) * P] for h in range(MH)]
                if n:
                    pe.wait_ge(ml_on, n)
                pe.wait_ge(ml_C, 2 * (s - 1) + d + 1)
                for h in range(MH):
                    r = e_r[:, 8 * s + 4 * d + h:8 * s + 4 * d + h + 1]
                    nc.tensor.matmul(ps[:, 0, h * P:(h + 1) * P], r.to_broadcast([P, P]), ident, start=True, stop=True)
                    nc.tensor.matmul(ps[:, 1, h * P:(h + 1) * P], q[h], e_kT[:, h, tile * P:(tile + 1) * P],
                                     start=True, stop=True)
                    ins = nc.tensor.matmul(ps[:, 2 + h // 2, (h % 2) * MX:(h % 2 + 1) * MX], q[h],
                                           e_C[:, 4 * d + h, 0:MX], start=True, stop=True)
                ins.then_inc(ml_R, 1)
                pe.wait_ge(ml_w, 2 * n + 2)
                for h in range(MH):
                    ins = nc.tensor.transpose(ps[:, 7, h * P:(h + 1) * P], e_rm[:, d, h * P:(h + 1) * P], ident)
                ins.then_inc(ml_R, 1)
                pe.wait_ge(ml_we2, 2 * n + 2)
                for h in range(MH):
                    ins = nc.tensor.matmul(ps[:, 4 + h // 2, (h % 2) * MX:(h % 2 + 1) * MX],
                                           e_sT[:, d, h * P:(h + 1) * P], e_vb[:, tile, h, 0:MX], start=True, stop=True)
                ins.then_inc(ml_R, 1)
                if s == 2:
                    pe.wait_ge(ml_on, n + 1)
                    update(s, d)
        for t in range(TT):
            pe.wait_ge(ml_on, 4 + t + 1)
            for h in range(MH):
                ins = nc.tensor.transpose(ps[:, t, h * P:(h + 1) * P], xn[:, t, h * P:(h + 1) * P], ident)
            ins.then_inc(ml_T, 1)
        w_out_pe(pe, at, 5, hT)

    def even_act(act, at):
        norm_act(act, at, 0, src=x_ctx)
        norm_act(act, at, 1)
        gate_act(act, at)
        for n, (q, _, _, _, dst, func, factor) in enumerate(EVEN):
            width = CH if q < 14 else 16
            act.wait_ge(even_ps, n + 1)
            src = ps[:, n % 4, 0:width]
            if len(dst.shape) == 3:
                src = src.rearrange("p (h c) -> p h c", h=2)
            nc.scalar.activation(dst, src, func, scale=factor).then_inc(even_s, 1)
        act.wait_ge(ml_gates, 1)
        act_steps.done(act, nc.scalar.activation(e_gl, e_ga, ACT.Abs))
        act_steps.done(act, nc.scalar.activation(e_gl, e_gl, ACT.Exp, scale=-1.0))
        nc.scalar.activation(e_gl, e_gl, ACT.Ln, bias=1.0).then_inc(ml_exps, 1)
        units = 2 * NH
        for u in range(units + 2):
            if u < units:
                act.wait_ge(even_m, u + 1)
                if u >= 2:
                    act.wait_ge(even_pt, u - 1)
                nc.scalar.activation(e_p[:, u % 2, :], ps[:, u % 2, :], ACT.Exp, bias=e_nm[:, u % 2:u % 2 + 1],
                                     accum_out=e_sum[:, u % 2:u % 2 + 1]).then_inc(even_e, 1)
            if u >= 2:
                v = u - 2
                h, t = divmod(v, 2)
                rows = slice((h % 2) * NDH, (h % 2 + 1) * NDH)
                act.wait_ge(even_o, v + 1)
                nc.scalar.activation(hT[rows, h // 2, t * P:(t + 1) * P], ps[rows, 4 + v % 2, 0:P], ACT.Copy)\
                    .then_inc(mix_in_ready, 1)
        act.wait_ge(ml_gates, 5)
        nc.scalar.activation(e_ap[:, 0:24], e_ap[:, 0:24], ACT.Exp)
        nc.scalar.activation(e_at[:, 0:24], e_at[:, 0:24], ACT.Exp).then_inc(ml_exps, 1)
        for n in range(4):
            act.wait_ge(ml_T, n + 1)
            nc.scalar.activation((e_qT if n < 2 else e_kT)[:, :, (n % 2) * P:(n % 2 + 1) * P],
                                 ps[:, n, :].rearrange("p (h c) -> p h c", c=P), ACT.Copy).then_inc(ml_Ts, 1)
        for n in range(4):
            d = n % 2
            act.wait_ge(ml_w, 2 * n + 1)
            nc.scalar.activation(e_wi[:, 4 * d:4 * d + 4], e_wi[:, 4 * d:4 * d + 4], ACT.Exp)
            nc.scalar.activation(e_em[:, 4 * d:4 * d + 4], e_em[:, 4 * d:4 * d + 4], ACT.Exp, scale=-1.0)
            nc.scalar.activation(e_rm[:, d, :], e_rm[:, d, :], ACT.Exp).then_inc(ml_we2, 1)
            act.wait_ge(ml_R, 3 * n + 2)
            nc.scalar.activation(e_sT[:, d, :], ps[:, 7, :], ACT.Copy).then_inc(ml_we2, 1)

    def even_dve(dve, at):
        step = dve_steps.done
        norm_dve(dve, at, amp[:, 7, :], mod_cols(0, 3, 1), k=0, src=x_ctx, dst=e_hx)
        norm_dve(dve, at, amp[:, 1, :], mod_cols(0, 3, 0), k=1)
        step(dve, nc.vector.memset(e_vb[:, :, :, MW:MX], 1.0))
        dve.wait_ge(even_s, len(EVEN))
        dve.wait_ge(rows_loaded, ROWS_DMAS)
        nc.vector.tensor_tensor(e_ga.rearrange("p (t c) -> p t c", t=4), e_g, bc_mid(e_gb[:, :], 4),
                                ALU.add).then_inc(ml_gates, 1)
        units = 2 * NH
        window = col(C_WINDOW, 2 * T).rearrange("p (t k) -> p t k", t=TT)
        for u in range(units + 1):
            if u < units:
                h, t = divmod(u, 2)
                slot_ = u % 2
                if t == 0:
                    dve.wait_ge(even_bias[h % 2], 64 * (h // 2 + 1))
                    step(dve, nc.vector.tensor_tensor(e_bias[:, h % 2, :, :], e_bias[:, h % 2, :, :], window, ALU.add))
                dve.wait_ge(even_z, u + 1)
                step(dve, nc.vector.tensor_tensor(ps[:, slot_, 0:T], ps[:, slot_, 0:T], e_bias[:, h % 2, t, :],
                                                  ALU.add))
                nc.vector.tensor_reduce(e_nm[:, slot_:slot_ + 1], ps[:, slot_, :], AX.X, ALU.max,
                                        negate=True).then_inc(even_m, 1)
            if u >= 1:
                v = u - 1
                r = e_rec[:, v % 2:v % 2 + 1]
                dve.wait_ge(even_e, v + 1)
                step(dve, nc.vector.reciprocal(r, e_sum[:, v % 2:v % 2 + 1]))
                nc.vector.tensor_scalar(e_p[:, v % 2, :], e_p[:, v % 2, :], r, None, ALU.mult).then_inc(even_p, 1)
                dve.wait_ge(even_pt, v + 1)
                if v >= 2:
                    dve.wait_ge(even_o, v - 1)
                nc.vector.tensor_copy(e_pT[:, v % 2, :], ps[:, 2 + v % 2, :]).then_inc(even_pts, 1)
        dve.wait_ge(ml_exps, 1)
        dve.wait_ge(mix_in_ready, mix_in_before(at) + units)
        step(dve, nc.vector.scalar_tensor_tensor(out=e_gl, in0=e_ga, scalar=0.0, in1=e_gl,
                                                 op0=ALU.min, op1=ALU.subtract))
        gi, gf = (v.rearrange("p (t h d g) -> p t h d g", t=4, h=MH, d=2) for v in (e_ga, e_gl))
        for d in range(2):
            for s in range(4):
                c = slice(8 * s + 4 * d, 8 * s + 4 * d + 4)
                nc.vector.tensor_copy(e_li[:, c], gi[:, TILE[d][s], :, d, 0])
                ins = nc.vector.tensor_copy(e_lf[:, c], gf[:, TILE[d][s], :, d, 1])
                if d == 0 or s < 3:
                    step(dve, ins)
        ins.then_inc(ml_gates, 1)
        dve.wait_ge(ml_sums, 1)
        step(dve, nc.vector.tensor_copy(e_b, ps[:, 6, 0:32]))
        step(dve, nc.vector.tensor_tensor(e_r, e_li, e_b, ALU.subtract))
        step(dve, nc.vector.tensor_copy(e_be, ps[:, 6, 32:64]))
        step(dve, nc.vector.tensor_copy(e_ber, ps[0:8, 6, 64:68]))
        nc.vector.tensor_tensor(e_we, e_be, e_r, ALU.add).then_inc(ml_gates, 1)
        dve.wait_ge(ml_sums, 2)
        step(dve, nc.vector.tensor_reduce(e_wmax, ps[0:8, 7, :].rearrange("p (s c) -> p s c", c=P), AX.X, ALU.max))
        step(dve, nc.vector.memset(e_m, 0.0))
        for s in range(3):
            nxt = e_m[:, s + 1:s + 2]
            step(dve, nc.vector.tensor_tensor(nxt, e_ber[:, s:s + 1], e_m[:, s:s + 1], ALU.add))
            step(dve, nc.vector.tensor_tensor(nxt, nxt, e_wmax[:, s:s + 1], ALU.max))
        nc.vector.tensor_tensor(e_md.rearrange("p (s c) -> p s c", c=8), consts[0:8, None, C_IDENT:C_IDENT + 8].to_broadcast([8, 4, 8]),
                                e_m[:, :, None].to_broadcast([8, 4, 8]), ALU.mult).then_inc(ml_gates, 1)
        dve.wait_ge(ml_sums, 3)
        step(dve, nc.vector.tensor_copy(e_mb, ps[:, 6, 128:160]))
        step(dve, nc.vector.tensor_tensor(e_t[:, 0:24], e_be[:, 0:24], e_mb[:, 0:24], ALU.add))
        step(dve, nc.vector.tensor_tensor(e_ap[:, 0:24], e_t[:, 0:24], e_mb[:, 8:32], ALU.subtract))
        nc.vector.tensor_tensor(e_at[:, 0:24], e_we[:, 0:24], e_mb[:, 8:32], ALU.subtract).then_inc(ml_gates, 1)
        for n, (src, t) in enumerate(((e_qb, 0), (e_qb, 1), (e_kb, 0), (e_kb, 1))):
            v = src[:, t, :].rearrange("p (h c two) -> p h c two", h=MH, two=2)
            for h in range(MH):
                def fin(ins):
                    if h < MH - 1:
                        step(dve, ins)
                    else:
                        ins.then_inc(ml_rot, 1)
                        dve.wait_ge(ml_rot, n + 1)
                x1, x2 = v[:, h:h + 1, :, 0], v[:, h:h + 1, :, 1]
                rotate(dve, step, x1, x2, x1, x2, col(C_AXIAL + P * t, 64), col(C_AXIAL + P * t + 64, 64), e_rot, fin)
        dve.wait_ge(ml_exps, 2)

        def heads(ap, w=P):
            return ap.rearrange("p (h c) -> p h c", c=w)

        def two_banks(bank):
            return ps[:, bank:bank + 2, 0:2 * MX].rearrange("p b (h c) -> p b h c", c=MX)

        def pairs(ap):
            return ap.rearrange("p (b h) c -> p b h c", b=2)

        def bc4(cols_ap):
            return cols_ap.rearrange("p (b h) -> p b h", b=2)[:, :, :, None].to_broadcast([P, 2, 2, MX])

        def update(s, d):
            n = 2 * s + d
            c = slice(8 * s + 4 * d, 8 * s + 4 * d + 4)
            if n:
                dve.wait_ge(ml_U, n)
            nc.vector.tensor_tensor(heads(e_ka), heads(e_kb[:, TILE[d][s], :]), bc_last(e_at[:, c], P), ALU.mult)\
                .then_inc(ml_ka, 1)
            state = e_C[:, 4 * d:4 * d + 4, 0:MX]
            if s:
                step(dve, nc.vector.tensor_tensor(state, state, bc_last(e_ap[:, c], MX), ALU.mult))
            dve.wait_ge(ml_U, n + 1)
            if s:
                ins = nc.vector.tensor_tensor(pairs(state), pairs(state), two_banks(4), ALU.add)
            else:
                ins = nc.vector.tensor_copy(pairs(state), two_banks(4))
            ins.then_inc(ml_C, 1)
            dve.wait_ge(ml_C, n + 1)

        for s in range(4):
            for d in range(2):
                if s < 2:
                    update(s, d)
                    continue
                n, tile = 2 * (s - 2) + d, TILE[d][s]
                c, c4 = slice(8 * s + 4 * d, 8 * s + 4 * d + 4), slice(4 * d, 4 * d + 4)
                rm = e_rm[:, d, :]
                mask = col(C_CNEG) if d == 0 else col(C_EARLIER)
                dve.wait_ge(ml_R, 3 * n + 1)
                step(dve, nc.vector.tensor_tensor(heads(rm), heads(ps[:, 0, :]), bc_mid(mask, MH), ALU.add))
                step(dve, nc.vector.tensor_reduce(e_mx[:, c4], heads(rm), AX.X, ALU.max))
                step(dve, nc.vector.tensor_tensor(e_mx[:, c4], e_mx[:, c4], e_mb[:, c], ALU.max))
                step(dve, nc.vector.tensor_tensor(e_wi[:, c4], e_mb[:, c], e_mx[:, c4], ALU.subtract))
                step(dve, nc.vector.tensor_tensor(e_em[:, c4], e_b[:, c], e_mx[:, c4], ALU.add))
                nc.vector.tensor_tensor(heads(rm), heads(rm), bc_last(e_mx[:, c4], P), ALU.subtract)\
                    .then_inc(ml_w, 1)
                dve.wait_ge(ml_we2, 2 * n + 1)
                nc.vector.tensor_tensor(rm, rm, ps[:, 1, :], ALU.mult).then_inc(ml_w, 1)
                o = pairs(e_o[:, :, 0:MX])
                step(dve, nc.vector.tensor_tensor(o, two_banks(2), bc4(e_wi[:, c4]), ALU.mult))
                dve.wait_ge(ml_R, 3 * n + 3)
                step(dve, nc.vector.tensor_tensor(o, o, two_banks(4), ALU.add))
                den, raw = e_den[:, c4], e_o[:, :, MW]
                step(dve, nc.vector.tensor_scalar(den, raw, -1.0, None, ALU.mult))
                step(dve, nc.vector.tensor_tensor(den, den, raw, ALU.max))
                step(dve, nc.vector.tensor_tensor(den, den, e_em[:, c4], ALU.max))
                step(dve, nc.vector.reciprocal(den, den))
                h_t = heads(xn[:, tile, 0:MH * P])
                if s == 2:
                    ins = nc.vector.tensor_tensor(h_t, e_o[:, :, 0:MW], bc_last(den, MW), ALU.mult)
                else:
                    step(dve, nc.vector.tensor_tensor(e_o[:, :, 0:MW], e_o[:, :, 0:MW], bc_last(den, MW), ALU.mult))
                    ins = nc.vector.tensor_tensor(h_t, h_t, e_o[:, :, 0:MW], ALU.add)
                ins.then_inc(ml_on, 1)
                dve.wait_ge(ml_on, n + 1)
                if s == 2:
                    update(s, d)
        h_all = xn[:, :, 0:MH * P]
        sq = xn[:, :, MH * P:D]
        step(dve, nc.vector.tensor_tensor(sq, h_all, h_all, ALU.mult))
        for t in range(TT):
            ins = nc.vector.tensor_reduce(e_hss[:, 4 * t:4 * t + 4], heads(sq[:, t, :]), AX.X, ALU.add)
            if t == 0:
                step(dve, ins)
        ins.then_inc(ml_gates, 1)
        dve.wait_ge(ml_rs, 1)
        for t in range(TT):
            v = xn[:, t, 0:MH * P]
            step(dve, nc.vector.tensor_tensor(heads(v), heads(v), bc_last(e_hss[:, 4 * t:4 * t + 4], P), ALU.mult))
            nc.vector.tensor_tensor(v, v, e_ob[:, t, :], ALU.mult).then_inc(ml_on, 1)
        for t in range(TT):
            dve.wait_ge(ml_T, 4 + t + 1)
            for k in range(2):
                gains = cols_T[:, 0, 98 + 2 * k:100 + 2 * k]
                nc.vector.tensor_tensor(hT[:, 4 + 2 * k:6 + 2 * k, t * P:(t + 1) * P],
                                        heads(ps[:, t, k * T:(k + 1) * T]), bc_last(gains, P), ALU.mult)\
                    .then_inc(mix_in_ready, 1)
        add_to_x(dve, w_out_done(dve, at), x_sb, 1.0, gate_row)

    def sgu_all_sp(sp, at):
        sgu_sp(sp, at)
        sgu_weights_sp(sp, at)

    SP = {"ffn": ffn_sp, "gdn": gdn_sp_, "sb": sb_sp, "dsa": dsa_sp, "ctx": ctx_sp, "even": even_sp,
          "sgu": sgu_all_sp, "final": final_sp}
    ACTS = {"ffn": ffn_act, "gdn": gdn_act, "sb": sb_act, "dsa": dsa_act, "ctx": nothing, "even": even_act,
            "sgu": sgu_act, "final": final_act}
    DVES = {"ffn": ffn_dve, "gdn": gdn_dve, "sb": sb_dve, "dsa": dsa_dve, "ctx": nothing, "even": even_dve,
            "sgu": sgu_dve, "final": final_dve}
    PES = {"ffn": ffn_pe, "gdn": gdn_pe, "sb": sb_pe, "dsa": dsa_pe, "ctx": ctx_pe, "even": even_pe,
           "sgu": sgu_pe, "final": nothing}
    POOLS = {"ffn": ffn_pool, "gdn": gdn_pool, "sb": norm_pool, "dsa": dsa_pool, "ctx": nothing,
             "even": even_pool, "sgu": sgu_pool, "final": final_pool}

    with nc.Block() as block:

        @block.sync
        def _(sp):
            sp.dma_start(consts[:, :], A["consts"]).then_inc(consts_loaded, 16)
            sp.dma_start(x_sb[:, :, :], A["x"][0].rearrange("(t p) d -> p t d", p=P)).then_inc(x_loaded, 16)
            r = 0
            for name, rows in (("ffn1_norm", 4), ("mix_norm", 4), ("ffn2_norm", 4)):
                sp.dma_start(gain_rows[r:r + rows, :], A[name]).then_inc(gains_loaded, 16)
                r += rows
            sp.dma_start(gain_rows[r:r + 6, :], A["norm_g_2"].rearrange("l j d -> (l j) d")).then_inc(gains_loaded, 16)
            sp.dma_start(gain_rows[18:19, :], A["c_2"]).then_inc(gains_loaded, 16)
            sp.dma_start(gain_rows[19:20, :], A["c_ctx_2"].rearrange("(a d) -> a d", a=1)).then_inc(gains_loaded, 16)
            for j in range(2):
                sp.dma_start(col_rows[0:96, j, :], A["gdn_conv"][j].rearrange("w (c p) -> (w c) p", p=P))\
                    .then_inc(gains_loaded, 16)
            for r, name in ((96, "gdn_norm"), (98, "ml_head_g_2"), (102, "dsa_cq_norm"), (105, "dsa_ckv_norm")):
                v = A[name].rearrange("l h d -> (l h) d") if name == "ml_head_g_2" else \
                    A[name].rearrange("l (c p) -> (l c) p", p=P)
                sp.dma_start(col_rows[r:r + v.shape[0], 0, :], v).then_inc(gains_loaded, 16)
            for j in range(2):
                for c, name in ((0, "gdn_dt_bias"), (8, "gdn_a_log")):
                    sp.dma_start(g_rows[:, j, c:c + 8], A[name][j].partition_broadcast(P)).then_inc(rows_loaded, 16)
            sp.dma_start(e_gb[:, :], A["ml_gate_b_2"].rearrange("a h d g -> (a h d g)").partition_broadcast(P))\
                .then_inc(rows_loaded, 16)
            sp.dma_start(d_gk[:, :], A["dsa_kidx_norm"][0].partition_broadcast(P)).then_inc(rows_loaded, 16)
            sp.dma_start(f_row[:, :], A["final_norm"].partition_broadcast(P)).then_inc(rows_loaded, 16)
            for l in range(2):
                sp.dma_start(m_rows[0:NMOD, l, :], A["b_mod_2"][l].rearrange("(n p) -> n p", p=P))\
                    .then_inc(gains_loaded, 16)
            for at in PLACES:
                SP[at["kind"]](sp, at)
            sp.wait_ge(out_done, 16 * TT)

        @block.scalar
        def _(act):
            act.wait_ge(gains_ready, 1)
            nc.scalar.activation(m_s[:, :, :], gain[:, :, 18:20], ACT.Silu).then_inc(gains_ready, 1)
            for at in PLACES:
                ACTS[at["kind"]](act, at)

        @block.vector
        def _(dve):
            dve.wait_ge(gains_turned, 1)
            nc.vector.tensor_copy(gain[:, :, :], ps[:, 4, 0:KD * NGAIN].rearrange("p (k n) -> p k n", n=NGAIN))\
                .then_inc(gains_ready, 1)
            nc.vector.tensor_copy(cols_T[:, 0, 0:107], ps[:, 5, 0:107]).then_inc(gains_ready, 1)
            nc.vector.tensor_copy(cols_T[:, 1, 0:96], ps[:, 5, P:P + 96]).then_inc(gains_ready, 1)
            dve.wait_ge(m_sum, 2)
            for l in range(2):
                nc.vector.tensor_copy(mod[:, l, :, :], ps[:, 6, l * P:l * P + NMOD, None].to_broadcast([P, NMOD, 2]))\
                    .then_inc(gains_ready, 1)
            dve.wait_ge(gains_ready, 6)
            for at in PLACES:
                DVES[at["kind"]](dve, at)

        @block.gpsimd
        def _(pool):
            pool.wait_ge(consts_loaded, 16)
            for at in PLACES:
                POOLS[at["kind"]](pool, at)

        @block.tensor
        def _(pe):
            pe.wait_ge(consts_loaded, 16)
            pe.wait_ge(gains_loaded, 16 * 14)
            for k in range(KD):
                ins = nc.tensor.transpose(ps[:, 4, k * NGAIN:(k + 1) * NGAIN], gain_rows[:, k * P:(k + 1) * P],
                                          consts[0:NGAIN, C_IDENT:C_IDENT + NGAIN])
            for j, rows in ((0, 107), (1, 96)):
                ins = nc.tensor.transpose(ps[:, 5, j * P:j * P + rows], col_rows[0:rows, j, :],
                                          consts[0:rows, C_IDENT:C_IDENT + rows])
            ins.then_inc(gains_turned, 1)
            for l in range(2):
                ins = nc.tensor.transpose(ps[:, 6, l * P:l * P + NMOD], m_rows[0:NMOD, l, :],
                                          consts[0:NMOD, C_IDENT:C_IDENT + NMOD])
                ins.then_inc(m_sum, 1)
            pe.wait_ge(gains_ready, 6)
            for at in PLACES:
                PES[at["kind"]](pe, at)

    ctx.close()


def kernel(**inputs):
    import numpy as _np
    import concourse.bacc as _bacc
    from concourse import mybir as _mybir
    from concourse.bass_utils import run_bass_kernel_spmd as _run

    nc = _bacc.Bacc("TRN2", target_bir_lowering=False, num_devices=1)
    arrays, A = {}, {}
    given = {name: inputs[name] for name in INPUTS}
    given["consts"] = constants(_np)
    for name, a in given.items():
        a = _np.ascontiguousarray(a)
        arrays[f"in_{name}"] = a
        A[name] = nc.dram_tensor(f"in_{name}", a.shape, _mybir.dt.from_np(a.dtype), kind="ExternalInput").ap()
    out = nc.dram_tensor("out_x", (1, T, D), FP32, kind="ExternalOutput").ap()
    build(nc, A, out)
    r = _run(nc, [arrays], core_ids=[0])
    return r.results[0]["out_x"]
```
